# Optimizing a Trainium2 kernel written in Bass

```python
import jax, jax.numpy as jnp
from jax import lax
import numpy as np

D_MODEL = 1024
BATCH = 1
SEQ = 512
DEPTH = 1
DEC_BATCH = 1
DEC_SEQ = 64
PAST_LEN = 128

CHUNK = 64
H_M = 4
HD_M = 128
D_M = H_M * HD_M
CONV_W = 4
H_FOX = 8
HD_FOX = 64
D_FOX = H_FOX * HD_FOX
FOX_BLOCK = 128
H_MEM = 4
HD_MEM = 128
D_MEM = H_MEM * HD_MEM
N_MEM = 256
N_BRANCH = 3
SPLIT_SIZES = (D_M, D_M, D_M, D_M, H_M, H_M, D_FOX, D_FOX, D_FOX, H_FOX, D_MEM, N_BRANCH * D_MODEL)
N_IN = 4 * D_M + 2 * H_M + 3 * D_FOX + H_FOX + D_MEM + N_BRANCH * D_MODEL
PEER_HEADS = 8
PEER_DQ = 256
N_KEYS = 128
N_EXPERTS = N_KEYS * N_KEYS
PEER_TOPK = 16
PEER_BLOCK = 256
EPS = 1e-6

kernel_name = 'hybrid_mlstm_fox_peer_stream'

def rmsnorm(x, g):
    xf = x.astype(jnp.float32)
    y = xf * lax.rsqrt(jnp.mean(xf * xf, axis=-1, keepdims=True) + EPS)
    return (y * g.astype(jnp.float32)).astype(x.dtype)

def split_cols(z):
    idx = np.cumsum(np.array(SPLIT_SIZES))[:-1].tolist()
    return jnp.split(z, idx, axis=-1)

def causal_conv(prev, x, w, b):
    s = x.shape[1]
    xp = jnp.concatenate([prev.astype(x.dtype), x], axis=1)
    y = b.astype(x.dtype)
    for j in range(CONV_W):
        y = y + w[j].astype(x.dtype) * xp[:, j:j + s]
    return jax.nn.silu(y), xp[:, xp.shape[1] - (CONV_W - 1):]

def mlstm_chunk(carry, xs):
    c, n, m = carry
    q, k, v, ig, lf = xs
    L = q.shape[1]
    bcum = jnp.cumsum(lf, axis=1)
    causal = jnp.tril(jnp.ones((L, L), dtype=bool))
    dmat = bcum[:, :, None, :] - bcum[:, None, :, :] + ig[:, None, :, :]
    dmat = jnp.where(causal[None, :, :, None], dmat, -jnp.inf)
    inter = bcum + m[:, None, :]
    m_t = jnp.maximum(inter, jnp.max(dmat, axis=2))
    w_intra = jnp.exp(dmat - m_t[:, :, None, :])
    w_state = jnp.exp(inter - m_t)
    sw = jnp.einsum('bthd,bshd->btsh', q, k) * w_intra
    num = jnp.einsum('btsh,bshd->bthd', sw, v) + w_state[..., None] * jnp.einsum('bthk,bhkv->bthv', q, c)
    den = jnp.sum(sw, axis=2) + w_state * jnp.einsum('bthk,bhk->bth', q, n)
    h = num / jnp.maximum(jnp.abs(den), jnp.exp(-m_t))[..., None]
    bl = bcum[:, -1]
    m_new = jnp.maximum(bl + m, jnp.max(bl[:, None] - bcum + ig, axis=1))
    decay_state = jnp.exp(bl + m - m_new)
    ws = jnp.exp(bl[:, None] - bcum + ig - m_new[:, None])
    c_new = decay_state[..., None, None] * c + jnp.einsum('bsh,bshk,bshv->bhkv', ws, k, v)
    n_new = decay_state[..., None] * n + jnp.einsum('bsh,bshk->bhk', ws, k)
    return (c_new, n_new, m_new), h

def mlstm_sequence(c, n, m, q, k, v, ig, lf):
    b, s = q.shape[:2]
    if s <= CHUNK:
        return mlstm_chunk((c, n, m), (q, k, v, ig, lf))
    nc = s // CHUNK

    def to_chunks(a):
        return jnp.moveaxis(a.reshape((b, nc, CHUNK) + a.shape[2:]), 1, 0)

    state, h = lax.scan(mlstm_chunk, (c, n, m),
                        (to_chunks(q), to_chunks(k), to_chunks(v), to_chunks(ig), to_chunks(lf)))
    return state, jnp.moveaxis(h, 0, 1).reshape((b, s) + h.shape[3:])

def fox_attend(q, k, v, fq, fk, q_pos, k_pos):
    sc = jnp.einsum('bqhd,bkhd->bhqk', q, k).astype(jnp.float32) * (HD_FOX ** -0.5)
    sc = sc + (jnp.transpose(fq, (0, 2, 1))[:, :, :, None] - jnp.transpose(fk, (0, 2, 1))[:, :, None, :])
    mask = k_pos[None, :] <= q_pos[:, None]
    sc = jnp.where(mask[None, None], sc, -jnp.inf)
    prob = jax.nn.softmax(sc, axis=-1)
    return jnp.einsum('bhqk,bkhd->bqhd', prob.astype(v.dtype), v)

def fox_attention(q, k, v, fq, fk, q_pos, k_pos):
    b, nq, h, d = q.shape
    if nq > FOX_BLOCK and nq % FOX_BLOCK == 0:
        nb = nq // FOX_BLOCK
        qb = jnp.moveaxis(q.reshape(b, nb, FOX_BLOCK, h, d), 1, 0)
        fqb = jnp.moveaxis(fq.reshape(b, nb, FOX_BLOCK, h), 1, 0)
        pb = q_pos.reshape(nb, FOX_BLOCK)
        out = lax.map(lambda a: fox_attend(a[0], k, v, a[1], fk, a[2], k_pos), (qb, fqb, pb))
        return jnp.moveaxis(out, 0, 1).reshape(b, nq, h, d)
    return fox_attend(q, k, v, fq, fk, q_pos, k_pos)

def memory_kv(mem, g, w):
    b, nm, _ = mem.shape
    k, v = jnp.split(rmsnorm(mem, g) @ w, 2, axis=-1)
    return k.reshape(b, nm, H_MEM, HD_MEM), v.reshape(b, nm, H_MEM, HD_MEM)

def peer_block(tok, wq, keys, u, v):
    p = tok.shape[0]
    qr = (tok @ wq).reshape(p, PEER_HEADS, 2, PEER_DQ // 2).astype(jnp.float32)
    s = jnp.einsum('phcd,hckd->phck', qr, keys.astype(jnp.float32))
    top_s, top_i = lax.top_k(s, PEER_TOPK)
    cand = top_s[:, :, 0, :, None] + top_s[:, :, 1, None, :]
    ids = top_i[:, :, 0, :, None] * N_KEYS + top_i[:, :, 1, None, :]
    best, j = lax.top_k(cand.reshape(p, PEER_HEADS, PEER_TOPK * PEER_TOPK), PEER_TOPK)
    eidx = jnp.take_along_axis(ids.reshape(p, PEER_HEADS, PEER_TOPK * PEER_TOPK), j, axis=-1)
    g = jax.nn.softmax(best, axis=-1)
    act = jax.nn.gelu(jnp.einsum('phkd,pd->phk', u[eidx], tok))
    return jnp.einsum('phk,phkd->pd', (g * act).astype(tok.dtype), v[eidx])

def peer_ffn(h, wq, keys, u, v):
    b, s, d = h.shape
    t = b * s
    nblk = -(-t // PEER_BLOCK)
    tok = jnp.pad(h.reshape(t, d), ((0, nblk * PEER_BLOCK - t), (0, 0))).reshape(nblk, PEER_BLOCK, d)
    out = lax.map(lambda blk: peer_block(blk, wq, keys, u, v), tok)
    return out.reshape(nblk * PEER_BLOCK, d)[:t].reshape(b, s, d)

def layer(x, mem_k, mem_v, conv_prev, c0, n0, m0, fk_past, fv_past, flf_past, p):
    f32 = jnp.float32
    b, s, _ = x.shape
    p0 = fk_past.shape[1]
    h = rmsnorm(x, p['norm_mix'])
    mq, mk, mv, mo, mi, mf, fq, fk, fv, ff, cq, gates = split_cols(h @ p['w_in'])
    qk_c, conv_new = causal_conv(conv_prev, jnp.concatenate([mq, mk], axis=-1), p['conv_w'], p['conv_b'])
    q_m, k_m = jnp.split(qk_c.astype(f32), 2, axis=-1)
    q_m = q_m.reshape(b, s, H_M, HD_M)
    k_m = k_m.reshape(b, s, H_M, HD_M) * (HD_M ** -0.5)
    v_m = mv.astype(f32).reshape(b, s, H_M, HD_M)
    ig = (mi + p['b_m_i']).astype(f32)
    lf = jax.nn.log_sigmoid((mf + p['b_m_f']).astype(f32))
    (c1, n1, m1), h_m = mlstm_sequence(c0.astype(f32), n0.astype(f32), m0.astype(f32), q_m, k_m, v_m, ig, lf)
    h_m = rmsnorm(h_m, p['norm_m_head'].reshape(H_M, HD_M)).reshape(b, s, D_M).astype(x.dtype)
    a_m = (h_m * jax.nn.sigmoid(mo)) @ p['w_up_m']
    k_f = fk.reshape(b, s, H_FOX, HD_FOX)
    v_f = fv.reshape(b, s, H_FOX, HD_FOX)
    lf_f = jax.nn.log_sigmoid((ff + p['b_fox_f']).astype(f32))
    k_all = jnp.concatenate([fk_past.astype(x.dtype), k_f], axis=1)
    v_all = jnp.concatenate([fv_past.astype(x.dtype), v_f], axis=1)
    cum = jnp.cumsum(jnp.concatenate([flf_past.astype(f32), lf_f], axis=1), axis=1)
    o_f = fox_attention(fq.reshape(b, s, H_FOX, HD_FOX), k_all, v_all, cum[:, p0:], cum,
                        p0 + jnp.arange(s), jnp.arange(p0 + s))
    a_f = o_f.reshape(b, s, D_FOX) @ p['w_up_f']
    sc = jnp.einsum('bqhd,bkhd->bhqk', cq.reshape(b, s, H_MEM, HD_MEM), mem_k.astype(x.dtype)).astype(f32) * (HD_MEM ** -0.5)
    o_c = jnp.einsum('bhqk,bkhd->bqhd', jax.nn.softmax(sc, axis=-1).astype(x.dtype), mem_v.astype(x.dtype))
    a_c = o_c.reshape(b, s, D_MEM) @ p['w_up_c']
    g_m, g_f, g_c = jnp.split(jax.nn.sigmoid(gates), N_BRANCH, axis=-1)
    x = x + (g_m * a_m + g_f * a_f + g_c * a_c) @ p['w_out']
    x = x + peer_ffn(rmsnorm(x, p['norm_ffn']), p['peer_wq'], p['peer_keys'], p['peer_u'], p['peer_v'])
    return x, conv_new, c1, n1, m1, k_f, v_f, lf_f

def setup_inputs(seed: int = 0) -> dict:
    key = jax.random.key(seed)
    k = jax.random.split(key, 40)
    f32 = jnp.float32

    def nrm(i, shape, scale):
        return jax.random.normal(k[i], shape, f32) * scale

    return {
        'x_prompt': nrm(0, (BATCH, SEQ, D_MODEL), 1.0),
        'x_sample': nrm(1, (DEC_BATCH, DEC_SEQ, D_MODEL), 1.0),
        'mem_prompt': nrm(2, (BATCH, N_MEM, D_MODEL), 1.0),
        'cache_fox_k': nrm(3, (DEPTH, DEC_BATCH, PAST_LEN, H_FOX, HD_FOX), 1.0),
        'cache_fox_v': nrm(4, (DEPTH, DEC_BATCH, PAST_LEN, H_FOX, HD_FOX), 1.0),
        'cache_fox_lf': jax.nn.log_sigmoid(3.0 + nrm(5, (DEPTH, DEC_BATCH, PAST_LEN, H_FOX), 1.0)),
        'state_mlstm_c': nrm(6, (DEPTH, DEC_BATCH, H_M, HD_M, HD_M), 0.1),
        'state_mlstm_n': nrm(7, (DEPTH, DEC_BATCH, H_M, HD_M), 0.1),
        'state_mlstm_m': nrm(8, (DEPTH, DEC_BATCH, H_M), 0.5),
        'state_conv': nrm(9, (DEPTH, DEC_BATCH, CONV_W - 1, 2 * D_M), 1.0),
        'cache_mem_k': nrm(10, (DEPTH, DEC_BATCH, N_MEM, H_MEM, HD_MEM), 1.0),
        'cache_mem_v': nrm(11, (DEPTH, DEC_BATCH, N_MEM, H_MEM, HD_MEM), 1.0),
        'norm_mix': 1.0 + nrm(12, (DEPTH, D_MODEL), 0.02),
        'w_in': nrm(13, (DEPTH, D_MODEL, N_IN), D_MODEL ** -0.5),
        'conv_w': nrm(14, (DEPTH, CONV_W, 2 * D_M), CONV_W ** -0.5),
        'conv_b': nrm(15, (DEPTH, 2 * D_M), 0.01),
        'b_m_i': nrm(16, (DEPTH, H_M), 0.1),
        'b_m_f': jnp.linspace(3.0, 6.0, H_M, dtype=f32)[None, :] + nrm(17, (DEPTH, H_M), 0.1),
        'norm_m_head': 1.0 + nrm(18, (DEPTH, D_M), 0.02),
        'b_fox_f': jnp.linspace(1.0, 5.0, H_FOX, dtype=f32)[None, :] + nrm(19, (DEPTH, H_FOX), 0.1),
        'norm_mem': 1.0 + nrm(20, (DEPTH, D_MODEL), 0.02),
        'w_mem_kv': nrm(21, (DEPTH, D_MODEL, 2 * D_MEM), D_MODEL ** -0.5),
        'w_up_m': nrm(22, (DEPTH, D_M, D_MODEL), D_M ** -0.5),
        'w_up_f': nrm(23, (DEPTH, D_FOX, D_MODEL), D_FOX ** -0.5),
        'w_up_c': nrm(24, (DEPTH, D_MEM, D_MODEL), D_MEM ** -0.5),
        'w_out': nrm(25, (DEPTH, D_MODEL, D_MODEL), D_MODEL ** -0.5),
        'norm_ffn': 1.0 + nrm(26, (DEPTH, D_MODEL), 0.02),
        'peer_wq': nrm(27, (DEPTH, D_MODEL, PEER_HEADS * PEER_DQ), D_MODEL ** -0.5),
        'peer_keys': nrm(28, (DEPTH, PEER_HEADS, 2, N_KEYS, PEER_DQ // 2), (PEER_DQ // 2) ** -0.5),
        'peer_u': nrm(29, (DEPTH, N_EXPERTS, D_MODEL), D_MODEL ** -0.5),
        'peer_v': nrm(30, (DEPTH, N_EXPERTS, D_MODEL), 0.25),
        'norm_final': 1.0 + nrm(31, (D_MODEL,), 0.02),
    }

def reference(x_prompt, x_sample, mem_prompt, cache_fox_k, cache_fox_v, cache_fox_lf,
              state_mlstm_c, state_mlstm_n, state_mlstm_m, state_conv, cache_mem_k, cache_mem_v,
              norm_mix, w_in, conv_w, conv_b, b_m_i, b_m_f, norm_m_head, b_fox_f, norm_mem, w_mem_kv,
              w_up_m, w_up_f, w_up_c, w_out, norm_ffn, peer_wq, peer_keys, peer_u, peer_v, norm_final):
    f32 = jnp.float32

    def params(l):
        return {'norm_mix': norm_mix[l], 'w_in': w_in[l], 'conv_w': conv_w[l], 'conv_b': conv_b[l],
                'b_m_i': b_m_i[l], 'b_m_f': b_m_f[l], 'norm_m_head': norm_m_head[l], 'b_fox_f': b_fox_f[l],
                'w_up_m': w_up_m[l], 'w_up_f': w_up_f[l], 'w_up_c': w_up_c[l], 'w_out': w_out[l],
                'norm_ffn': norm_ffn[l], 'peer_wq': peer_wq[l], 'peer_keys': peer_keys[l],
                'peer_u': peer_u[l], 'peer_v': peer_v[l]}

    xp = x_prompt
    bp = x_prompt.shape[0]
    new_p = [[] for _ in range(9)]
    for l in range(DEPTH):
        mk, mv = memory_kv(mem_prompt, norm_mem[l], w_mem_kv[l])
        xp, conv1, c1, n1, m1, kf, vf, lff = layer(
            xp, mk, mv,
            jnp.zeros((bp, CONV_W - 1, 2 * D_M), xp.dtype),
            jnp.zeros((bp, H_M, HD_M, HD_M), f32), jnp.zeros((bp, H_M, HD_M), f32), jnp.zeros((bp, H_M), f32),
            jnp.zeros((bp, 0, H_FOX, HD_FOX), xp.dtype), jnp.zeros((bp, 0, H_FOX, HD_FOX), xp.dtype),
            jnp.zeros((bp, 0, H_FOX), f32), params(l))
        for lst, a in zip(new_p, (kf, vf, lff, c1, n1, m1, conv1, mk, mv)):
            lst.append(a)
    y_prompt = rmsnorm(xp, norm_final)
    fox_k_p, fox_v_p, fox_lf_p, mlstm_c_p, mlstm_n_p, mlstm_m_p, conv_p, mem_k_p, mem_v_p = [jnp.stack(a) for a in new_p]

    xs = x_sample
    new_s = [[] for _ in range(7)]
    for l in range(DEPTH):
        xs, conv1, c1, n1, m1, kf, vf, lff = layer(
            xs, cache_mem_k[l], cache_mem_v[l], state_conv[l],
            state_mlstm_c[l], state_mlstm_n[l], state_mlstm_m[l],
            cache_fox_k[l], cache_fox_v[l], cache_fox_lf[l], params(l))
        for lst, a in zip(new_s, (kf, vf, lff, c1, n1, m1, conv1)):
            lst.append(a)
    y_sample = rmsnorm(xs, norm_final)
    fox_k_s, fox_v_s, fox_lf_s, mlstm_c_s, mlstm_n_s, mlstm_m_s, conv_s = [jnp.stack(a) for a in new_s]

    return (y_prompt, y_sample, fox_k_p, fox_v_p, fox_lf_p, mlstm_c_p, mlstm_n_p, mlstm_m_p, conv_p, mem_k_p, mem_v_p,
            fox_k_s, fox_v_s, fox_lf_s, mlstm_c_s, mlstm_n_s, mlstm_m_s, conv_s)


_drawn_inputs = setup_inputs


def setup_inputs(seed=0):
    import zlib

    import numpy as np

    out = dict(_drawn_inputs(seed))
    spreads = {}
    factors = {'cache_fox_lf': 3.477,
     'state_mlstm_n': 5.129,
     'norm_m_head': 5.167,
     'norm_mem': 2.94,
     'norm_ffn': 2.973,
     'norm_final': 2.898}
    for name, (base, spread) in spreads.items():
        noise = np.random.default_rng([zlib.crc32(name.encode()), seed]).standard_normal(out[name].shape)
        drawn = base * np.exp(spread * noise) if base else spread * noise
        out[name] = __import__('jax').numpy.asarray(drawn.astype(out[name].dtype))
    for name, factor in factors.items():
        out[name] = (out[name] * factor).astype(out[name].dtype)
    return out
```

```python
from contextlib import ExitStack

import concourse.bass as bass
from concourse import mybir

F32 = mybir.dt.float32
BF16 = mybir.dt.bfloat16
U32 = mybir.dt.uint32
ALU = mybir.AluOpType
ACT = mybir.ActivationFunctionType
AX = mybir.AxisListType

P = 128
D = 1024
KT = D // P
TP, TS = 512, 64
T = TP + TS
HALF = T // 2
NTT = 5
NMEM = 256
PAST = 128
HM, HF, HC = 4, 8, 4
FD = 64
NB = 3
EPS = 1e-6
NPH = 8
NKEY = 128
TOPK = 16
NHC = NPH * 2
NCH = 128
GRP = 4
NG = NCH // GRP
SQRT_HM = 128 ** -0.5

N_MEMK, N_MEMV, N_T, N_MV, N_FV, N_SMALL = 4, 4, 24, 4, 4, 1
U_MEMV = N_MEMK
U_T = U_MEMV + N_MEMV
U_MV = U_T + N_T
U_FV = U_MV + N_MV
U_SMALL = U_FV + N_FV
U_MERGE = U_SMALL + N_SMALL
N_JP = 4
N_PER_JP = NB + 2 * NB
U_OUT = U_MERGE + N_JP * N_PER_JP
U_WQ = U_OUT + KT
U_PEER = U_WQ + NHC
RAW, RING = 4, 8

MQ, MK, FQ, FK, CQ, MO = 0, 4, 8, 12, 16, 20
C_MIX, C_FFN, C_FIN, C_MEM, C_HEAD, C_CW, C_CB, C_ZB, C_IB = 0, 8, 16, 24, 32, 36, 68, 76, 77
N_PAR = 78

TBLK = 96
NBLK = T // TBLK
GT = 4
N_TK = 25
TK_BEST, TK_TRIP = 21, 24
N_MD, N_MA = 13, 13


def attention_items():
    items = [("fox", 2 * hp + hh, qi) for hp in range(HF // 2) for qi in range(NTT) for hh in range(2)]
    return items + [("mem", h, qi) for h in range(HC) for qi in range(NTT)]


def out_slot(kind, h):
    return h // 2 if kind == "fox" else 4 + h


def columns(kind, qi):
    if kind == "mem":
        return NMEM
    return (qi + 1) * P if qi < 4 else PAST + TS


def scale_of(kind):
    return FD ** -0.5 if kind == "fox" else 128 ** -0.5


def out_index(i):
    nf = HF * NTT
    return i // 2 if i < nf else nf // 2 + i - nf


def program(nc, a, o):
    ctx = ExitStack()
    with ctx:
        BASE = (nc.sbuf_base + 63) // 64 * 64
        used = [BASE]

        def place(name, offset, shape, dt):
            return nc.alloc_sbuf_tensor_at(name, shape, dt, offset=offset)

        def sb(name, shape, dt):
            size = 2 if dt == BF16 else 4
            n = size
            for x in shape[1:]:
                n *= x
            t = place(name, used[0], shape, dt)
            used[0] += (n + 31) // 32 * 32
            return t

        def sem(name):
            return ctx.enter_context(nc.semaphore(name))

        ps = ctx.enter_context(nc.psum_tensor("ps", [P, 8, 512], F32))

        xT = sb("xT", [P, KT, T], F32)
        act_hi = sb("act_hi", [P, KT, T], BF16)
        act_lo = sb("act_lo", [P, KT, T], BF16)
        raw = sb("raw", [P, RAW, 1024], F32)
        w_hi = sb("w_hi", [P, RING, 1024], BF16)
        w_lo = sb("w_lo", [P, RING, 1024], BF16)
        par = sb("par", [P, N_PAR], F32)
        ones = sb("ones", [P, P], F32)
        ident = sb("ident", [P, P], F32)
        causal = sb("causal", [P, P], F32)
        identb = sb("identb", [P, P], BF16)
        maskneg = sb("maskneg", [P, P], BF16)
        iota = sb("iota", [P, P], F32)
        epsb = sb("epsb", [P, 1], F32)
        oneb = sb("oneb", [P, 1], F32)
        ARENA = used[0]

        proj = place("proj", ARENA, [P, 24, T], F32)
        proj_b = place("proj_b", ARENA, [P, 24, 2, T], BF16)
        mem_x = place("mem_x", ARENA, [P, KT, NMEM], F32)
        mem_sq = place("mem_sq", ARENA + 8192, [P, KT, NMEM], F32)
        mem_h = place("mem_h", ARENA + 16384, [P, KT, NMEM], F32)
        mix_sq = place("mix_sq", ARENA, [P, KT, T], F32)
        mix_h = place("mix_h", ARENA + 24576, [P, KT, T], F32)
        used[0] = ARENA + 24 * T * 4
        V0 = used[0]
        mv = sb("mv", [P, NTT, 512], F32)
        fv = sb("fv", [P, NTT, 512], F32)
        qz = place("qz", V0, [P, 2, 2, T], F32)
        mg_hi = place("mg_hi", V0, [P, KT, T], BF16)
        mg_lo = place("mg_lo", V0 + KT * T * 2, [P, KT, T], BF16)
        mem_hi = place("mem_hi", V0, [P, KT, NMEM], BF16)
        mem_lo = place("mem_lo", V0 + 4096, [P, KT, NMEM], BF16)
        mkT = sb("mkT", [P, HC, NMEM], F32)
        mvN = sb("mvN", [P, 2, 512], F32)
        kc = sb("kc", [P, HC, NMEM], F32)
        vc = sb("vc", [P, 2, 512], F32)
        kpast = sb("kpast", [P, HF // 2, PAST], F32)
        vpast = sb("vpast", [P, 512], F32)
        W0 = used[0]
        wk = sb("wk", [P, 5, T], F32)
        R0 = used[0]
        lsig = sb("lsig", [40, T], F32)
        m_row = sb("m_row", [4, T], F32)
        nM = sb("nM", [4, T], F32)
        cum = sb("cum", [P, 704], F32)
        c_row = sb("c_row", [4, T], F32)
        cS = sb("cS", [P, NTT, HM], F32)
        zrow = place("zrow", W0, [40, T], F32)
        trow = place("trow", W0 + 2304, [40, T], F32)
        st = sb("st", [P, 2, 4], F32)
        sm = sb("sm", [P, 2, TS], F32)
        ws = sb("ws", [P, 8], F32)
        c0 = sb("c0", [P, HM, P], F32)
        n0 = sb("n0", [P, HM], F32)
        m0b = sb("m0b", [P, HM], F32)
        m0 = sb("m0", [4, 1], F32)
        xs = place("xs", W0 + 2 * T * 4, [P, KT, 3 + TS], F32)
        assert used[0] <= nc.sbuf_usable_end, used[0] - nc.sbuf_usable_end

        S = place("S", ARENA, [P, NTT, NHC, NKEY], F32)
        keys = place("keys", ARENA + 40960, [P, NHC, NKEY], F32)
        qr = place("qr", ARENA + 49152, [P, 2, T], F32)
        used[0] = ARENA + 49152 + 2 * T * 4
        sA = sb("sA", [P, NHC, NKEY], F32)
        sB = sb("sB", [P, NHC, NKEY], F32)
        candA = sb("candA", [P, NPH, TOPK * TOPK], F32)
        candB = sb("candB", [P, NPH, TOPK * TOPK], F32)
        top = sb("top", [P, NHC, TOPK], F32)
        topi = sb("topi", [P, NHC, TOPK], U32)
        topf = sb("topf", [P, NHC, TOPK], F32)
        best = sb("best", [P, NPH, TOPK], F32)
        bi = sb("bi", [P, NPH, TOPK], U32)
        ab = sb("ab", [P, 2, NPH, TOPK], U32)
        abf = sb("abf", [P, 2, NPH, TOPK], F32)
        trip = sb("trip", [P, 3, P], F32)
        gs = sb("gs", [P, 2, NPH], F32)
        eq = sA[:, :, :].rearrange("p a (k c) -> p (a k) c", c=TOPK)
        PAIR = ARENA + 98304
        assert used[0] <= PAIR, used[0] - PAIR
        used[0] = PAIR
        pair = sb("pair", [P, 3, NTT * P], F32)
        hot1 = sb("hot1", [P, 2, GT, P], F32)
        hot2 = sb("hot2", [P, 2, GT, P], F32)
        tcol = sb("tcol", [P, 2, 3, GT], F32)
        assert used[0] <= nc.sbuf_usable_end
        gsb = place("gsb", ARENA, [P, 2, P, TBLK], F32)

        used[0] = ARENA
        W_hi = sb("W_hi", [P, 2, GRP, T], BF16)
        W_lo = sb("W_lo", [P, 2, GRP, T], BF16)
        Gb = sb("Gb", [P, 2, GRP, T], F32)
        hb = sb("hb", [P, 2, T], F32)
        wb = sb("wb", [P, 2, T], F32)
        fin_sq = sb("fin_sq", [P, KT, T], F32)
        fin_y = sb("fin_y", [P, KT, T], F32)

        gd = nc.dram_tensor("gd", (NCH, P, T), F32, kind="Internal").ap()

        raw_loaded = [sem(f"raw_loaded{i}") for i in range(RAW)]
        hi_ready, lo_ready, unit_used = sem("hi_ready"), sem("lo_ready"), sem("unit_used")
        mem_in, x_in, par_in, small_in, cw_in = sem("mem_in"), sem("x_in"), sem("par_in"), sem("small_in"), sem("cw_in")
        keys_in = sem("keys_in")
        consts, filled = sem("consts"), sem("filled")
        n_sq, n_ssq, n_rms, n_inv = sem("n_sq"), sem("n_ssq"), sem("n_rms"), sem("n_inv")
        n_scaled, n_hi, n_lo = sem("n_scaled"), sem("n_hi"), sem("n_lo")
        t_evac, nat_evac = sem("t_evac"), sem("nat_evac")
        row_dve, row_act, c_turned, cS_ready = sem("row_dve"), sem("row_act"), sem("c_turned"), sem("cS_ready")
        xs_ready, conv_step, conv_y, conv_done = sem("xs_ready"), sem("conv_step"), sem("conv_y"), sem("conv_done")
        early_out, late_out, conv_out = sem("early_out"), sem("late_out"), sem("conv_out")
        m_bc, m_s, m_arg, m_exp, m_mask = sem("m_bc"), sem("m_s"), sem("m_arg"), sem("m_exp"), sem("m_mask")
        m_sw, m_acc, m_act, m_dve, m_ssq = sem("m_sw"), sem("m_acc"), sem("m_act"), sem("m_dve"), sem("m_ssq")
        m_kt, m_st = sem("m_kt"), sem("m_st")
        q_apart, cum_zero = sem("q_apart"), sem("cum_zero")
        a_sc, a_max, a_neg, a_exp = sem("a_sc"), sem("a_max"), sem("a_neg"), sem("a_exp")
        a_rcp, a_norm, a_tr, a_pt = sem("a_rcp"), sem("a_norm"), sem("a_tr"), sem("a_pt")
        a_pv, a_oh, a_ol = sem("a_pv"), sem("a_oh"), sem("a_ol")
        g_ready, g_evac, g_prod, g_acc, g_mhi, g_mlo = (
            sem("g_ready"), sem("g_evac"), sem("g_prod"), sem("g_acc"), sem("g_mhi"), sem("g_mlo"))
        x2_ready = sem("x2_ready")
        q_evac, s_ready, s_evac = sem("q_evac"), sem("s_ready"), sem("s_evac")
        tk, tk_exp, tk_turned, tk_pair = sem("tk"), sem("tk_exp"), sem("tk_turned"), sem("tk_pair")
        b_col, b_hot, b_prod, b_evac, b_written = (
            sem("b_col"), sem("b_hot"), sem("b_prod"), sem("b_evac"), [sem("b_written0"), sem("b_written1")])
        g_in = [sem("g_in0"), sem("g_in1")]
        gelu_done, w_mul, w_hi_done, w_lo_done = sem("gelu_done"), sem("w_mul"), sem("w_hi_done"), sem("w_lo_done")
        v_ready, acc_done = sem("v_ready"), sem("acc_done")
        y_out = sem("y_out")

        items = attention_items()
        block = ctx.enter_context(nc.Block())

        def pos_u(g):
            return U_PEER + GRP + 8 * (g - 1)

        def pos_v(g, last=False):
            return U_PEER + 2 * NCH - GRP if last else U_PEER + 2 * GRP + 8 * g

        @block.sync
        def _(sp):
            def load(src, slot, first, need):
                if not first:
                    sp.wait_ge(lo_ready, need)
                sp.dma_start(raw[:, slot, :], src).then_inc(raw_loaded[slot], 16)

            for n in range(RAW):
                load(a["units"][n], n, True, 0)
            with sp.Fori(1, U_PEER // RAW) as i:
                for k in range(RAW):
                    load(a["units"][i * RAW + k], k, False, i * RAW + k - RAW + 1)
            for n in range(U_PEER // RAW * RAW, U_PEER):
                load(a["units"][n], n % RAW, False, n - RAW + 1)
            for g in range(2):
                for k in range(GRP):
                    n = U_PEER + g * GRP + k
                    load(a["u_units"][g * GRP + k], n % RAW, False, n - RAW + 1)

            gd_out = gd.rearrange("k1 k2 t -> k2 k1 t")
            with sp.Fori(0, NBLK // 2) as i:
                for b in range(2):
                    sp.wait_ge(b_evac, (i * 2 + b + 1) * (TBLK // GT))
                    sp.dma_start(gd_out[:, :, bass.ds((i * 2 + b) * TBLK, TBLK)], gsb[:, b, :, :]).then_inc(b_written[b], 16)
            for b in range(2):
                sp.wait_ge(b_written[b], 8 * NBLK)

            def load_g(g, pg, need):
                if need is not None:
                    sp.wait_ge(w_mul, need)
                sp.dma_start(Gb[:, pg, :, :], gd[bass.ds(g * GRP, GRP)].rearrange("k1 k2 t -> k2 k1 t"))\
                    .then_inc(g_in[pg], 16)

            def load_group(g, pg, need, u, v):
                load_g(g, pg, need)
                for k in range(GRP):
                    if u:
                        load(a["u_units"][g * GRP + k], (U_PEER + k) % RAW, False, pos_u(g) + k - RAW + 1)
                for k in range(GRP):
                    if v:
                        load(a["v_units"][(g - 1) * GRP + k], (U_PEER + k) % RAW, False, pos_v(g - 1) + k - RAW + 1)

            load_g(0, 0, None)
            load_group(1, 1, None, False, True)
            with sp.Fori(0, (NG - 2) // 2) as i:
                for b in range(2):
                    load_group(i * 2 + 2 + b, b, (i * 2 + b) * GRP + GRP, True, True)
            for k in range(GRP):
                load(a["v_units"][(NG - 1) * GRP + k], (U_PEER + k) % RAW, False, pos_v(None, last=True) + k - RAW + 1)

            sp.wait_ge(n_scaled, 4 * KT)
            sp.dma_start(o["y"], fin_y[:, :, :]).then_inc(y_out, 16)
            sp.wait_ge(y_out, 16)

        @block.gpsimd
        def _(pool):
            pool.memset(ones[:, :], 1.0).then_inc(consts, 1)
            pool.memset(ident[:, :], 0.0).then_inc(filled, 1)
            pool.memset(identb[:, :], 0.0).then_inc(filled, 1)
            pool.memset(causal[:, :], 1.0).then_inc(filled, 1)
            pool.memset(maskneg[:, :], 0.0).then_inc(filled, 1)
            pool.memset(epsb[:, :], EPS).then_inc(consts, 1)
            pool.memset(oneb[:, :], 1.0).then_inc(consts, 1)
            pool.memset(cum[:, :], 0.0).then_inc(cum_zero, 1)
            pool.iota(iota[:, :], [[1, P]], base=0, channel_multiplier=0,
                      allow_small_or_imprecise_dtypes=True).then_inc(consts, 1)
            pool.wait_ge(filled, 4)
            for m in (ident, identb):
                pool.affine_select(out=m[:, :], in_=m[:, :], compare_op=ALU.not_equal, fill=1.0, base=0,
                                   pattern=[[-1, P]], channel_multiplier=1).then_inc(consts, 1)
            pool.affine_select(out=causal[:, :], in_=causal[:, :], compare_op=ALU.is_ge, fill=0.0, base=0,
                               pattern=[[1, P]], channel_multiplier=-1).then_inc(consts, 1)
            pool.affine_select(out=maskneg[:, :], in_=maskneg[:, :], compare_op=ALU.is_ge, fill=-1e30, base=0,
                               pattern=[[-1, P]], channel_multiplier=1).then_inc(consts, 1)

            def low_half(n, k):
                pool.wait_ge(hi_ready, n + 1)
                pool.tensor_tensor(w_lo[:, k % RING, :], raw[:, k % RAW, :], w_hi[:, k % RING, :],
                                   ALU.subtract).then_inc(lo_ready, 1)

            with pool.Fori(0, U_PEER // RING) as i:
                for k in range(RING):
                    low_half(i * RING + k, k)
            for n in range(U_PEER // RING * RING, U_PEER):
                low_half(n, n)
            with pool.Fori(0, 2 * NCH // RING) as i:
                for k in range(RING):
                    low_half(i * RING + U_PEER + k, U_PEER + k)

        @block.scalar
        def _(act):
            act.dma_start(mem_x[:, :, :], a["memT"]).then_inc(mem_in, 16)
            act.dma_start(par[:, :], a["par"]).then_inc(par_in, 16)
            act.dma_start(xT[:, :, :], a["xT"]).then_inc(x_in, 16)
            act.dma_start(xs[:, :, 0:3], a["conv_state"]).then_inc(cw_in, 16)
            act.wait_ge(cum_zero, 1)
            act.dma_start(cum[32:40, TP:TP + PAST], a["lf_past"]).then_inc(small_in, 16)
            act.dma_start(c0[:, :, :], a["c0"]).then_inc(small_in, 16)
            act.dma_start(n0[:, :], a["n0"]).then_inc(small_in, 16)
            act.dma_start(m0[:, :], a["m0"].rearrange("a h -> h a")).then_inc(small_in, 16)
            act.dma_start(m0b[:, :], a["m0"].broadcast_to((P, HM))).then_inc(small_in, 16)
            act.dma_start(kc[:, :, :], a["kc"]).then_inc(small_in, 16)
            act.dma_start(vc[:, :, :], a["vc"]).then_inc(small_in, 16)
            act.dma_start(kpast[:, :, :], a["kpast"]).then_inc(small_in, 16)
            act.dma_start(vpast[:, :], a["vpast"]).then_inc(small_in, 16)

            def square(i, x, sq):
                act.activation(sq, x, ACT.Square).then_inc(n_sq, 1)

            def root(i, out, sums):
                act.wait_ge(n_ssq, i + 1)
                act.activation(out, sums, ACT.Sqrt, bias=epsb[:, 0:1], scale=1.0 / D).then_inc(n_rms, 1)

            def high(i, h, hi):
                act.wait_ge(n_scaled, KT * (i + 1))
                act.activation(hi, h, ACT.Copy).then_inc(n_hi, 1)

            def high_half(n, k, load_count=None):
                act.wait_ge(raw_loaded[k % RAW], load_count)
                act.activation(w_hi[:, k % RING, :], raw[:, k % RAW, :], ACT.Copy).then_inc(hi_ready, 1)

            def high_unit(n):
                if n >= RING:
                    act.wait_ge(unit_used, n - RING + 1)
                high_half(n, n, 16 * (n // RAW + 1))

            act.wait_ge(consts, 8)
            act.wait_ge(mem_in, 16)
            square(0, mem_x[:, :, :], mem_sq[:, :, :])
            root(0, wk[:, 0, 0:NMEM], ps[:, 4, 0:NMEM])
            act.wait_ge(par_in, 16)
            for n in range(RAW):
                high_unit(n)
            high(0, mem_h[:, :, :], mem_hi[:, :, :])
            act.wait_ge(x_in, 16)
            act.wait_ge(n_lo, 1)
            square(1, xT[:, :, :], mix_sq[:, :, :])
            root(1, wk[:, 1, :].rearrange("p (a b) -> p a b", a=2), ps[:, 0:2, 0:HALF])
            for n in range(RAW, RING):
                high_unit(n)
            high(1, mix_h[:, :, :], act_hi[:, :, :])

            for n in range(RING, RING + U_T):
                high_unit(n)
            act.activation(mvN[:, :, :], ps[:, 4:6, :], ACT.Copy).then_inc(nat_evac, 1)
            with act.Fori(0, N_T // RING) as i:
                for k in range(RING):
                    act.wait_ge(unit_used, i * RING + U_T + k + 1)
                    high_half(None, U_T + k, i * 32 + 16 * ((U_T + RING + k) // RAW + 1))
            act.wait_ge(t_evac, N_MEMK + N_T)
            act.dma_start(o["conv_p"], proj[:, 0:KT, TP - 3:TP]).then_inc(conv_out, 16)
            act.dma_start(o["conv_s"], proj[:, 0:KT, T - 3:T]).then_inc(conv_out, 16)
            act.dma_start(o["fk"], proj[:, FK:FK + 4, :]).then_inc(early_out, 16)
            act.dma_start(o["memk"], mkT[:, :, :]).then_inc(early_out, 16)
            act.wait_ge(nat_evac, 1)
            act.dma_start(o["memv"], mvN[:, :, :]).then_inc(early_out, 16)
            for first, buf in ((U_MV, mv), (U_FV, fv)):
                for n in range(first, first + 4):
                    high_unit(n + RING)
                if buf is fv:
                    act.wait_ge(conv_out, 2 * 16)
                    for c in range(KT):
                        act.wait_ge(conv_y, c + 1)
                        act.activation(proj[:, c, :], wk[:, 3 + c % 2, :], ACT.Silu).then_inc(conv_done, 1)
                act.activation(buf[:, 0:4, :], ps[:, 4:8, :], ACT.Copy).then_inc(nat_evac, 1)
                act.activation(buf[0:TS, 4, :], ps[0:TS, 2 if buf is mv else 3, :], ACT.Copy).then_inc(nat_evac, 1)
            high_unit(U_SMALL + RING)

            act.wait_ge(nat_evac, 5)
            act.dma_start(o["fv_p"], fv[:, 0:4, :]).then_inc(early_out, 16)
            act.dma_start(o["fv_s"], fv[0:TS, 4, :]).then_inc(early_out, 16)

            act.wait_ge(row_dve, 2)
            act.activation(trow[:, :], zrow[:, :], ACT.Abs).then_inc(row_act, 1)
            act.wait_ge(row_act, 1)
            act.activation(trow[:, :], trow[:, :], ACT.Exp, scale=-1.0).then_inc(row_act, 1)
            act.wait_ge(row_act, 2)
            act.activation(trow[:, :], trow[:, :], ACT.Ln, bias=oneb[0:40, 0:1]).then_inc(row_act, 1)

            act.wait_ge(row_dve, 16)
            act.dma_start(o["lf_p"], lsig[32:40, 0:TP]).then_inc(late_out, 16)
            act.dma_start(o["lf_s"], lsig[32:40, TP:T]).then_inc(late_out, 16)
            act.dma_start(o["m_p"], m_row[:, TP - 1:TP]).then_inc(late_out, 16)
            act.dma_start(o["m_s"], m_row[:, T - 1:T]).then_inc(late_out, 16)

            act.wait_ge(small_in, 9 * 16)
            for h in range(HM):
                for j in range(5):
                    q = 5 * h + j
                    n = TP - P * j if j < 4 else TS
                    rows = P if j < 4 else TS
                    act.wait_ge(m_arg, q + 1)
                    buf = wk[0:rows, j % 2, 0:n]
                    act.activation(buf, buf, ACT.Exp).then_inc(m_exp, 1)
                    if j == 0:
                        act.wait_ge(m_bc, h + 1)
                        act.activation(sm[:, 0, :], ps[:, 3, 0:TS], ACT.Exp, bias=m0b[:, h:h + 1]).then_inc(m_act, 1)
                        act.activation(wk[:, 2, 0:TP], ps[:, 4, :], ACT.Exp, scale=-1.0).then_inc(m_act, 1)
                        act.activation(wk[:, 2, TP:T], ps[:, 3, TS:2 * TS], ACT.Exp, scale=-1.0).then_inc(m_act, 1)
                        act.wait_ge(m_dve, N_MD * h + 1)
                        act.activation(ws[:, 0:4], cS[:, 0:4, h], ACT.Exp, bias=ws[:, 6:7]).then_inc(m_act, 1)
                        act.activation(ws[0:TS, 4:5], cS[0:TS, 4, h:h + 1], ACT.Exp, bias=ws[0:TS, 7:8]).then_inc(m_act, 1)
                        act.activation(ws[:, 5:6], m0b[:, h:h + 1], ACT.Exp, bias=ws[:, 7:8]).then_inc(m_act, 1)
                act.wait_ge(m_acc, 5 * h + 5)
                act.activation(wk[:, 3, 0:TP], ps[:, 6, :], ACT.Abs).then_inc(m_act, 1)
                act.activation(wk[:, 3, TP:T], ps[:, 7, TS:2 * TS], ACT.Abs).then_inc(m_act, 1)
                act.wait_ge(m_dve, N_MD * h + 6)
                act.activation(wk[:, 2, :], wk[:, 4, :], ACT.Square).then_inc(m_act, 1)
                act.wait_ge(m_ssq, h + 1)
                act.activation(wk[:, 2, 0:TP], ps[:, 0, :], ACT.Sqrt, bias=epsb[:, 0:1], scale=1.0 / P).then_inc(m_act, 1)
                act.activation(wk[:, 2, TP:T], ps[:, 1, 0:TS], ACT.Sqrt, bias=epsb[:, 0:1], scale=1.0 / P).then_inc(m_act, 1)
                act.activation(wk[:, 3, :], proj[:, MO + h, :], ACT.Sigmoid).then_inc(m_act, 1)
                act.wait_ge(m_dve, N_MD * h + 9)
                act.activation(proj_b[:, MO + h, 0, :], wk[:, 4, :], ACT.Copy).then_inc(m_act, 1)
            act.wait_ge(m_dve, N_MD * HM)
            act.dma_start(o["cn_p"], proj[:, 0:HM, 0:P + 1]).then_inc(late_out, 16)
            act.dma_start(o["cn_s"], proj[:, 0:HM, 256:256 + P + 1]).then_inc(late_out, 16)
            act.wait_ge(late_out, 6 * 16)
            act.wait_ge(early_out, 5 * 16)

            def copy_turned(i):
                kind, h, qi = items[i]
                nb = (qi + 1 if qi < 4 else 2) if kind == "fox" else 2
                act.wait_ge(a_tr, i + 1)
                if i >= 2:
                    act.wait_ge(a_pv, i - 1)
                dst = wk[:, 2 + i % 2, 0:512]
                if qi < 4:
                    act.activation(dst[:, 0:nb * P], ps[:, 2 + i % 2, 0:nb * P], ACT.Copy).then_inc(a_pt, 1)
                elif kind == "mem":
                    act.activation(dst.rearrange("p (b t) -> p b t", b=4)[:, 0:2, 0:TS],
                                   ps[:, 2 + i % 2, :].rearrange("p (b t) -> p b t", b=4)[:, 0:2, 0:TS],
                                   ACT.Copy).then_inc(a_pt, 1)
                else:
                    act.activation(dst[:, 0:TS], ps[:, 2 + i % 2, 0:TS], ACT.Copy)
                    act.activation(dst[0:TS, P:P + TS], ps[0:TS, 2 + i % 2, P:P + TS], ACT.Copy).then_inc(a_pt, 1)

            def out_high(i):
                kind, h, qi = items[i]
                if kind == "fox" and h % 2 == 0:
                    return
                slot, n = out_slot(kind, h), P if qi < 4 else TS
                act.wait_ge(a_pv, i + 1)
                act.activation(proj_b[:, slot, 0, qi * P:qi * P + n], ps[:, 4 + out_index(i) % 2, 0:n],
                               ACT.Copy).then_inc(a_oh, 1)

            for i in range(len(items)):
                kind, h, qi = items[i]
                n, cols = P if qi < 4 else TS, columns(kind, qi)
                act.wait_ge(a_neg, i + 1)
                if i >= 2:
                    act.wait_ge(a_tr, i - 1)
                act.activation(wk[0:n, i % 2, 0:cols], ps[0:n, i % 2, 0:cols], ACT.Exp,
                               bias=st[0:n, i % 2, 0:1], scale=scale_of(kind),
                               accum_out=st[0:n, i % 2, 1:2]).then_inc(a_exp, 1)
                if i >= 1:
                    copy_turned(i - 1)
                if i >= 2:
                    out_high(i - 2)
            copy_turned(len(items) - 1)
            out_high(len(items) - 2)
            out_high(len(items) - 1)

            for jp in range(N_JP):
                for u in range(N_PER_JP):
                    n = U_MERGE + jp * N_PER_JP + u
                    if u < NB:
                        for j2 in range(2):
                            r = jp * 12 + 2 * u + j2
                            if j2:
                                act.wait_ge(unit_used, n + 1)
                            else:
                                act.wait_ge(g_ready, jp * NB + u + 1)
                            if jp:
                                act.wait_ge(g_prod, 6 * (jp - 1) + 3 * j2 + u + 1)
                            act.activation(proj[:, 8 + 2 * u + j2, :].rearrange("p (a b) -> p a b", a=2),
                                           ps[:, 2 * (r % 2):2 * (r % 2) + 2, 0:HALF], ACT.Copy).then_inc(g_evac, 1)
                    else:
                        r = jp * 12 + 6 + (u - NB)
                        m = jp * 6 + (u - NB)
                        act.wait_ge(unit_used, n + 1)
                        if m >= 2:
                            act.wait_ge(g_prod, m - 1)
                        act.activation(proj[:, 14 + m % 2, :].rearrange("p (a b) -> p a b", a=2),
                                       ps[:, 2 * (r % 2):2 * (r % 2) + 2, 0:HALF], ACT.Sigmoid).then_inc(g_evac, 1)
                    high_unit(n + RING)
                    if u >= NB and (u - NB) % NB == 0 and jp * 2 + (u - NB) // NB > 0:
                        j = jp * 2 + (u - NB) // NB - 1
                        act.wait_ge(g_acc, 2 * (j + 1))
                        act.activation(mg_hi[:, j, :], proj[:, 16 + j % 2, :], ACT.Copy).then_inc(g_mhi, 1)
            act.wait_ge(g_acc, 2 * KT)
            act.activation(mg_hi[:, KT - 1, :], proj[:, 16 + (KT - 1) % 2, :], ACT.Copy).then_inc(g_mhi, 1)
            for n in range(U_OUT, U_WQ):
                high_unit(n + RING)

            act.wait_ge(x2_ready, KT)
            square(2, xT[:, :, :], proj[:, 0:KT, :])
            act.dma_start(keys[:, :, :], a["keysT"]).then_inc(keys_in, 16)
            root(2, wk[:, 1, :].rearrange("p (a b) -> p a b", a=2), ps[:, 0:2, 0:HALF])
            high(2, proj[:, 8:8 + KT, :], act_hi[:, :, :])

            for q in range(NHC):
                n = U_WQ + q
                act.wait_ge(unit_used, n + 1)
                if q >= 2:
                    act.wait_ge(s_ready, q - 1)
                act.activation(qr[:, q % 2, :].rearrange("p (a b) -> p a b", a=2),
                               ps[:, 2 * (q % 2):2 * (q % 2) + 2, 0:HALF], ACT.Copy).then_inc(q_evac, 1)
                high_unit(n + RING)

            with act.Fori(0, NTT) as i:
                act.wait_ge(tk, i * N_TK + TK_BEST)
                act.activation(trip[:, 2, :], trip[:, 2, :], ACT.Exp).then_inc(tk_exp, 1)

            with act.Fori(0, NBLK // 2) as i:
                for b in range(2):
                    with act.Fori(0, TBLK // GT // 2) as s:
                        for c in range(2):
                            act.wait_ge(b_prod, i * (2 * (TBLK // GT)) + s * 2 + (b * (TBLK // GT) + c + 1))
                            act.wait_ge(b_written[b], i * 16)
                            act.activation(gsb[:, b, :, bass.ds(s * (2 * GT) + c * GT, GT)].rearrange("p k u -> p u k"),
                                           ps[:, c, :].rearrange("p (u k) -> p u k", u=GT),
                                           ACT.Copy).then_inc(b_evac, 1)
            for b in range(2):
                act.wait_ge(b_written[b], 8 * NBLK)

            def split_w(c, pg, k):
                act.wait_ge(w_mul, c + 1)
                act.activation(W_hi[:, pg, k, :], wb[:, k % 2, :], ACT.Copy).then_inc(w_hi_done, 1)

            def peer_act(g, pg, u0, v0, more_v, first=False):
                for k in range(GRP):
                    c = g * GRP + k
                    act.wait_ge(unit_used, u0 + k + 1)
                    if not (first and k < 2):
                        act.wait_ge(w_mul, c - 1)
                    act.activation(hb[:, k % 2, :].rearrange("p (a b) -> p a b", a=2),
                                   ps[:, 2 * (k % 2):2 * (k % 2) + 2, 0:HALF], ACT.Gelu_apprx_tanh).then_inc(gelu_done, 1)
                    if first:
                        high_unit(u0 + k + RING)
                    else:
                        high_half(None, U_PEER + GRP + k, loads_u(g, k))
                    if k:
                        split_w(c - 1, pg, k - 1)
                split_w(g * GRP + GRP - 1, pg, GRP - 1)
                if more_v:
                    for k in range(GRP):
                        act.wait_ge(unit_used, v0 + k + 1)
                        high_half(None, U_PEER + k, loads_v(g, k))

            def loads_u(g, k):
                return g * 32 + 16 * ((U_PEER + GRP + k) // RAW + 1)

            def loads_v(g, k):
                return g * 32 + 16 * ((U_PEER + 2 * GRP + k) // RAW + 1)

            peer_act(0, 0, U_PEER, None, False, first=True)
            with act.Fori(0, (NG - 2) // 2) as i:
                for b in range(2):
                    g = i * 2 + (1 + b)
                    peer_act(g, (1 + b) % 2, pos_u(g), pos_v(g - 1), True)
            peer_act(NG - 1, (NG - 1) % 2, pos_u(NG - 1), None, False)

            act.wait_ge(acc_done, NG * KT)
            square(3, xT[:, :, :], fin_sq[:, :, :])
            root(3, hb[:, 0, :].rearrange("p (a b) -> p a b", a=2), ps[:, 0:2, 0:HALF])

        @block.vector
        def _(dve):
            def norm(i, x, col, rs, h, hi, lo):
                dve.wait_ge(n_rms, i + 1)
                dve.reciprocal(rs, rs).then_inc(n_inv, 1)
                dve.wait_ge(n_inv, i + 1)
                for k in range(KT):
                    dve.scalar_tensor_tensor(out=h[:, k, :], in0=x[:, k, :], scalar=par[:, col + k:col + k + 1],
                                             in1=rs, op0=ALU.mult, op1=ALU.mult).then_inc(n_scaled, 1)
                if hi is not None:
                    dve.wait_ge(n_hi, i + 1)
                    dve.wait_ge(n_scaled, KT * (i + 1))
                    dve.tensor_tensor(lo, h, hi, ALU.subtract).then_inc(n_lo, 1)

            dve.wait_ge(par_in, 16)
            norm(0, mem_x, C_MEM, wk[:, 0, 0:NMEM], mem_h[:, :, :], mem_hi[:, :, :], mem_lo[:, :, :])
            norm(1, xT, C_MIX, wk[:, 1, :], mix_h[:, :, :], act_hi[:, :, :], act_lo[:, :, :])

            for q in range(N_MEMK):
                dve.wait_ge(unit_used, q + 1)
                dve.tensor_copy(mkT[:, q, :], ps[:, 2 * (q % 2), 0:NMEM]).then_inc(t_evac, 1)
            with dve.Fori(0, N_T // RING) as i:
                for k in range(RING):
                    dve.wait_ge(unit_used, i * RING + U_T + k + 1)
                    dve.tensor_copy(proj[:, bass.ds(i * RING + k, 1), :].rearrange("p o (a b) -> p (o a) b", a=2),
                                    ps[:, 2 * (k % 2):2 * (k % 2) + 2, 0:HALF]).then_inc(t_evac, 1)

            dve.wait_ge(t_evac, N_MEMK + N_T)
            dve.wait_ge(cw_in, 16)
            dve.tensor_copy(xs[:, :, 3:3 + TS], proj[:, 0:KT, TP:T]).then_inc(xs_ready, 1)
            dve.wait_ge(xs_ready, 1)
            step = 0
            for c in range(KT):
                y = wk[:, 3 + c % 2, :]
                w = [par[:, C_CW + 8 * j + c:C_CW + 8 * j + c + 1] for j in range(4)]
                if c >= 2:
                    dve.wait_ge(conv_done, c - 1)
                dve.tensor_scalar(y, proj[:, c, :], w[3], par[:, C_CB + c:C_CB + c + 1], ALU.mult,
                                  ALU.add).then_inc(conv_step, 1)
                step += 1
                for j in range(1, 4):
                    dve.wait_ge(conv_step, step)
                    dve.scalar_tensor_tensor(out=y[:, j:TP], in0=proj[:, c, 0:TP - j], scalar=w[3 - j],
                                             in1=y[:, j:TP], op0=ALU.mult, op1=ALU.add)
                    last = dve.scalar_tensor_tensor(out=y[:, TP:T], in0=xs[:, c, 3 - j:3 - j + TS], scalar=w[3 - j],
                                                    in1=y[:, TP:T], op0=ALU.mult, op1=ALU.add)
                    last.then_inc(conv_step if j < 3 else conv_y, 1)
                    step += j < 3

            rd = [0]

            def row(ins, wait=True):
                rd[0] += 1
                ins.then_inc(row_dve, 1)
                if wait:
                    dve.wait_ge(row_dve, rd[0])

            two = lambda x: x.rearrange("p (a b) -> p a b", a=2)
            dve.wait_ge(unit_used, U_SMALL + 1)
            row(dve.tensor_scalar(two(zrow[:, :]), ps[0:40, 0:2, 0:HALF], par[0:40, C_ZB:C_ZB + 1], None, ALU.add), False)
            row(dve.tensor_scalar(two(c_row[:, :]), ps[64:68, 0:2, 0:HALF], par[64:68, C_IB:C_IB + 1], None, ALU.add), True)
            dve.wait_ge(row_act, 3)
            row(dve.scalar_tensor_tensor(out=lsig[:, :], in0=zrow[:, :], scalar=0.0, in1=trow[:, :],
                                         op0=ALU.min, op1=ALU.subtract))
            for lo_, hi_ in ((0, TP), (TP, T)):
                row(dve.tensor_tensor_scan(m_row[:, lo_:hi_], ones[0:4, 0:1].broadcast_to((4, hi_ - lo_)),
                                           lsig[0:4, lo_:hi_], 0.0, ALU.mult, ALU.add), hi_ == T)
            row(dve.tensor_tensor(c_row[:, :], c_row[:, :], m_row[:, :], ALU.subtract))
            dve.wait_ge(small_in, 9 * 16)
            row(dve.tensor_tensor_scan(nM[:, 0:TP], c_row[:, 0:TP], c_row[:, 0:TP], 0.0, ALU.max, ALU.max), False)
            row(dve.tensor_tensor_scan(nM[:, TP:T], c_row[:, TP:T], c_row[:, TP:T], m0[:, 0:1], ALU.max, ALU.max))
            row(dve.tensor_tensor(m_row[:, :], m_row[:, :], nM[:, :], ALU.add))
            row(dve.tensor_scalar(nM[:, :], nM[:, :], -1.0, None, ALU.mult))
            row(dve.tensor_copy(cum[32:40, TP + PAST:704], lsig[32:40, TP:T]), True)
            row(dve.tensor_tensor_scan(cum[32:40, 0:TP], ones[32:40, 0:1].broadcast_to((8, TP)), lsig[32:40, 0:TP],
                                       0.0, ALU.mult, ALU.add), False)
            row(dve.tensor_tensor_scan(wk[32:40, 2, 0:192], ones[32:40, 0:1].broadcast_to((8, 192)),
                                       cum[32:40, TP:704], 0.0, ALU.mult, ALU.add))
            row(dve.tensor_scalar(cum[32:40, 0:TP], cum[32:40, 0:TP], -(FD ** 0.5), None, ALU.mult), False)
            row(dve.tensor_scalar(cum[32:40, TP:704], wk[32:40, 2, 0:192], -(FD ** 0.5), None, ALU.mult))
            dve.wait_ge(c_turned, 1)
            dve.tensor_copy(cS[:, 0:4, :], ps[:, 2, 0:16].rearrange("p (a b) -> p a b", a=4)).then_inc(cS_ready, 1)
            dve.tensor_copy(cS[0:TS, 4, :], ps[0:TS, 2, 16:20]).then_inc(cS_ready, 1)
            row(dve.memset(st[:, :, :], 0.0))
            dve.wait_ge(cS_ready, 2)

            for h in range(HM):
                md = N_MD * h
                dve.wait_ge(m_bc, h + 1)
                dve.tensor_copy(ws[:, 6:7], ps[:, 2, TP - 1:TP])
                dve.tensor_copy(ws[:, 7:8], ps[:, 3, TS - 1:TS]).then_inc(m_dve, 1)

                def argument(j):
                    q = 5 * h + j
                    n = TP - P * j if j < 4 else TS
                    rows = P if j < 4 else TS
                    src = ps[0:rows, 2, P * j:TP] if j < 4 else ps[0:rows, 3, 0:TS]
                    if q >= 2:
                        dve.wait_ge(m_acc, q - 1)
                    dve.tensor_scalar(wk[0:rows, j % 2, 0:n], src, cS[0:rows, j, h:h + 1], 0.0, ALU.add,
                                      ALU.min).then_inc(m_arg, 1)

                def weigh(j):
                    q = 5 * h + j
                    n = TP - P * j if j < 4 else TS
                    rows = P if j < 4 else TS
                    buf = wk[0:rows, j % 2, :]
                    dve.wait_ge(m_exp, q + 1)
                    dve.tensor_tensor(buf[:, 0:rows], buf[:, 0:rows], causal[0:rows, 0:rows], ALU.mult).then_inc(m_mask, 1)
                    dve.wait_ge(m_mask, q + 1)
                    dve.wait_ge(m_s, q + 1)
                    dve.scalar_tensor_tensor(out=buf[:, 0:n], in0=ps[0:rows, j % 2, 0:n], scalar=SQRT_HM,
                                             in1=buf[:, 0:n], op0=ALU.mult, op1=ALU.mult).then_inc(m_sw, 1)

                argument(0)
                argument(1)
                dve.wait_ge(m_act, N_MA * h + 1)
                dve.tensor_tensor(sm[:, 1, :], sm[:, 0, :], proj[:, MQ + h, TP:T], ALU.mult).then_inc(m_dve, 1)
                for j in range(5):
                    weigh(j)
                    if j + 2 < 5:
                        argument(j + 2)
                dve.wait_ge(m_act, N_MA * h + 8)
                dve.tensor_tensor(wk[:, 3, :], wk[:, 3, :], wk[:, 2, :], ALU.max).then_inc(m_dve, 1)
                dve.wait_ge(m_dve, md + 3)
                dve.reciprocal(wk[:, 3, :], wk[:, 3, :]).then_inc(m_dve, 1)
                dve.wait_ge(m_dve, md + 4)
                dve.tensor_tensor(wk[:, 4, 0:TP], ps[:, 5, :], wk[:, 3, 0:TP], ALU.mult).then_inc(m_dve, 1)
                dve.tensor_tensor(wk[:, 4, TP:T], ps[:, 7, 0:TS], wk[:, 3, TP:T], ALU.mult).then_inc(m_dve, 1)
                dve.wait_ge(m_act, N_MA * h + 11)
                dve.reciprocal(wk[:, 2, :], wk[:, 2, :]).then_inc(m_dve, 1)
                dve.wait_ge(m_dve, md + 7)
                dve.scalar_tensor_tensor(out=wk[:, 4, :], in0=wk[:, 4, :], scalar=par[:, C_HEAD + h:C_HEAD + h + 1],
                                         in1=wk[:, 2, :], op0=ALU.mult, op1=ALU.mult).then_inc(m_dve, 1)
                dve.wait_ge(m_dve, md + 8)
                dve.wait_ge(m_act, N_MA * h + 12)
                dve.tensor_tensor(wk[:, 4, :], wk[:, 4, :], wk[:, 3, :], ALU.mult).then_inc(m_dve, 1)
                dve.wait_ge(m_kt, h + 1)
                for j in range(4):
                    dve.tensor_scalar(wk[:, 0, j * P:(j + 1) * P], ps[:, 4, j * P:(j + 1) * P], ws[:, j:j + 1], SQRT_HM,
                                      ALU.mult, ALU.mult)
                dve.tensor_scalar(wk[0:TS, 1, 0:P], ps[0:TS, 3, 128:256], ws[0:TS, 4:5], SQRT_HM, ALU.mult,
                                  ALU.mult).then_inc(m_dve, 1)
                dve.wait_ge(m_act, N_MA * h + 13)
                dve.wait_ge(m_dve, md + 9)
                dve.tensor_tensor(proj_b[:, MO + h, 1, :], wk[:, 4, :], proj_b[:, MO + h, 0, :],
                                  ALU.subtract).then_inc(m_dve, 1)
                dve.wait_ge(m_st, h + 1)
                dve.tensor_copy(proj[:, MQ + h, 0:P + 1], ps[:, 2, 0:P + 1]).then_inc(m_dve, 1)
                dve.scalar_tensor_tensor(out=proj[:, MQ + h, 256:256 + P], in0=c0[:, h, :], scalar=ws[:, 5:6],
                                         in1=ps[:, 2, 256:256 + P], op0=ALU.mult, op1=ALU.add)
                dve.scalar_tensor_tensor(out=proj[:, MQ + h, 384:385], in0=n0[:, h:h + 1], scalar=ws[:, 5:6],
                                         in1=ps[:, 2, 384:385], op0=ALU.mult, op1=ALU.add).then_inc(m_dve, 1)

            def maxima(i):
                kind, h, qi = items[i]
                n, cols = P if qi < 4 else TS, columns(kind, qi)
                dve.wait_ge(a_sc, i + 1)
                if i >= 2:
                    dve.wait_ge(a_norm, i - 1)
                dve.reduce_max(st[0:n, i % 2, 3:4], ps[0:n, i % 2, 0:cols], AX.X).then_inc(a_max, 1)
                dve.wait_ge(a_max, i + 1)
                dve.tensor_scalar(st[0:n, i % 2, 0:1], st[0:n, i % 2, 3:4], -scale_of(kind), None,
                                  ALU.mult).then_inc(a_neg, 1)

            def out_low(i):
                kind, h, qi = items[i]
                if kind == "fox" and h % 2 == 0:
                    return
                slot, n, x = out_slot(kind, h), P if qi < 4 else TS, out_index(i)
                dve.wait_ge(a_oh, x + 1)
                dve.tensor_tensor(proj_b[:, slot, 1, qi * P:qi * P + n], ps[:, 4 + x % 2, 0:n],
                                  proj_b[:, slot, 0, qi * P:qi * P + n], ALU.subtract).then_inc(a_ol, 1)

            dve.wait_ge(late_out, 6 * 16)
            def queries_apart(hp):
                for hh in range(2):
                    rows = slice(FD * hh, FD * hh + FD)
                    last = dve.tensor_copy(qz[rows, hp % 2, hh, :], proj[rows, FQ + hp, :])
                last.then_inc(q_apart, 1)

            dve.memset(qz[FD:P, :, 0, :], 0.0)
            dve.memset(qz[0:FD, :, 1, :], 0.0)
            queries_apart(0)
            queries_apart(1)
            maxima(0)
            for i in range(len(items)):
                kind, h, qi = items[i]
                n, cols = P if qi < 4 else TS, columns(kind, qi)
                if i + 1 < len(items):
                    maxima(i + 1)
                if kind == "fox" and i % (2 * NTT) == 0 and 1 <= i // (2 * NTT) < HF // 2 - 1:
                    queries_apart(i // (2 * NTT) + 1)
                dve.wait_ge(a_exp, i + 1)
                dve.reciprocal(st[0:n, i % 2, 2:3], st[0:n, i % 2, 1:2]).then_inc(a_rcp, 1)
                dve.wait_ge(a_rcp, i + 1)
                dve.tensor_scalar(wk[0:n, i % 2, 0:cols], wk[0:n, i % 2, 0:cols], st[0:n, i % 2, 2:3], None,
                                  ALU.mult).then_inc(a_norm, 1)
                if i >= 2:
                    out_low(i - 2)
            out_low(len(items) - 2)
            out_low(len(items) - 1)

            def merged_low(j):
                dve.wait_ge(g_mhi, j + 1)
                dve.tensor_tensor(mg_lo[:, j, :], proj[:, 16 + j % 2, :], mg_hi[:, j, :], ALU.subtract).then_inc(g_mlo, 1)

            for j in range(KT):
                jp, j2 = j // 2, j % 2
                acc = proj[:, 16 + j % 2, :]
                for b in range(NB):
                    m = 3 * j + b
                    if b == 0 and j >= 2:
                        dve.wait_ge(g_mlo, j - 1)
                    if b == 2:
                        dve.wait_ge(g_acc, 2 * j + 1)
                    dve.wait_ge(g_evac, jp * 12 + 6 + 3 * j2 + b + 1)
                    dst = acc if b == 0 else proj[:, 17 + b, :]
                    dve.tensor_tensor(dst, proj[:, 14 + m % 2, :], proj[:, 8 + 2 * b + j2, :], ALU.mult).then_inc(g_prod, 1)
                    if b:
                        dve.wait_ge(g_prod, m + 1)
                        dve.tensor_tensor(acc, acc, dst, ALU.add).then_inc(g_acc, 1)
                if j:
                    merged_low(j - 1)
            merged_low(KT - 1)

            for j in range(KT):
                dve.wait_ge(unit_used, U_OUT + j + 1)
                dve.tensor_tensor(two(xT[:, j, :]), ps[:, 2 * (j % 2):2 * (j % 2) + 2, 0:HALF], two(xT[:, j, :]),
                                  ALU.add).then_inc(x2_ready, 1)
            dve.wait_ge(x2_ready, KT)
            norm(2, xT, C_FFN, wk[:, 1, :], proj[:, 8:8 + KT, :], act_hi[:, :, :], act_lo[:, :, :])

            dve.wait_ge(n_lo, 3)
            dve.memset(S[64:128, 4, :, :], 0.0)
            for q in range(NHC):
                dve.wait_ge(s_ready, q + 1)
                dve.tensor_copy(S[:, 0:4, q, :], ps[:, 4 + 2 * (q % 2), :].rearrange("p (a b) -> p a b", a=4))
                dve.tensor_copy(S[0:TS, 4, q, :], ps[0:TS, 5 + 2 * (q % 2), 0:NKEY]).then_inc(s_evac, 1)
            dve.wait_ge(s_evac, NHC)

            with dve.Fori(0, NTT) as i:
                k = [0]

                def step(ins, wait=True):
                    k[0] += 1
                    ins.then_inc(tk, 1)
                    if wait:
                        dve.wait_ge(tk, i * N_TK + k[0])

                def hold():
                    dve.memset(gs[:, 0, :], 0.0)

                def top16(src, rest, vals, idx, count):
                    hold()
                    for x in range(count):
                        ins = dve.max(vals[:, x, 0:8], src[:, x, :])
                    step(ins)
                    hold()
                    for x in range(count):
                        dve.max_index(idx[:, x, 0:8], vals[:, x, 0:8], src[:, x, :])
                        ins = dve.match_replace(rest[:, x, :], vals[:, x, 0:8], src[:, x, :], -3e38)
                    step(ins)
                    hold()
                    for x in range(count):
                        ins = dve.max(vals[:, x, 8:16], rest[:, x, :])
                    step(ins)
                    hold()
                    for x in range(count):
                        ins = dve.max_index(idx[:, x, 8:16], vals[:, x, 8:16], rest[:, x, :])
                    step(ins)

                step(dve.tensor_copy(sA[:, :, :], S[:, bass.ds(i, 1), :, :].rearrange("p o a b -> p (o a) b")))
                top16(sA, sB, top, topi, NHC)
                step(dve.tensor_copy(topf[:, :, :], topi[:, :, :]))
                for h in range(NPH):
                    ins = dve.tensor_tensor(candA[:, h, :].rearrange("p (a b) -> p a b", a=TOPK),
                                            top[:, 2 * h, :].unsqueeze(2).broadcast_to((P, TOPK, TOPK)),
                                            top[:, 2 * h + 1, :].unsqueeze(1).broadcast_to((P, TOPK, TOPK)), ALU.add)
                step(ins)
                top16(candA, candB, best, bi, NPH)
                step(dve.tensor_scalar(ab[:, 0, :, :], bi[:, :, :], 4, None, ALU.logical_shift_right), False)
                step(dve.tensor_scalar(ab[:, 1, :, :], bi[:, :, :], 15, None, ALU.bitwise_and))
                step(dve.tensor_copy(abf[:, :, :, :], ab[:, :, :, :]))
                for half in range(2):
                    step(dve.tensor_tensor(eq, abf[:, half, :, :].rearrange("p h k -> p (h k)").unsqueeze(2)
                                           .broadcast_to((P, P, TOPK)),
                                           iota[:, 0:TOPK].unsqueeze(1).broadcast_to((P, P, TOPK)), ALU.is_equal))
                    eh = eq.rearrange("p (h k) c -> p h k c", h=NPH)
                    for h in range(NPH):
                        ins = dve.tensor_tensor(eh[:, h, :, :], eh[:, h, :, :],
                                                topf[:, 2 * h + half, :].unsqueeze(1).broadcast_to((P, TOPK, TOPK)),
                                                ALU.mult)
                    step(ins)
                    if half == 0:
                        dve.wait_ge(tk_turned, i)
                    step(dve.tensor_reduce(trip[:, half, :], eq, AX.X, ALU.add))
                w3 = trip[:, 2, :].rearrange("p (h k) -> p h k", h=NPH)
                step(dve.tensor_tensor(w3, best[:, :, :], best[:, :, 0:1].broadcast_to((P, NPH, TOPK)), ALU.subtract))
                assert k[0] == TK_BEST
                dve.wait_ge(tk_exp, i + 1)
                step(dve.tensor_reduce(gs[:, 0, :], w3, AX.X, ALU.add))
                step(dve.reciprocal(gs[:, 1, :], gs[:, 0, :]))
                step(dve.tensor_tensor(w3, w3, gs[:, 1, :].unsqueeze(2).broadcast_to((P, NPH, TOPK)), ALU.mult))
                assert k[0] == TK_TRIP
                dve.wait_ge(tk_turned, i + 1)
                step(dve.tensor_copy(pair[:, :, bass.ds(i * P, P)], ps[:, 0, 0:3 * P].rearrange("p (c t) -> p c t", c=3)))
                assert k[0] == N_TK

            def one_hots(i, first=False):
                for c in range(2):
                    if not first:
                        dve.wait_ge(b_prod, i * 2 + c - 1)
                    dve.tensor_copy(tcol[:, c, :, :], pair[:, :, bass.ds(i * (2 * GT) + c * GT, GT)]).then_inc(b_col, 1)
                    dve.wait_ge(b_col, i * 2 + c + 1)
                    for u in range(GT):
                        dve.tensor_scalar(hot2[:, c, u, :], iota[:, :], tcol[:, c, 1, u:u + 1], None, ALU.is_equal)
                        last = dve.tensor_scalar(hot1[:, c, u, :], iota[:, :], tcol[:, c, 0, u:u + 1],
                                                 tcol[:, c, 2, u:u + 1], ALU.is_equal, ALU.mult)
                    last.then_inc(b_hot, 1)

            one_hots(0, first=True)
            with dve.Fori(1, T // GT // 2) as i:
                one_hots(i)

            def w_low(c, pg, k):
                dve.wait_ge(w_hi_done, c + 1)
                dve.tensor_tensor(W_lo[:, pg, k, :], wb[:, k % 2, :], W_hi[:, pg, k, :], ALU.subtract).then_inc(w_lo_done, 1)

            def peer_w(g, pg, loads):
                dve.wait_ge(g_in[pg], loads)
                for k in range(GRP):
                    c = g * GRP + k
                    dve.wait_ge(gelu_done, c + 1)
                    if k >= 2:
                        dve.wait_ge(w_lo_done, c - 1)
                    dve.tensor_tensor(wb[:, k % 2, :], hb[:, k % 2, :], Gb[:, pg, k, :], ALU.mult).then_inc(w_mul, 1)
                    if k:
                        w_low(c - 1, pg, k - 1)
                w_low(g * GRP + GRP - 1, pg, GRP - 1)

            def peer_acc(g, last=False):
                for d in range(KT):
                    if d < KT - 1:
                        dve.wait_ge(v_ready, g * (KT - 1) + d + 1)
                    else:
                        dve.wait_ge(unit_used, pos_v(g, last) + GRP)
                    dve.tensor_tensor(two(xT[:, d, :]), ps[:, 4 + 2 * (d % 2):6 + 2 * (d % 2), 0:HALF], two(xT[:, d, :]),
                                      ALU.add).then_inc(acc_done, 1)

            peer_w(0, 0, 16)
            with dve.Fori(0, (NG - 2) // 2) as i:
                for b in range(2):
                    g = i * 2 + (1 + b)
                    dve.wait_ge(w_lo_done, g * GRP)
                    peer_w(g, (1 + b) % 2, i * 16 + (16 if b == 0 else 32))
                    peer_acc(g - 1)
            dve.wait_ge(w_lo_done, (NG - 1) * GRP)
            peer_w(NG - 1, (NG - 1) % 2, 16 * (NG // 2))
            peer_acc(NG - 2)
            peer_acc(NG - 1, last=True)
            norm(3, xT, C_FIN, hb[:, 0, :], fin_y, None, None)

        @block.tensor
        def _(pe):
            def sums(i, sq, out, n):
                pe.wait_ge(n_sq, i + 1)
                for half in range(len(out)):
                    for k in range(KT):
                        last = pe.matmul(out[half], ones[:, :], sq[:, k, half * n:(half + 1) * n],
                                         start=(k == 0), stop=(k == KT - 1))
                last.then_inc(n_ssq, 1)

            def tile(slot, rhs_hi, rhs_lo, bank, kts=KT, width=P, c0_=0, n=HALF, halves=2):
                for k in range(kts):
                    col = k * width + c0_
                    for w, x in ((w_hi, rhs_hi), (w_hi, rhs_lo), (w_lo, rhs_hi)):
                        for half in range(halves):
                            last = pe.matmul(ps[:, bank + half, 0:n], w[:, slot, col:col + P],
                                             x(k)[:, half * n:(half + 1) * n],
                                             start=(k == 0 and w is w_hi and x is rhs_hi),
                                             stop=(k == kts - 1 and w is w_lo))
                return last

            def natural(first, u, hi, lo, frames, banks):
                n = first + u
                pe.wait_ge(lo_ready, n + 1)
                for (f0, nf), bank in zip(frames, banks):
                    for k2 in range(2):
                        k = 2 * u + k2
                        for x, w in ((hi, w_hi), (lo, w_hi), (hi, w_lo)):
                            last = pe.matmul(ps[0:nf, bank, :], x[:, k, f0:f0 + nf],
                                             w[:, n % RING, k2 * 512:(k2 + 1) * 512],
                                             start=(k == 0 and x is hi and w is w_hi), stop=(k == KT - 1 and w is w_lo))
                last.then_inc(unit_used, 1)

            a_hi, a_lo = (lambda k: act_hi[:, k, :]), (lambda k: act_lo[:, k, :])

            pe.wait_ge(consts, 8)
            sums(0, mem_sq, [ps[:, 4, 0:NMEM]], NMEM)
            sums(1, mix_sq, [ps[:, 0, 0:HALF], ps[:, 1, 0:HALF]], HALF)

            pe.wait_ge(n_lo, 1)
            pe.wait_ge(n_rms, 2)
            for q in range(N_MEMK):
                pe.wait_ge(lo_ready, q + 1)
                if q >= 2:
                    pe.wait_ge(t_evac, q - 1)
                tile(q % RING, lambda k: mem_hi[:, k, :], lambda k: mem_lo[:, k, :], 2 * (q % 2), n=NMEM,
                     halves=1).then_inc(unit_used, 1)
            for u in range(N_MEMV):
                natural(U_MEMV, u, mem_hi, mem_lo, [(0, P), (P, P)], [4, 5])

            pe.wait_ge(n_lo, 2)
            with pe.Fori(0, N_T // RING) as i:
                for k in range(RING):
                    pe.wait_ge(lo_ready, i * RING + U_T + k + 1)
                    pe.wait_ge(t_evac, i * RING + N_MEMK + k - 1)
                    tile((U_T + k) % RING, a_hi, a_lo, 2 * (k % 2)).then_inc(unit_used, 1)
            frames = [(t * P, P) for t in range(4)] + [(TP, TS)]
            pe.wait_ge(nat_evac, 1)
            pe.wait_ge(t_evac, N_MEMK + N_T)
            for u in range(N_MV):
                natural(U_MV, u, act_hi, act_lo, frames, [4, 5, 6, 7, 2])
            pe.wait_ge(nat_evac, 3)
            for u in range(N_FV):
                natural(U_FV, u, act_hi, act_lo, frames, [4, 5, 6, 7, 3])
            pe.wait_ge(lo_ready, U_SMALL + 1)
            tile(U_SMALL % RING, a_hi, a_lo, 0).then_inc(unit_used, 1)

            pe.wait_ge(row_dve, 8)
            pe.wait_ge(nat_evac, 5)
            for t in range(NTT):
                n = P if t < 4 else TS
                last = pe.transpose(ps[0:n, 2, 4 * t:4 * t + 4], c_row[:, t * P:t * P + n], ident[0:4, 0:4])
            last.then_inc(c_turned, 1)

            pe.wait_ge(row_dve, 16)
            pe.wait_ge(cS_ready, 2)
            pe.wait_ge(conv_done, KT)
            pe.wait_ge(small_in, 9 * 16)
            for h in range(HM):
                pick = ident[0:4, h:h + 1].broadcast_to((4, P))
                qT, kT = proj[:, MQ + h, :], proj[:, MK + h, :]
                if h:
                    pe.wait_ge(m_dve, N_MD * h)
                pe.matmul(ps[:, 2, :], pick, nM[:, 0:TP], start=True, stop=True)
                pe.matmul(ps[:, 3, 0:TS], pick, nM[:, TP:T], start=True, stop=True)
                pe.matmul(ps[:, 4, :], pick, m_row[:, 0:TP], start=True, stop=True)
                pe.matmul(ps[:, 3, TS:2 * TS], pick, m_row[:, TP:T], start=True, stop=True).then_inc(m_bc, 1)

                def scores(j):
                    q = 5 * h + j
                    if j >= 2:
                        pe.wait_ge(m_sw, q - 1)
                    if j < 4:
                        pe.matmul(ps[:, j % 2, 0:TP - P * j], kT[:, P * j:P * (j + 1)], qT[:, P * j:TP],
                                  start=True, stop=True).then_inc(m_s, 1)
                    else:
                        pe.matmul(ps[0:TS, 0, 0:TS], kT[:, TP:T], qT[:, TP:T], start=True, stop=True).then_inc(m_s, 1)

                scores(0)
                scores(1)
                for j in range(5):
                    pe.wait_ge(m_sw, 5 * h + j + 1)
                    if j < 4:
                        sw = wk[:, j % 2, 0:TP - P * j]
                        pe.matmul(ps[:, 5, P * j:TP], mv[:, j, P * h:P * (h + 1)], sw, start=(j == 0), stop=(j == 3))
                        pe.matmul(ps[:, 6, P * j:TP], ones[:, :], sw, start=(j == 0), stop=(j == 3)).then_inc(m_acc, 1)
                    else:
                        sw = wk[0:TS, 0, 0:TS]
                        pe.wait_ge(m_dve, N_MD * h + 2)
                        pe.matmul(ps[:, 7, 0:TS], mv[0:TS, 4, P * h:P * (h + 1)], sw, start=True, stop=False)
                        pe.matmul(ps[:, 7, 0:TS], c0[:, h, :], sm[:, 1, :], start=False, stop=True)
                        pe.matmul(ps[:, 7, TS:2 * TS], ones[0:TS, :], sw, start=True, stop=False)
                        pe.matmul(ps[:, 7, TS:2 * TS], n0[:, h:h + 1].broadcast_to((P, P)), sm[:, 1, :], start=False,
                                  stop=True).then_inc(m_acc, 1)
                    if j + 2 < 5:
                        scores(j + 2)
                pe.wait_ge(m_act, N_MA * h + 3)
                for j in range(4):
                    pe.transpose(ps[:, 4, P * j:P * (j + 1)], kT[:, P * j:P * (j + 1)], ident[:, :])
                pe.transpose(ps[0:TS, 3, 128:256], kT[:, TP:T], ident[:, :]).then_inc(m_kt, 1)
                pe.wait_ge(m_act, N_MA * h + 9)
                pe.matmul(ps[:, 0, :], ones[:, :], wk[:, 2, 0:TP], start=True, stop=True)
                pe.matmul(ps[:, 1, 0:TS], ones[:, :], wk[:, 2, TP:T], start=True, stop=True).then_inc(m_ssq, 1)
                pe.wait_ge(m_dve, N_MD * h + 10)
                for col, rhs in ((0, lambda j: mv[:, j, P * h:P * (h + 1)]), (P, lambda j: ones[:, 0:1])):
                    for j in range(4):
                        pe.matmul(ps[:, 2, col:col + (P if col == 0 else 1)], wk[:, 0, P * j:P * (j + 1)], rhs(j),
                                  start=(j == 0), stop=(j == 3))
                pe.matmul(ps[:, 2, 256:256 + P], wk[0:TS, 1, 0:P], mv[0:TS, 4, P * h:P * (h + 1)], start=True, stop=True)
                pe.matmul(ps[:, 2, 384:385], wk[0:TS, 1, 0:P], ones[0:TS, 0:1], start=True, stop=True).then_inc(m_st, 1)

            def att_scores(i):
                kind, h, qi = items[i]
                n, cols = P if qi < 4 else TS, columns(kind, qi)
                out = ps[0:n, i % 2, 0:cols]
                if i >= 2:
                    pe.wait_ge(a_exp, i - 1)
                if kind == "mem":
                    keys_ = mkT if qi < 4 else kc
                    pe.matmul(out, proj[:, CQ + h, qi * P:qi * P + n], keys_[:, h, :], start=True, stop=True).then_inc(a_sc, 1)
                    return
                hp = h // 2
                pe.wait_ge(q_apart, hp + 1)
                q = qz[:, hp % 2, h % 2, qi * P:qi * P + n]
                pick = ident[:, 32 + h:33 + h].broadcast_to((P, n))
                c_lo = 0 if qi < 4 else TP
                pe.matmul(out, pick, cum[:, c_lo:c_lo + cols], start=True, stop=False)
                if qi < 4:
                    pe.matmul(out, q, proj[:, FK + hp, 0:cols], start=False, stop=False)
                else:
                    pe.matmul(out[:, 0:PAST], q, kpast[:, hp, :], start=False, stop=False)
                    pe.matmul(out[:, PAST:cols], q, proj[:, FK + hp, TP:T], start=False, stop=False)
                pe.matmul(out[:, cols - n:cols], identb[0:n, 0:n], maskneg[0:n, 0:n], start=False,
                          stop=True).then_inc(a_sc, 1)

            def att_values(i):
                kind, h, qi = items[i]
                n, cols = P if qi < 4 else TS, columns(kind, qi)
                blocks = [(b * P, min(P, cols - b * P)) for b in range((cols + P - 1) // P)]
                pe.wait_ge(a_norm, i + 1)
                if i >= 2:
                    pe.wait_ge(a_pt, i - 1)
                for b, (s0, ns) in enumerate(blocks):
                    last = pe.transpose(ps[0:ns, 2 + i % 2, b * P:b * P + n], wk[0:n, i % 2, s0:s0 + ns], ident[0:n, 0:n])
                last.then_inc(a_tr, 1)

            def att_out(i):
                kind, h, qi = items[i]
                n, cols = P if qi < 4 else TS, columns(kind, qi)
                blocks = [(b * P, min(P, cols - b * P)) for b in range((cols + P - 1) // P)]
                x = out_index(i)
                pe.wait_ge(a_pt, i + 1)
                if x >= 2:
                    pe.wait_ge(a_ol, x - 1)
                r0 = FD * (h % 2) if kind == "fox" else 0
                rows = FD if kind == "fox" else P
                for b, (s0, ns) in enumerate(blocks):
                    if kind == "mem":
                        v = (mvN if qi < 4 else vc)[:, b, P * h:P * (h + 1)]
                    elif qi < 4:
                        v = fv[:, b, FD * h:FD * (h + 1)]
                    else:
                        v = vpast[:, FD * h:FD * (h + 1)] if b == 0 else fv[0:TS, 4, FD * h:FD * (h + 1)]
                    last = pe.matmul(ps[r0:r0 + rows, 4 + x % 2, 0:n], v, wk[0:ns, 2 + i % 2, b * P:b * P + n],
                                     start=(b == 0), stop=(b == len(blocks) - 1))
                last.then_inc(a_pv, 1)

            pe.wait_ge(m_dve, N_MD * HM)
            pe.wait_ge(m_act, N_MA * HM)
            att_scores(0)
            for i in range(len(items)):
                if i + 1 < len(items):
                    att_scores(i + 1)
                att_values(i)
                if i >= 1:
                    att_out(i - 1)
            att_out(len(items) - 1)

            branch_slot = [MO, 0, 4]
            pe.wait_ge(a_ol, HF * NTT // 2 + HC * NTT)
            for jp in range(N_JP):
                for u in range(N_PER_JP):
                    n = U_MERGE + jp * N_PER_JP + u
                    pe.wait_ge(lo_ready, n + 1)
                    if u < NB:
                        s0 = branch_slot[u]
                        for j2 in range(2):
                            r = jp * 12 + 2 * u + j2
                            if r >= 2:
                                pe.wait_ge(g_evac, r - 1)
                            last = tile(n % RING, lambda k: proj_b[:, s0 + k, 0, :], lambda k: proj_b[:, s0 + k, 1, :],
                                        2 * (r % 2), kts=4, width=2 * P, c0_=j2 * P)
                            last.then_inc(unit_used if j2 else g_ready, 1)
                    else:
                        r = jp * 12 + 6 + (u - NB)
                        pe.wait_ge(g_evac, r - 1)
                        tile(n % RING, a_hi, a_lo, 2 * (r % 2)).then_inc(unit_used, 1)

            pe.wait_ge(g_mlo, KT)
            pe.wait_ge(g_evac, 12 * N_JP)
            for j in range(KT):
                n = U_OUT + j
                pe.wait_ge(lo_ready, n + 1)
                if j >= 2:
                    pe.wait_ge(x2_ready, j - 1)
                tile(n % RING, lambda k: mg_hi[:, k, :], lambda k: mg_lo[:, k, :], 2 * (j % 2)).then_inc(unit_used, 1)

            sums(2, proj[:, 0:KT, :], [ps[:, 0, 0:HALF], ps[:, 1, 0:HALF]], HALF)

            def key_scores(q):
                pe.wait_ge(q_evac, q + 1)
                if q >= 2:
                    pe.wait_ge(s_evac, q - 1)
                for t in range(NTT):
                    n = P if t < 4 else TS
                    bank, col = (4 + 2 * (q % 2), t * P) if t < 4 else (5 + 2 * (q % 2), 0)
                    last = pe.matmul(ps[0:n, bank, col:col + NKEY], qr[:, q % 2, t * P:t * P + n], keys[:, q, :],
                                     start=True, stop=True)
                last.then_inc(s_ready, 1)

            pe.wait_ge(n_lo, 3)
            pe.wait_ge(n_rms, 3)
            pe.wait_ge(keys_in, 16)
            for q in range(NHC):
                n = U_WQ + q
                pe.wait_ge(lo_ready, n + 1)
                if q >= 2:
                    pe.wait_ge(q_evac, q - 1)
                tile(n % RING, a_hi, a_lo, 2 * (q % 2)).then_inc(unit_used, 1)
                if q:
                    key_scores(q - 1)
            key_scores(NHC - 1)

            pe.wait_ge(q_evac, NHC)
            with pe.Fori(0, NTT) as i:
                pe.wait_ge(tk, i * N_TK + TK_TRIP)
                for c in range(3):
                    last = pe.transpose(ps[:, 0, c * P:(c + 1) * P], trip[:, c, :], ident[:, :])
                last.then_inc(tk_turned, 1)

            pe.wait_ge(tk, NTT * N_TK)
            def g_products(i, first=False):
                for c in range(2):
                    pe.wait_ge(b_hot, i * 2 + c + 1)
                    if not first:
                        pe.wait_ge(b_evac, i * 2 + c - 1)
                    for u in range(GT):
                        last = pe.matmul(ps[:, c, u * P:(u + 1) * P], hot2[:, c, u, :], hot1[:, c, u, :],
                                         start=True, stop=True)
                    last.then_inc(b_prod, 1)

            g_products(0, first=True)
            with pe.Fori(1, T // GT // 2) as i:
                g_products(i)
            pe.wait_ge(b_evac, T // GT)

            def peer_h(g, u0, first=False):
                for k in range(GRP):
                    pe.wait_ge(lo_ready, u0 + k + 1)
                    if not (first and k < 2):
                        pe.wait_ge(gelu_done, g * GRP + k - 1)
                    tile((U_PEER + (0 if first else GRP) + k) % RING, a_hi, a_lo, 2 * (k % 2)).then_inc(unit_used, 1)

            def peer_v(g, pg, first=False, last_g=False):
                pe.wait_ge(lo_ready, pos_v(g, last_g) + GRP)
                pe.wait_ge(w_lo_done, g * GRP + GRP)
                for d in range(KT):
                    if not (first and d < 2):
                        pe.wait_ge(acc_done, g * KT + d - 1)
                    bank = 4 + 2 * (d % 2)
                    for k in range(GRP):
                        slot = (U_PEER + (1 if last_g else 2) * GRP + k) % RING
                        for w, x in ((w_hi, W_hi), (w_hi, W_lo), (w_lo, W_hi)):
                            for half in range(2):
                                last = pe.matmul(ps[:, bank + half, 0:HALF], w[:, slot, d * P:(d + 1) * P],
                                                 x[:, pg, k, half * HALF:(half + 1) * HALF],
                                                 start=(k == 0 and w is w_hi and x is W_hi),
                                                 stop=(k == GRP - 1 and w is w_lo))
                        if d == KT - 1:
                            last.then_inc(unit_used, 1)
                    if d < KT - 1:
                        last.then_inc(v_ready, 1)

            peer_h(0, U_PEER, first=True)
            peer_h(1, pos_u(1))
            peer_v(0, 0, first=True)
            with pe.Fori(0, (NG - 2) // 2) as i:
                for b in range(2):
                    g = i * 2 + (2 + b)
                    peer_h(g, pos_u(g))
                    peer_v(g - 1, (1 + b) % 2)
            peer_v(NG - 1, (NG - 1) % 2, last_g=True)

            sums(3, fin_sq, [ps[:, 0, 0:HALF], ps[:, 1, 0:HALF]], HALF)


_OUTS = {
    "y": (P, KT, T), "fk": (P, 4, T), "fv_p": (P, 4, 512), "fv_s": (TS, 512), "lf_p": (8, TP), "lf_s": (8, TS),
    "cn_p": (P, HM, P + 1), "m_p": (HM, 1), "conv_p": (P, KT, 3), "memk": (P, HC, NMEM),
    "memv": (P, 2, 512), "cn_s": (P, HM, P + 1), "m_s": (HM, 1), "conv_s": (P, KT, 3),
}


def kernel(**x):
    import numpy as np
    import concourse.bacc as bacc
    from concourse.bass_utils import run_bass_kernel_spmd as run

    x = {k: np.asarray(v) for k, v in x.items()}
    f32 = np.float32
    assert x["x_prompt"].shape == (1, TP, D) and x["x_sample"].shape == (1, TS, D)

    def channels(v):
        return v.reshape((-1, P) + v.shape[1:]).swapaxes(0, 1)

    def tiles(w, width=P):
        k, c = w.shape
        return w.reshape(k // P, P, c // width, width).transpose(2, 1, 0, 3).reshape(c // width, P, -1)

    def pairs(w):
        return w.reshape(4, 2, P, 512).transpose(0, 2, 1, 3).reshape(4, P, 1024)

    w_in = x["w_in"][0]
    bounds = np.cumsum([0, 512, 512, 512, 512, HM, HM, 512, 512, 512, HF, 512, NB * D])
    mq, mk, mv, mo, mi, mf, fq, fk, fv, ff, cq, gates = [w_in[:, s:e] for s, e in zip(bounds[:-1], bounds[1:])]
    small = np.zeros((D, P), f32)
    small[:, 0:HM], small[:, 32:32 + HF], small[:, 64:64 + HM] = mf, ff, mi
    memkv = x["w_mem_kv"][0]
    gate_units = tiles(gates)
    up_units = [tiles(x[n][0], 2 * P) for n in ("w_up_m", "w_up_f", "w_up_c")]
    merge = []
    for jp in range(N_JP):
        merge += [up_units[b][jp] for b in range(NB)]
        merge += [gate_units[b * KT + 2 * jp + j2] for j2 in range(2) for b in range(NB)]
    units = np.concatenate([
        tiles(memkv[:, :512]), pairs(memkv[:, 512:]),
        tiles(np.concatenate([mq, mk, fq, fk, cq, mo], axis=1)), pairs(mv), pairs(fv), tiles(small),
        np.stack(merge), tiles(x["w_out"][0]), tiles(x["peer_wq"][0]),
    ])
    assert units.shape == (U_PEER, P, 1024)

    par = np.zeros((P, N_PAR), f32)
    for col, name in ((C_MIX, "norm_mix"), (C_FFN, "norm_ffn"), (C_FIN, "norm_final"), (C_MEM, "norm_mem")):
        par[:, col:col + KT] = channels(x[name].reshape(-1))
    par[:, C_HEAD:C_HEAD + HM] = channels(x["norm_m_head"][0])
    par[:, C_CW:C_CW + 32] = x["conv_w"][0].reshape(4, KT, P).transpose(2, 0, 1).reshape(P, 32)
    par[:, C_CB:C_CB + KT] = channels(x["conv_b"][0])
    par[0:HM, C_ZB], par[32:32 + HF, C_ZB], par[64:64 + HM, C_IB] = x["b_m_f"][0], x["b_fox_f"][0], x["b_m_i"][0]

    ins = {
        "units": units,
        "u_units": x["peer_u"][0].reshape(NCH, P, KT, P).transpose(0, 3, 2, 1).reshape(NCH, P, 1024),
        "v_units": x["peer_v"][0].reshape(NCH, P, D),
        "par": par,
        "xT": channels(np.concatenate([x["x_prompt"][0], x["x_sample"][0]]).T),
        "memT": channels(x["mem_prompt"][0].T),
        "conv_state": channels(x["state_conv"][0, 0].T),
        "lf_past": x["cache_fox_lf"][0, 0].T,
        "c0": x["state_mlstm_c"][0, 0].transpose(1, 0, 2),
        "n0": x["state_mlstm_n"][0, 0].T,
        "m0": x["state_mlstm_m"][0],
        "kc": x["cache_mem_k"][0, 0].transpose(2, 1, 0),
        "vc": x["cache_mem_v"][0, 0].reshape(2, P, 512).transpose(1, 0, 2),
        "kpast": channels(x["cache_fox_k"][0, 0].reshape(PAST, 512).T),
        "vpast": x["cache_fox_v"][0, 0].reshape(PAST, 512),
        "keysT": x["peer_keys"][0].reshape(NHC, NKEY, P).transpose(2, 0, 1),
    }
    ins = {k: np.ascontiguousarray(v) for k, v in ins.items()}

    nc = bacc.Bacc("TRN2", target_bir_lowering=False, num_devices=1)
    a = {k: nc.dram_tensor(f"in_{k}", v.shape, mybir.dt.from_np(v.dtype), kind="ExternalInput").ap()
         for k, v in ins.items()}
    o = {k: nc.dram_tensor(f"out_{k}", s, F32, kind="ExternalOutput").ap() for k, s in _OUTS.items()}
    program(nc, a, o)
    r = run(nc, [{f"in_{k}": v for k, v in ins.items()}], core_ids=[0]).results[0]
    r = {k: r[f"out_{k}"] for k in _OUTS}

    def rows(v):
        return v.transpose(2, 1, 0).reshape(v.shape[2], -1)

    y, fk = rows(r["y"]), rows(r["fk"])
    heads = (HF, FD)
    out = (
        y[:TP].reshape(1, TP, D), y[TP:].reshape(1, TS, D),
        fk[:TP].reshape(1, 1, TP, *heads), r["fv_p"].transpose(1, 0, 2).reshape(1, 1, TP, *heads),
        r["lf_p"].T.reshape(1, 1, TP, HF), r["cn_p"][:, :, :P].transpose(1, 0, 2).reshape(1, 1, HM, P, P),
        r["cn_p"][:, :, P].T.reshape(1, 1, HM, P), r["m_p"].reshape(1, 1, HM),
        rows(r["conv_p"]).reshape(1, 1, 3, D),
        r["memk"].transpose(2, 1, 0).reshape(1, 1, NMEM, HC, P),
        r["memv"].transpose(1, 0, 2).reshape(1, 1, NMEM, HC, P),
        fk[TP:].reshape(1, 1, TS, *heads), r["fv_s"].reshape(1, 1, TS, *heads),
        r["lf_s"].T.reshape(1, 1, TS, HF), r["cn_s"][:, :, :P].transpose(1, 0, 2).reshape(1, 1, HM, P, P),
        r["cn_s"][:, :, P].T.reshape(1, 1, HM, P), r["m_s"].reshape(1, 1, HM),
        rows(r["conv_s"]).reshape(1, 1, 3, D),
    )
    return tuple(np.ascontiguousarray(v) for v in out)
```

```python
from contextlib import ExitStack

import concourse.bass as bass
from concourse import mybir

F32 = mybir.dt.float32
BF16 = mybir.dt.bfloat16
U32 = mybir.dt.uint32
ALU = mybir.AluOpType
ACT = mybir.ActivationFunctionType
AX = mybir.AxisListType

P = 128
D = 1024
KT = D // P
TP, TS = 512, 64
T = TP + TS
HALF = T // 2
NTT = 5
NMEM = 256
PAST = 128
HM, HF, HC = 4, 8, 4
FD = 64
NB = 3
EPS = 1e-6
NPH = 8
NKEY = 128
TOPK = 16
NHC = NPH * 2
NCH = 128
GRP = 4
NG = NCH // GRP
SQRT_HM = 128 ** -0.5

N_MEMK, N_MEMV, N_T, N_MV, N_FV, N_SMALL = 4, 4, 24, 4, 4, 1
U_MEMV = N_MEMK
U_T = U_MEMV + N_MEMV
U_MV = U_T + N_T
U_FV = U_MV + N_MV
U_SMALL = U_FV + N_FV
U_MERGE = U_SMALL + N_SMALL
N_JP = 4
N_PER_JP = NB + 2 * NB
U_OUT = U_MERGE + N_JP * N_PER_JP
U_WQ = U_OUT + KT
U_PEER = U_WQ + NHC
U_V = U_PEER + NCH
RAW, RING = 4, 8

MQ, MK, FQ, FK, CQ, MO = 0, 4, 8, 12, 16, 20
C_MIX, C_FFN, C_FIN, C_MEM, C_HEAD, C_CW, C_CB, C_ZB, C_IB = 0, 8, 16, 24, 32, 36, 68, 76, 77
N_PAR = 78

TBLK = 96
NBLK = T // TBLK
GT = 4
BODY = RING
J_G = 6
G_BODY = 2 * BODY
J_END = J_G + T // GT // G_BODY
PIECES = 8
N_TK = 21
N_MD, N_MA = 13, 13


def attention_items():
    items = [("fox", 2 * hp + hh, qi) for hp in range(HF // 2) for qi in range(NTT) for hh in range(2)]
    return items + [("mem", h, qi) for h in range(HC) for qi in range(NTT)]


def out_slot(kind, h):
    return h // 2 if kind == "fox" else 4 + h


def columns(kind, qi):
    if kind == "mem":
        return NMEM
    return (qi + 1) * P if qi < 4 else PAST + TS


def scale_of(kind):
    return FD ** -0.5 if kind == "fox" else 128 ** -0.5


def out_index(i):
    nf = HF * NTT
    return i // 2 if i < nf else nf // 2 + i - nf


def program(nc, a, o):
    ctx = ExitStack()
    with ctx:
        BASE = (nc.sbuf_base + 63) // 64 * 64
        used = [BASE]

        def place(name, offset, shape, dt):
            return nc.alloc_sbuf_tensor_at(name, shape, dt, offset=offset)

        def sb(name, shape, dt):
            size = 2 if dt == BF16 else 4
            n = size
            for x in shape[1:]:
                n *= x
            t = place(name, used[0], shape, dt)
            used[0] += (n + 31) // 32 * 32
            return t

        def sem(name):
            return ctx.enter_context(nc.semaphore(name))

        ps = ctx.enter_context(nc.psum_tensor("ps", [P, 8, 512], F32))

        xT = sb("xT", [P, KT, T], F32)
        act_hi = sb("act_hi", [P, KT, T], BF16)
        act_lo = sb("act_lo", [P, KT, T], BF16)
        raw = sb("raw", [P, RAW, 1024], F32)
        w_hi = sb("w_hi", [P, RING, 1024], BF16)
        w_lo = sb("w_lo", [P, RING, 1024], BF16)
        par = sb("par", [P, N_PAR], F32)
        ones = sb("ones", [P, P], F32)
        ident = sb("ident", [P, P], F32)
        causal = sb("causal", [P, P], F32)
        identb = sb("identb", [P, P], BF16)
        maskneg = sb("maskneg", [P, P], BF16)
        iota = sb("iota", [P, P], F32)
        epsb = sb("epsb", [P, 1], F32)
        oneb = sb("oneb", [P, 1], F32)
        ARENA = used[0]

        proj = place("proj", ARENA, [P, 24, T], F32)
        proj_b = place("proj_b", ARENA, [P, 24, 2, T], BF16)
        mem_x = place("mem_x", ARENA, [P, KT, NMEM], F32)
        mem_sq = place("mem_sq", ARENA + 8192, [P, KT, NMEM], F32)
        mem_h = place("mem_h", ARENA + 16384, [P, KT, NMEM], F32)
        mix_sq = place("mix_sq", ARENA, [P, KT, T], F32)
        mix_h = place("mix_h", ARENA + 24576, [P, KT, T], F32)
        used[0] = ARENA + 24 * T * 4
        V0 = used[0]
        mv = sb("mv", [P, NTT, 512], F32)
        fv = sb("fv", [P, NTT, 512], F32)
        qz = place("qz", V0, [P, 2, 2, T], F32)
        mg_hi = place("mg_hi", V0, [P, KT, T], BF16)
        mg_lo = place("mg_lo", V0 + KT * T * 2, [P, KT, T], BF16)
        mem_hi = place("mem_hi", V0, [P, KT, NMEM], BF16)
        mem_lo = place("mem_lo", V0 + 4096, [P, KT, NMEM], BF16)
        mkT = sb("mkT", [P, HC, NMEM], F32)
        mvN = sb("mvN", [P, 2, 512], F32)
        kc = sb("kc", [P, HC, NMEM], F32)
        vc = sb("vc", [P, 2, 512], F32)
        kpast = sb("kpast", [P, HF // 2, PAST], F32)
        vpast = sb("vpast", [P, 512], F32)
        W0 = used[0]
        wk = sb("wk", [P, 5, T], F32)
        R0 = used[0]
        lsig = sb("lsig", [40, T], F32)
        m_row = sb("m_row", [4, T], F32)
        nM = sb("nM", [4, T], F32)
        cum = sb("cum", [P, 704], F32)
        c_row = sb("c_row", [4, T], F32)
        cS = sb("cS", [P, NTT, HM], F32)
        zrow = place("zrow", W0, [40, T], F32)
        trow = place("trow", W0 + 2304, [40, T], F32)
        st = sb("st", [P, 2, 4], F32)
        sm = sb("sm", [P, 2, TS], F32)
        ws = sb("ws", [P, 8], F32)
        c0 = sb("c0", [P, HM, P], F32)
        n0 = sb("n0", [P, HM], F32)
        m0b = sb("m0b", [P, HM], F32)
        m0 = sb("m0", [4, 1], F32)
        xs = place("xs", W0 + 2 * T * 4, [P, KT, 3 + TS], F32)
        assert used[0] <= nc.sbuf_usable_end, used[0] - nc.sbuf_usable_end

        S = place("S", ARENA, [P, NTT, NHC, NKEY], F32)
        keys = place("keys", ARENA + 40960, [P, NHC, NKEY], F32)
        qr = place("qr", ARENA + 49152, [P, 2, T], F32)
        used[0] = ARENA + 40960
        sA = sb("sA", [P, NHC, NKEY], F32)
        sB = sb("sB", [P, NHC, NKEY], F32)
        candA = sb("candA", [P, NPH, TOPK * TOPK], F32)
        candB = sb("candB", [P, NPH, TOPK * TOPK], F32)
        top = sb("top", [P, NHC, TOPK], F32)
        topi = sb("topi", [P, NHC, TOPK], U32)
        topf = sb("topf", [P, NHC, TOPK], F32)
        best = sb("best", [P, NPH, TOPK], F32)
        bi = sb("bi", [P, NPH, TOPK], U32)
        ab = sb("ab", [P, 2, NPH, TOPK], U32)
        abf = sb("abf", [P, 2, NPH, TOPK], F32)
        trip = sb("trip", [P, 3, NTT, P], F32)
        gs = sb("gs", [P, 2, NTT * NPH], F32)
        w16 = sb("w16", [P, T], BF16)
        eq = sA[:, :, :].rearrange("p a (k c) -> p (a k) c", c=TOPK)
        gsb = place("gsb", ARENA, [P, 2, P, TBLK], F32)
        assert used[0] <= ARENA + 2 * P * TBLK * 4
        used[0] = ARENA + 2 * P * TBLK * 4
        pair = sb("pair", [P, 4, T], F32)
        hot_hi = sb("hot_hi", [P, 2, GT, P], BF16)
        hot_lo = sb("hot_lo", [P, 2, GT, P], BF16)
        hot2 = sb("hot2", [P, 2, GT, P], BF16)
        hb = sb("hb", [P, 2, T], F32)
        tcol = causal[:, 0:2 * 4 * GT].rearrange("p (a c u) -> p a c u", a=2, c=4)
        assert used[0] <= nc.sbuf_usable_end, used[0] - nc.sbuf_usable_end

        used[0] = ARENA
        W_hi = sb("W_hi", [P, 2, GRP, T], BF16)
        W_lo = sb("W_lo", [P, 2, GRP, T], BF16)
        Gb = sb("Gb", [P, 2, NBLK, GRP, TBLK], F32)
        Hb = sb("Hb", [P, 2, GRP, T], F32)
        wb = sb("wb", [P, 2, T], F32)
        fin_sq = sb("fin_sq", [P, KT, T], F32)
        fin_y = sb("fin_y", [P, KT, T], F32)

        gd = nc.dram_tensor("gd", (NBLK, P, NCH, TBLK), F32, kind="Internal").ap()
        hd = nc.dram_tensor("hd", (NCH, P, T), F32, kind="Internal").ap()

        raw_loaded = [sem(f"raw_loaded{i}") for i in range(RAW)]
        hi_ready, lo_ready, unit_used = sem("hi_ready"), sem("lo_ready"), sem("unit_used")
        mem_in, x_in, par_in, small_in, cw_in = sem("mem_in"), sem("x_in"), sem("par_in"), sem("small_in"), sem("cw_in")
        keys_in = sem("keys_in")
        consts, filled = sem("consts"), sem("filled")
        n_sq, n_ssq, n_rms, n_inv = sem("n_sq"), sem("n_ssq"), sem("n_rms"), sem("n_inv")
        n_scaled, n_hi, n_lo = sem("n_scaled"), sem("n_hi"), sem("n_lo")
        t_evac, nat_evac = sem("t_evac"), sem("nat_evac")
        row_dve, row_act, c_turned, cS_ready = sem("row_dve"), sem("row_act"), sem("c_turned"), sem("cS_ready")
        xs_ready, conv_step, conv_y, conv_done = sem("xs_ready"), sem("conv_step"), sem("conv_y"), sem("conv_done")
        early_out, late_out, conv_out = sem("early_out"), sem("late_out"), sem("conv_out")
        m_bc, m_s, m_arg, m_exp, m_mask = sem("m_bc"), sem("m_s"), sem("m_arg"), sem("m_exp"), sem("m_mask")
        m_sw, m_acc, m_act, m_dve, m_ssq = sem("m_sw"), sem("m_acc"), sem("m_act"), sem("m_dve"), sem("m_ssq")
        m_kt, m_st = sem("m_kt"), sem("m_st")
        q_apart, cum_zero = sem("q_apart"), sem("cum_zero")
        a_sc, a_max, a_neg, a_exp = sem("a_sc"), sem("a_max"), sem("a_neg"), sem("a_exp")
        a_rcp, a_norm, a_tr, a_pt = sem("a_rcp"), sem("a_norm"), sem("a_tr"), sem("a_pt")
        a_pv, a_oh, a_ol = sem("a_pv"), sem("a_oh"), sem("a_ol")
        g_ready, g_evac, g_prod, g_acc, g_mhi, g_mlo = (
            sem("g_ready"), sem("g_evac"), sem("g_prod"), sem("g_acc"), sem("g_mhi"), sem("g_mlo"))
        x2_ready = sem("x2_ready")
        q_evac, s_ready, s_evac = sem("q_evac"), sem("s_ready"), sem("s_evac")
        tk, tk_exp, tk_turned, soft, paired = sem("tk"), sem("tk_exp"), sem("tk_turned"), sem("soft"), sem("paired")
        b_col, b_hot, b_prod, b_evac, b_written = (
            sem("b_col"), sem("b_hot"), sem("b_prod"), sem("b_evac"), [sem("b_written0"), sem("b_written1")])
        h_written = [sem("h_written0"), sem("h_written1")]
        gh_in = [sem("gh_in0"), sem("gh_in1")]
        gelu_done, w_mul, w_hi_done, w_lo_done = sem("gelu_done"), sem("w_mul"), sem("w_hi_done"), sem("w_lo_done")
        v_ready, acc_done = sem("v_ready"), sem("acc_done")
        y_out = sem("y_out")

        items = attention_items()
        block = ctx.enter_context(nc.Block())

        @block.sync
        def _(sp):
            def load(src, slot, first, need):
                if not first:
                    sp.wait_ge(lo_ready, need)
                sp.dma_start(raw[:, slot, :], src).then_inc(raw_loaded[slot], 16)

            for n in range(RAW):
                load(a["units"][n], n, True, 0)
            with sp.Fori(1, U_PEER // RAW) as i:
                for k in range(RAW):
                    load(a["units"][i * RAW + k], k, False, i * RAW + k - RAW + 1)
            for n in range(U_PEER // RAW * RAW, U_PEER):
                load(a["units"][n], n % RAW, False, n - RAW + 1)
            with sp.Fori(0, NCH // RAW) as i:
                for k in range(RAW):
                    load(a["u_units"][i * RAW + k], (U_PEER + k) % RAW, False, i * RAW + (U_PEER + k - RAW + 1))
            for k in range(GRP):
                load(a["v_units"][k], (U_V + k) % RAW, False, U_V + k - RAW + 1)

            def load_gh(g, pg, need):
                if need is not None:
                    sp.wait_ge(w_mul, need)
                sp.dma_start(Gb[:, pg, :, :, :].rearrange("e b c t -> e b (c t)"),
                             gd[:, :, bass.ds(g * GRP, GRP), :].rearrange("b e c t -> e b (c t)")).then_inc(gh_in[pg], 16)
                sp.dma_start(Hb[:, pg, :, :], hd[bass.ds(g * GRP, GRP)].rearrange("c e t -> e c t")).then_inc(gh_in[pg], 16)

            def load_group(g, pg):
                load_gh(g, pg, (g - 1) * GRP)
                for k in range(GRP):
                    load(a["v_units"][g * GRP + k], (U_V + k) % RAW, False, g * GRP + (U_V + k - RAW + 1))

            for b in range(2):
                sp.wait_ge(b_written[b], NBLK // 2 * PIECES * 16)
                sp.wait_ge(h_written[b], 8 * (NCH - 2 * GRP))
            load_gh(0, 0, None)
            for k in range(GRP, 2 * GRP):
                load(a["v_units"][k], (U_V + k) % RAW, False, U_V + k - RAW + 1)
            load_gh(1, 1, None)
            with sp.Fori(0, (NG - 4) // 2) as i:
                for b in range(2):
                    load_group(i * 2 + 2 + b, b)
            for b in range(2):
                sp.wait_ge(h_written[b], 8 * NCH)
            for g in range(NG - 2, NG):
                load_group(g, g % 2)

            for k in range(0, KT, 2):
                sp.wait_ge(n_scaled, 3 * KT + k + 2)
                sp.dma_start(o["y"][:, k:k + 2, :], fin_y[:, k:k + 2, :]).then_inc(y_out, 16)
            sp.wait_ge(y_out, KT // 2 * 16)

        @block.gpsimd
        def _(pool):
            pool.memset(ones[:, :], 1.0).then_inc(consts, 1)
            pool.memset(ident[:, :], 0.0).then_inc(filled, 1)
            pool.memset(identb[:, :], 0.0).then_inc(filled, 1)
            pool.memset(causal[:, :], 1.0).then_inc(filled, 1)
            pool.memset(maskneg[:, :], 0.0).then_inc(filled, 1)
            pool.memset(epsb[:, :], EPS).then_inc(consts, 1)
            pool.memset(oneb[:, :], 1.0).then_inc(consts, 1)
            pool.memset(cum[:, :], 0.0).then_inc(cum_zero, 1)
            pool.iota(iota[:, :], [[1, P]], base=0, channel_multiplier=0,
                      allow_small_or_imprecise_dtypes=True).then_inc(consts, 1)
            pool.wait_ge(filled, 4)
            for m in (ident, identb):
                pool.affine_select(out=m[:, :], in_=m[:, :], compare_op=ALU.not_equal, fill=1.0, base=0,
                                   pattern=[[-1, P]], channel_multiplier=1).then_inc(consts, 1)
            pool.affine_select(out=causal[:, :], in_=causal[:, :], compare_op=ALU.is_ge, fill=0.0, base=0,
                               pattern=[[1, P]], channel_multiplier=-1).then_inc(consts, 1)
            pool.affine_select(out=maskneg[:, :], in_=maskneg[:, :], compare_op=ALU.is_ge, fill=-1e30, base=0,
                               pattern=[[-1, P]], channel_multiplier=1).then_inc(consts, 1)

            def low_half(n, k):
                pool.wait_ge(hi_ready, n + 1)
                pool.tensor_tensor(w_lo[:, k % RING, :], raw[:, k % RAW, :], w_hi[:, k % RING, :],
                                   ALU.subtract).then_inc(lo_ready, 1)

            with pool.Fori(0, U_PEER // RING) as i:
                for k in range(RING):
                    low_half(i * RING + k, k)
            for n in range(U_PEER // RING * RING, U_PEER):
                low_half(n, n)
            with pool.Fori(0, 2 * NCH // RING) as i:
                for k in range(RING):
                    low_half(i * RING + U_PEER + k, U_PEER + k)

        @block.scalar
        def _(act):
            act.dma_start(mem_x[:, :, :], a["memT"]).then_inc(mem_in, 16)
            act.dma_start(par[:, :], a["par"]).then_inc(par_in, 16)
            act.dma_start(xT[:, :, :], a["xT"]).then_inc(x_in, 16)
            act.dma_start(xs[:, :, 0:3], a["conv_state"]).then_inc(cw_in, 16)
            act.wait_ge(cum_zero, 1)
            act.dma_start(cum[32:40, TP:TP + PAST], a["lf_past"]).then_inc(small_in, 16)
            act.dma_start(c0[:, :, :], a["c0"]).then_inc(small_in, 16)
            act.dma_start(n0[:, :], a["n0"]).then_inc(small_in, 16)
            act.dma_start(m0[:, :], a["m0"].rearrange("a h -> h a")).then_inc(small_in, 16)
            act.dma_start(m0b[:, :], a["m0"].broadcast_to((P, HM))).then_inc(small_in, 16)
            act.dma_start(kc[:, :, :], a["kc"]).then_inc(small_in, 16)
            act.dma_start(vc[:, :, :], a["vc"]).then_inc(small_in, 16)
            act.dma_start(kpast[:, :, :], a["kpast"]).then_inc(small_in, 16)
            act.dma_start(vpast[:, :], a["vpast"]).then_inc(small_in, 16)

            def square(x, sq, ready=None):
                for k in range(KT):
                    if ready:
                        act.wait_ge(*ready(k))
                    act.activation(sq[:, k, :], x[:, k, :], ACT.Square).then_inc(n_sq, 1)

            def root(i, out, sums):
                act.wait_ge(n_ssq, i + 1)
                act.activation(out, sums, ACT.Sqrt, bias=epsb[:, 0:1], scale=1.0 / D).then_inc(n_rms, 1)

            def high(i, h, hi):
                for k in range(KT):
                    act.wait_ge(n_scaled, KT * i + k + 1)
                    act.activation(hi[:, k, :], h[:, k, :], ACT.Copy).then_inc(n_hi, 1)

            def high_half(n, k, load_count=None):
                act.wait_ge(raw_loaded[k % RAW], load_count)
                act.activation(w_hi[:, k % RING, :], raw[:, k % RAW, :], ACT.Copy).then_inc(hi_ready, 1)

            def high_unit(n):
                if n >= RING:
                    act.wait_ge(unit_used, n - RING + 1)
                high_half(n, n, 16 * (n // RAW + 1))

            act.wait_ge(consts, 8)
            act.wait_ge(mem_in, 16)
            square(mem_x, mem_sq)
            root(0, wk[:, 0, 0:NMEM], ps[:, 4, 0:NMEM])
            act.wait_ge(par_in, 16)
            for n in range(RAW):
                high_unit(n)
            high(0, mem_h, mem_hi)
            act.wait_ge(x_in, 16)
            act.wait_ge(n_lo, KT)
            square(xT, mix_sq)
            root(1, wk[:, 1, :].rearrange("p (a b) -> p a b", a=2), ps[:, 0:2, 0:HALF])
            for n in range(RAW, RING):
                high_unit(n)
            high(1, mix_h, act_hi)

            for n in range(RING, RING + U_T):
                high_unit(n)
            act.activation(mvN[:, :, :], ps[:, 4:6, :], ACT.Copy).then_inc(nat_evac, 1)
            with act.Fori(0, N_T // RING) as i:
                for k in range(RING):
                    act.wait_ge(unit_used, i * RING + U_T + k + 1)
                    high_half(None, U_T + k, i * 32 + 16 * ((U_T + RING + k) // RAW + 1))
            act.wait_ge(t_evac, N_MEMK + N_T)
            act.dma_start(o["conv_p"], proj[:, 0:KT, TP - 3:TP]).then_inc(conv_out, 16)
            act.dma_start(o["conv_s"], proj[:, 0:KT, T - 3:T]).then_inc(conv_out, 16)
            act.dma_start(o["fk"], proj[:, FK:FK + 4, :]).then_inc(early_out, 16)
            act.dma_start(o["memk"], mkT[:, :, :]).then_inc(early_out, 16)
            act.wait_ge(nat_evac, 1)
            act.dma_start(o["memv"], mvN[:, :, :]).then_inc(early_out, 16)
            for first, buf in ((U_MV, mv), (U_FV, fv)):
                for n in range(first, first + 4):
                    high_unit(n + RING)
                if buf is fv:
                    act.wait_ge(conv_out, 2 * 16)
                    for c in range(KT):
                        act.wait_ge(conv_y, c + 1)
                        act.activation(proj[:, c, :], wk[:, 3 + c % 2, :], ACT.Silu).then_inc(conv_done, 1)
                act.activation(buf[:, 0:4, :], ps[:, 4:8, :], ACT.Copy).then_inc(nat_evac, 1)
                act.activation(buf[0:TS, 4, :], ps[0:TS, 2 if buf is mv else 3, :], ACT.Copy).then_inc(nat_evac, 1)
            high_unit(U_SMALL + RING)

            act.wait_ge(nat_evac, 5)
            act.dma_start(o["fv_p"], fv[:, 0:4, :]).then_inc(early_out, 16)
            act.dma_start(o["fv_s"], fv[0:TS, 4, :]).then_inc(early_out, 16)

            act.wait_ge(row_dve, 2)
            act.activation(trow[:, :], zrow[:, :], ACT.Abs).then_inc(row_act, 1)
            act.wait_ge(row_act, 1)
            act.activation(trow[:, :], trow[:, :], ACT.Exp, scale=-1.0).then_inc(row_act, 1)
            act.wait_ge(row_act, 2)
            act.activation(trow[:, :], trow[:, :], ACT.Ln, bias=oneb[0:40, 0:1]).then_inc(row_act, 1)

            act.wait_ge(row_dve, 16)
            act.dma_start(o["lf_p"], lsig[32:40, 0:TP]).then_inc(late_out, 16)
            act.dma_start(o["lf_s"], lsig[32:40, TP:T]).then_inc(late_out, 16)
            act.dma_start(o["m_p"], m_row[:, TP - 1:TP]).then_inc(late_out, 16)
            act.dma_start(o["m_s"], m_row[:, T - 1:T]).then_inc(late_out, 16)

            act.wait_ge(small_in, 9 * 16)
            for h in range(HM):
                for j in range(5):
                    q = 5 * h + j
                    n = TP - P * j if j < 4 else TS
                    rows = P if j < 4 else TS
                    act.wait_ge(m_arg, q + 1)
                    buf = wk[0:rows, j % 2, 0:n]
                    act.activation(buf, buf, ACT.Exp).then_inc(m_exp, 1)
                    if j == 0:
                        act.wait_ge(m_bc, h + 1)
                        act.activation(sm[:, 0, :], ps[:, 3, 0:TS], ACT.Exp, bias=m0b[:, h:h + 1]).then_inc(m_act, 1)
                        act.activation(wk[:, 2, 0:TP], ps[:, 4, :], ACT.Exp, scale=-1.0).then_inc(m_act, 1)
                        act.activation(wk[:, 2, TP:T], ps[:, 3, TS:2 * TS], ACT.Exp, scale=-1.0).then_inc(m_act, 1)
                        act.wait_ge(m_dve, N_MD * h + 1)
                        act.activation(ws[:, 0:4], cS[:, 0:4, h], ACT.Exp, bias=ws[:, 6:7]).then_inc(m_act, 1)
                        act.activation(ws[0:TS, 4:5], cS[0:TS, 4, h:h + 1], ACT.Exp, bias=ws[0:TS, 7:8]).then_inc(m_act, 1)
                        act.activation(ws[:, 5:6], m0b[:, h:h + 1], ACT.Exp, bias=ws[:, 7:8]).then_inc(m_act, 1)
                act.wait_ge(m_acc, 5 * h + 5)
                act.activation(wk[:, 3, 0:TP], ps[:, 6, :], ACT.Abs).then_inc(m_act, 1)
                act.activation(wk[:, 3, TP:T], ps[:, 7, TS:2 * TS], ACT.Abs).then_inc(m_act, 1)
                act.wait_ge(m_dve, N_MD * h + 6)
                act.activation(wk[:, 2, :], wk[:, 4, :], ACT.Square).then_inc(m_act, 1)
                act.wait_ge(m_ssq, h + 1)
                act.activation(wk[:, 2, 0:TP], ps[:, 0, :], ACT.Sqrt, bias=epsb[:, 0:1], scale=1.0 / P).then_inc(m_act, 1)
                act.activation(wk[:, 2, TP:T], ps[:, 1, 0:TS], ACT.Sqrt, bias=epsb[:, 0:1], scale=1.0 / P).then_inc(m_act, 1)
                act.activation(wk[:, 3, :], proj[:, MO + h, :], ACT.Sigmoid).then_inc(m_act, 1)
                act.wait_ge(m_dve, N_MD * h + 9)
                act.activation(proj_b[:, MO + h, 0, :], wk[:, 4, :], ACT.Copy).then_inc(m_act, 1)
            act.wait_ge(m_dve, N_MD * HM)
            act.dma_start(o["cn_p"], proj[:, 0:HM, 0:P + 1]).then_inc(late_out, 16)
            act.dma_start(o["cn_s"], proj[:, 0:HM, 256:256 + P + 1]).then_inc(late_out, 16)
            act.wait_ge(late_out, 6 * 16)
            act.wait_ge(early_out, 5 * 16)

            def copy_turned(i):
                kind, h, qi = items[i]
                nb = (qi + 1 if qi < 4 else 2) if kind == "fox" else 2
                act.wait_ge(a_tr, i + 1)
                if i >= 2:
                    act.wait_ge(a_pv, i - 1)
                dst = wk[:, 2 + i % 2, 0:512]
                if qi < 4:
                    act.activation(dst[:, 0:nb * P], ps[:, 2 + i % 2, 0:nb * P], ACT.Copy).then_inc(a_pt, 1)
                elif kind == "mem":
                    act.activation(dst.rearrange("p (b t) -> p b t", b=4)[:, 0:2, 0:TS],
                                   ps[:, 2 + i % 2, :].rearrange("p (b t) -> p b t", b=4)[:, 0:2, 0:TS],
                                   ACT.Copy).then_inc(a_pt, 1)
                else:
                    act.activation(dst[:, 0:TS], ps[:, 2 + i % 2, 0:TS], ACT.Copy)
                    act.activation(dst[0:TS, P:P + TS], ps[0:TS, 2 + i % 2, P:P + TS], ACT.Copy).then_inc(a_pt, 1)

            def out_high(i):
                kind, h, qi = items[i]
                if kind == "fox" and h % 2 == 0:
                    return
                slot, n = out_slot(kind, h), P if qi < 4 else TS
                act.wait_ge(a_pv, i + 1)
                act.activation(proj_b[:, slot, 0, qi * P:qi * P + n], ps[:, 4 + out_index(i) % 2, 0:n],
                               ACT.Copy).then_inc(a_oh, 1)

            for i in range(len(items)):
                kind, h, qi = items[i]
                n, cols = P if qi < 4 else TS, columns(kind, qi)
                act.wait_ge(a_neg, i + 1)
                if i >= 2:
                    act.wait_ge(a_tr, i - 1)
                act.activation(wk[0:n, i % 2, 0:cols], ps[0:n, i % 2, 0:cols], ACT.Exp,
                               bias=st[0:n, i % 2, 0:1], scale=scale_of(kind),
                               accum_out=st[0:n, i % 2, 1:2]).then_inc(a_exp, 1)
                if i >= 1:
                    copy_turned(i - 1)
                if i >= 2:
                    out_high(i - 2)
            copy_turned(len(items) - 1)
            out_high(len(items) - 2)
            out_high(len(items) - 1)

            for jp in range(N_JP):
                for u in range(N_PER_JP):
                    n = U_MERGE + jp * N_PER_JP + u
                    if u < NB:
                        for j2 in range(2):
                            r = jp * 12 + 2 * u + j2
                            if j2:
                                act.wait_ge(unit_used, n + 1)
                            else:
                                act.wait_ge(g_ready, jp * NB + u + 1)
                            if jp:
                                act.wait_ge(g_prod, 6 * (jp - 1) + 3 * j2 + u + 1)
                            act.activation(proj[:, 8 + 2 * u + j2, :].rearrange("p (a b) -> p a b", a=2),
                                           ps[:, 2 * (r % 2):2 * (r % 2) + 2, 0:HALF], ACT.Copy).then_inc(g_evac, 1)
                    else:
                        r = jp * 12 + 6 + (u - NB)
                        m = jp * 6 + (u - NB)
                        act.wait_ge(unit_used, n + 1)
                        if m >= 2:
                            act.wait_ge(g_prod, m - 1)
                        act.activation(proj[:, 14 + m % 2, :].rearrange("p (a b) -> p a b", a=2),
                                       ps[:, 2 * (r % 2):2 * (r % 2) + 2, 0:HALF], ACT.Sigmoid).then_inc(g_evac, 1)
                    high_unit(n + RING)
                    if u >= NB and (u - NB) % NB == 0 and jp * 2 + (u - NB) // NB > 0:
                        j = jp * 2 + (u - NB) // NB - 1
                        act.wait_ge(g_acc, 2 * (j + 1))
                        act.activation(mg_hi[:, j, :], proj[:, 16 + j % 2, :], ACT.Copy).then_inc(g_mhi, 1)
            act.wait_ge(g_acc, 2 * KT)
            act.activation(mg_hi[:, KT - 1, :], proj[:, 16 + (KT - 1) % 2, :], ACT.Copy).then_inc(g_mhi, 1)
            for n in range(U_OUT, U_WQ):
                high_unit(n + RING)

            square(xT, proj[:, 0:KT, :], lambda k: (x2_ready, k + 1))
            act.dma_start(keys[:, :, :], a["keysT"]).then_inc(keys_in, 16)
            root(2, wk[:, 1, :].rearrange("p (a b) -> p a b", a=2), ps[:, 4:6, 0:HALF])
            high(2, proj[:, 8:8 + KT, :], act_hi)

            for q in range(NHC):
                n = U_WQ + q
                act.wait_ge(unit_used, n + 1)
                if q >= 2:
                    act.wait_ge(s_ready, q - 1)
                act.activation(qr[:, q % 2, :].rearrange("p (a b) -> p a b", a=2),
                               ps[:, 2 * (q % 2):2 * (q % 2) + 2, 0:HALF], ACT.Copy).then_inc(q_evac, 1)
                high_unit(n + RING)

            def chunk(j, k, first=False):
                c = j * BODY + k
                act.wait_ge(unit_used, j * BODY + (U_PEER + k + 1))
                if not (first and k < 2):
                    act.wait_ge(h_written[k % 2], j * (16 * BODY // 2) + 16 * (k // 2))
                act.activation(hb[:, k % 2, :].rearrange("p (a b) -> p a b", a=2),
                               ps[:, 2 * (k % 2):2 * (k % 2) + 2, 0:HALF], ACT.Gelu_apprx_tanh).then_inc(gelu_done, 1)
                high_half(None, U_PEER + k, j * 32 + 16 * ((U_PEER + RING + k) // RAW + 1))
                act.wait_ge(gelu_done, j * BODY + (k + 1))
                act.dma_start(hd[bass.ds(c, 1)].rearrange("c e t -> e (c t)"), hb[:, k % 2, :]).then_inc(h_written[k % 2], 16)

            def write_piece(blk, b, piece, evacuated):
                rows = slice(piece * (NCH // PIECES), (piece + 1) * (NCH // PIECES))
                act.wait_ge(b_evac, evacuated)
                act.dma_start(gd[bass.ds(blk, 1), :, rows, :].rearrange("o e c t -> (o e) (c t)"),
                              gsb[:, b, rows, :].rearrange("e c t -> e (c t)")).then_inc(b_written[b], 16)

            steps = TBLK // GT

            def three_bodies(it, first=False):
                for jj in range(3):
                    for k in range(BODY):
                        chunk(it * 3 + (J_G + jj), k)
                        at_chunk = jj * BODY + k
                        for e in range(2):
                            s = 2 * at_chunk + e
                            b, at = s // steps, (s % steps) * GT
                            act.wait_ge(b_prod, it * (2 * steps) + s + 1)
                            if at == 0 and b == 0 and not first:
                                act.wait_ge(b_written[0], it * (PIECES * 16))
                            if at == 0 and b == 1 and not first:
                                act.wait_ge(b_written[1], it * (PIECES * 16))
                            act.activation(gsb[:, b, :, at:at + GT].rearrange("p k u -> p u k"),
                                           ps[:, 4 + e, :].rearrange("p (u k) -> p u k", u=GT), ACT.Copy).then_inc(b_evac, 1)
                        if at_chunk < PIECES and not first:
                            write_piece(it * 2 - 1, 1, at_chunk, it * (2 * steps))
                        if steps // 2 <= at_chunk < steps // 2 + PIECES:
                            write_piece(it * 2, 0, at_chunk - steps // 2, it * (2 * steps) + steps)

            for k in range(BODY):
                chunk(0, k, first=True)
            with act.Fori(1, J_G) as j:
                for k in range(BODY):
                    chunk(j, k)
            act.wait_ge(tk, NTT * N_TK)
            act.activation(trip[:, 2, :, :], trip[:, 2, :, :], ACT.Exp).then_inc(tk_exp, 1)
            act.wait_ge(paired, 1)
            three_bodies(0, first=True)
            with act.Fori(1, NBLK // 2) as it:
                three_bodies(it)
            for k in range(BODY):
                if k < 4:
                    for piece in range(k * PIECES // 4, (k + 1) * PIECES // 4):
                        write_piece(NBLK - 1, 1, piece, T // GT)
                chunk(J_END, k)

            def second(g, b, more):
                if g is not None:
                    act.wait_ge(unit_used, g * GRP + (U_V - GRP))
                for k in range(GRP):
                    act.wait_ge(w_mul, (0 if g is None else g * GRP) + k + 1)
                    act.activation(W_hi[:, b, k, :], wb[:, k % 2, :], ACT.Copy).then_inc(w_hi_done, 1)
                if more:
                    for k in range(GRP):
                        act.wait_ge(unit_used, g * GRP + (U_V - GRP + k + 1))
                        high_half(None, U_V + (0 if b else GRP) + k, loads(g, k))

            def loads(g, k):
                return g * 16 + 16 * ((U_V + GRP + k) // RAW + 1)

            second(None, 0, False)
            with act.Fori(0, (NG - 2) // 2) as i:
                for b in range(2):
                    second(i * 2 + (1 + b), (1 + b) % 2, True)
            second(NG - 1, (NG - 1) % 2, False)

            square(xT, fin_sq, lambda k: (acc_done, (NG - 1) * KT + k + 1))
            root(3, wb[:, 0, :].rearrange("p (a b) -> p a b", a=2), ps[:, 0:2, 0:HALF])

        @block.vector
        def _(dve):
            def norm(i, x, col, rs, h, hi, lo):
                dve.wait_ge(n_rms, i + 1)
                dve.reciprocal(rs, rs).then_inc(n_inv, 1)
                dve.wait_ge(n_inv, i + 1)
                for k in range(KT + 1):
                    if k < KT:
                        dve.scalar_tensor_tensor(out=h[:, k, :], in0=x[:, k, :], scalar=par[:, col + k:col + k + 1],
                                                 in1=rs, op0=ALU.mult, op1=ALU.mult).then_inc(n_scaled, 1)
                    if k and hi is not None:
                        dve.wait_ge(n_hi, KT * i + k)
                        dve.tensor_tensor(lo[:, k - 1, :], h[:, k - 1, :], hi[:, k - 1, :], ALU.subtract).then_inc(n_lo, 1)

            dve.wait_ge(par_in, 16)
            norm(0, mem_x, C_MEM, wk[:, 0, 0:NMEM], mem_h, mem_hi, mem_lo)
            norm(1, xT, C_MIX, wk[:, 1, :], mix_h, act_hi, act_lo)

            for q in range(N_MEMK):
                dve.wait_ge(unit_used, q + 1)
                dve.tensor_copy(mkT[:, q, :], ps[:, 2 * (q % 2), 0:NMEM]).then_inc(t_evac, 1)
            with dve.Fori(0, N_T // RING) as i:
                for k in range(RING):
                    dve.wait_ge(unit_used, i * RING + U_T + k + 1)
                    dve.tensor_copy(proj[:, bass.ds(i * RING + k, 1), :].rearrange("p o (a b) -> p (o a) b", a=2),
                                    ps[:, 2 * (k % 2):2 * (k % 2) + 2, 0:HALF]).then_inc(t_evac, 1)

            dve.wait_ge(t_evac, N_MEMK + N_T)
            dve.wait_ge(cw_in, 16)
            dve.tensor_copy(xs[:, :, 3:3 + TS], proj[:, 0:KT, TP:T]).then_inc(xs_ready, 1)
            dve.wait_ge(xs_ready, 1)
            step = 0
            for c in range(KT):
                y = wk[:, 3 + c % 2, :]
                w = [par[:, C_CW + 8 * j + c:C_CW + 8 * j + c + 1] for j in range(4)]
                if c >= 2:
                    dve.wait_ge(conv_done, c - 1)
                dve.tensor_scalar(y, proj[:, c, :], w[3], par[:, C_CB + c:C_CB + c + 1], ALU.mult,
                                  ALU.add).then_inc(conv_step, 1)
                step += 1
                for j in range(1, 4):
                    dve.wait_ge(conv_step, step)
                    dve.scalar_tensor_tensor(out=y[:, j:TP], in0=proj[:, c, 0:TP - j], scalar=w[3 - j],
                                             in1=y[:, j:TP], op0=ALU.mult, op1=ALU.add)
                    last = dve.scalar_tensor_tensor(out=y[:, TP:T], in0=xs[:, c, 3 - j:3 - j + TS], scalar=w[3 - j],
                                                    in1=y[:, TP:T], op0=ALU.mult, op1=ALU.add)
                    last.then_inc(conv_step if j < 3 else conv_y, 1)
                    step += j < 3

            rd = [0]

            def row(ins, wait=True):
                rd[0] += 1
                ins.then_inc(row_dve, 1)
                if wait:
                    dve.wait_ge(row_dve, rd[0])

            two = lambda x: x.rearrange("p (a b) -> p a b", a=2)
            dve.wait_ge(unit_used, U_SMALL + 1)
            row(dve.tensor_scalar(two(zrow[:, :]), ps[0:40, 0:2, 0:HALF], par[0:40, C_ZB:C_ZB + 1], None, ALU.add), False)
            row(dve.tensor_scalar(two(c_row[:, :]), ps[64:68, 0:2, 0:HALF], par[64:68, C_IB:C_IB + 1], None, ALU.add), True)
            dve.wait_ge(row_act, 3)
            row(dve.scalar_tensor_tensor(out=lsig[:, :], in0=zrow[:, :], scalar=0.0, in1=trow[:, :],
                                         op0=ALU.min, op1=ALU.subtract))
            for lo_, hi_ in ((0, TP), (TP, T)):
                row(dve.tensor_tensor_scan(m_row[:, lo_:hi_], ones[0:4, 0:1].broadcast_to((4, hi_ - lo_)),
                                           lsig[0:4, lo_:hi_], 0.0, ALU.mult, ALU.add), hi_ == T)
            row(dve.tensor_tensor(c_row[:, :], c_row[:, :], m_row[:, :], ALU.subtract))
            dve.wait_ge(small_in, 9 * 16)
            row(dve.tensor_tensor_scan(nM[:, 0:TP], c_row[:, 0:TP], c_row[:, 0:TP], 0.0, ALU.max, ALU.max), False)
            row(dve.tensor_tensor_scan(nM[:, TP:T], c_row[:, TP:T], c_row[:, TP:T], m0[:, 0:1], ALU.max, ALU.max))
            row(dve.tensor_tensor(m_row[:, :], m_row[:, :], nM[:, :], ALU.add))
            row(dve.tensor_scalar(nM[:, :], nM[:, :], -1.0, None, ALU.mult))
            row(dve.tensor_copy(cum[32:40, TP + PAST:704], lsig[32:40, TP:T]), True)
            row(dve.tensor_tensor_scan(cum[32:40, 0:TP], ones[32:40, 0:1].broadcast_to((8, TP)), lsig[32:40, 0:TP],
                                       0.0, ALU.mult, ALU.add), False)
            row(dve.tensor_tensor_scan(wk[32:40, 2, 0:192], ones[32:40, 0:1].broadcast_to((8, 192)),
                                       cum[32:40, TP:704], 0.0, ALU.mult, ALU.add))
            row(dve.tensor_scalar(cum[32:40, 0:TP], cum[32:40, 0:TP], -(FD ** 0.5), None, ALU.mult), False)
            row(dve.tensor_scalar(cum[32:40, TP:704], wk[32:40, 2, 0:192], -(FD ** 0.5), None, ALU.mult))
            dve.wait_ge(c_turned, 1)
            dve.tensor_copy(cS[:, 0:4, :], ps[:, 2, 0:16].rearrange("p (a b) -> p a b", a=4)).then_inc(cS_ready, 1)
            dve.tensor_copy(cS[0:TS, 4, :], ps[0:TS, 2, 16:20]).then_inc(cS_ready, 1)
            row(dve.memset(st[:, :, :], 0.0))
            dve.wait_ge(cS_ready, 2)

            for h in range(HM):
                md = N_MD * h
                dve.wait_ge(m_bc, h + 1)
                dve.tensor_copy(ws[:, 6:7], ps[:, 2, TP - 1:TP])
                dve.tensor_copy(ws[:, 7:8], ps[:, 3, TS - 1:TS]).then_inc(m_dve, 1)

                def argument(j):
                    q = 5 * h + j
                    n = TP - P * j if j < 4 else TS
                    rows = P if j < 4 else TS
                    src = ps[0:rows, 2, P * j:TP] if j < 4 else ps[0:rows, 3, 0:TS]
                    if q >= 2:
                        dve.wait_ge(m_acc, q - 1)
                    dve.tensor_scalar(wk[0:rows, j % 2, 0:n], src, cS[0:rows, j, h:h + 1], 0.0, ALU.add,
                                      ALU.min).then_inc(m_arg, 1)

                def weigh(j):
                    q = 5 * h + j
                    n = TP - P * j if j < 4 else TS
                    rows = P if j < 4 else TS
                    buf = wk[0:rows, j % 2, :]
                    dve.wait_ge(m_exp, q + 1)
                    dve.tensor_tensor(buf[:, 0:rows], buf[:, 0:rows], causal[0:rows, 0:rows], ALU.mult).then_inc(m_mask, 1)
                    dve.wait_ge(m_mask, q + 1)
                    dve.wait_ge(m_s, q + 1)
                    dve.scalar_tensor_tensor(out=buf[:, 0:n], in0=ps[0:rows, j % 2, 0:n], scalar=SQRT_HM,
                                             in1=buf[:, 0:n], op0=ALU.mult, op1=ALU.mult).then_inc(m_sw, 1)

                argument(0)
                argument(1)
                dve.wait_ge(m_act, N_MA * h + 1)
                dve.tensor_tensor(sm[:, 1, :], sm[:, 0, :], proj[:, MQ + h, TP:T], ALU.mult).then_inc(m_dve, 1)
                for j in range(5):
                    weigh(j)
                    if j + 2 < 5:
                        argument(j + 2)
                dve.wait_ge(m_act, N_MA * h + 8)
                dve.tensor_tensor(wk[:, 3, :], wk[:, 3, :], wk[:, 2, :], ALU.max).then_inc(m_dve, 1)
                dve.wait_ge(m_dve, md + 3)
                dve.reciprocal(wk[:, 3, :], wk[:, 3, :]).then_inc(m_dve, 1)
                dve.wait_ge(m_dve, md + 4)
                dve.tensor_tensor(wk[:, 4, 0:TP], ps[:, 5, :], wk[:, 3, 0:TP], ALU.mult).then_inc(m_dve, 1)
                dve.tensor_tensor(wk[:, 4, TP:T], ps[:, 7, 0:TS], wk[:, 3, TP:T], ALU.mult).then_inc(m_dve, 1)
                dve.wait_ge(m_act, N_MA * h + 11)
                dve.reciprocal(wk[:, 2, :], wk[:, 2, :]).then_inc(m_dve, 1)
                dve.wait_ge(m_dve, md + 7)
                dve.scalar_tensor_tensor(out=wk[:, 4, :], in0=wk[:, 4, :], scalar=par[:, C_HEAD + h:C_HEAD + h + 1],
                                         in1=wk[:, 2, :], op0=ALU.mult, op1=ALU.mult).then_inc(m_dve, 1)
                dve.wait_ge(m_dve, md + 8)
                dve.wait_ge(m_act, N_MA * h + 12)
                dve.tensor_tensor(wk[:, 4, :], wk[:, 4, :], wk[:, 3, :], ALU.mult).then_inc(m_dve, 1)
                dve.wait_ge(m_kt, h + 1)
                for j in range(4):
                    dve.tensor_scalar(wk[:, 0, j * P:(j + 1) * P], ps[:, 4, j * P:(j + 1) * P], ws[:, j:j + 1], SQRT_HM,
                                      ALU.mult, ALU.mult)
                dve.tensor_scalar(wk[0:TS, 1, 0:P], ps[0:TS, 3, 128:256], ws[0:TS, 4:5], SQRT_HM, ALU.mult,
                                  ALU.mult).then_inc(m_dve, 1)
                dve.wait_ge(m_act, N_MA * h + 13)
                dve.wait_ge(m_dve, md + 9)
                dve.tensor_tensor(proj_b[:, MO + h, 1, :], wk[:, 4, :], proj_b[:, MO + h, 0, :],
                                  ALU.subtract).then_inc(m_dve, 1)
                dve.wait_ge(m_st, h + 1)
                dve.tensor_copy(proj[:, MQ + h, 0:P + 1], ps[:, 2, 0:P + 1]).then_inc(m_dve, 1)
                dve.scalar_tensor_tensor(out=proj[:, MQ + h, 256:256 + P], in0=c0[:, h, :], scalar=ws[:, 5:6],
                                         in1=ps[:, 2, 256:256 + P], op0=ALU.mult, op1=ALU.add)
                dve.scalar_tensor_tensor(out=proj[:, MQ + h, 384:385], in0=n0[:, h:h + 1], scalar=ws[:, 5:6],
                                         in1=ps[:, 2, 384:385], op0=ALU.mult, op1=ALU.add).then_inc(m_dve, 1)

            def maxima(i):
                kind, h, qi = items[i]
                n, cols = P if qi < 4 else TS, columns(kind, qi)
                dve.wait_ge(a_sc, i + 1)
                if i >= 2:
                    dve.wait_ge(a_norm, i - 1)
                dve.reduce_max(st[0:n, i % 2, 3:4], ps[0:n, i % 2, 0:cols], AX.X).then_inc(a_max, 1)
                dve.wait_ge(a_max, i + 1)
                dve.tensor_scalar(st[0:n, i % 2, 0:1], st[0:n, i % 2, 3:4], -scale_of(kind), None,
                                  ALU.mult).then_inc(a_neg, 1)

            def out_low(i):
                kind, h, qi = items[i]
                if kind == "fox" and h % 2 == 0:
                    return
                slot, n, x = out_slot(kind, h), P if qi < 4 else TS, out_index(i)
                dve.wait_ge(a_oh, x + 1)
                dve.tensor_tensor(proj_b[:, slot, 1, qi * P:qi * P + n], ps[:, 4 + x % 2, 0:n],
                                  proj_b[:, slot, 0, qi * P:qi * P + n], ALU.subtract).then_inc(a_ol, 1)

            dve.wait_ge(late_out, 6 * 16)
            def queries_apart(hp):
                for hh in range(2):
                    rows = slice(FD * hh, FD * hh + FD)
                    last = dve.tensor_copy(qz[rows, hp % 2, hh, :], proj[rows, FQ + hp, :])
                last.then_inc(q_apart, 1)

            dve.memset(qz[FD:P, :, 0, :], 0.0)
            dve.memset(qz[0:FD, :, 1, :], 0.0)
            queries_apart(0)
            queries_apart(1)
            maxima(0)
            for i in range(len(items)):
                kind, h, qi = items[i]
                n, cols = P if qi < 4 else TS, columns(kind, qi)
                if i + 1 < len(items):
                    maxima(i + 1)
                if kind == "fox" and i % (2 * NTT) == 0 and 1 <= i // (2 * NTT) < HF // 2 - 1:
                    queries_apart(i // (2 * NTT) + 1)
                dve.wait_ge(a_exp, i + 1)
                dve.reciprocal(st[0:n, i % 2, 2:3], st[0:n, i % 2, 1:2]).then_inc(a_rcp, 1)
                dve.wait_ge(a_rcp, i + 1)
                dve.tensor_scalar(wk[0:n, i % 2, 0:cols], wk[0:n, i % 2, 0:cols], st[0:n, i % 2, 2:3], None,
                                  ALU.mult).then_inc(a_norm, 1)
                if i >= 2:
                    out_low(i - 2)
            out_low(len(items) - 2)
            out_low(len(items) - 1)

            def merged_low(j):
                dve.wait_ge(g_mhi, j + 1)
                dve.tensor_tensor(mg_lo[:, j, :], proj[:, 16 + j % 2, :], mg_hi[:, j, :], ALU.subtract).then_inc(g_mlo, 1)

            for j in range(KT):
                jp, j2 = j // 2, j % 2
                acc = proj[:, 16 + j % 2, :]
                for b in range(NB):
                    m = 3 * j + b
                    if b == 0 and j >= 2:
                        dve.wait_ge(g_mlo, j - 1)
                    if b == 2:
                        dve.wait_ge(g_acc, 2 * j + 1)
                    dve.wait_ge(g_evac, jp * 12 + 6 + 3 * j2 + b + 1)
                    dst = acc if b == 0 else proj[:, 17 + b, :]
                    dve.tensor_tensor(dst, proj[:, 14 + m % 2, :], proj[:, 8 + 2 * b + j2, :], ALU.mult).then_inc(g_prod, 1)
                    if b:
                        dve.wait_ge(g_prod, m + 1)
                        dve.tensor_tensor(acc, acc, dst, ALU.add).then_inc(g_acc, 1)
                if j:
                    merged_low(j - 1)
            merged_low(KT - 1)

            for j in range(KT):
                dve.wait_ge(unit_used, U_OUT + j + 1)
                dve.tensor_tensor(two(xT[:, j, :]), ps[:, 2 * (j % 2):2 * (j % 2) + 2, 0:HALF], two(xT[:, j, :]),
                                  ALU.add).then_inc(x2_ready, 1)
            dve.wait_ge(x2_ready, KT)
            norm(2, xT, C_FFN, wk[:, 1, :], proj[:, 8:8 + KT, :], act_hi, act_lo)

            dve.wait_ge(n_lo, 3 * KT)
            dve.memset(S[64:128, 4, :, :], 0.0)
            for q in range(NHC):
                dve.wait_ge(s_ready, q + 1)
                dve.tensor_copy(S[:, 0:4, q, :], ps[:, 4 + 2 * (q % 2), :].rearrange("p (a b) -> p a b", a=4))
                dve.tensor_copy(S[0:TS, 4, q, :], ps[0:TS, 5 + 2 * (q % 2), 0:NKEY]).then_inc(s_evac, 1)
            dve.wait_ge(s_evac, NHC)

            with dve.Fori(0, NTT) as i:
                k = [0]

                def step(ins, wait=True):
                    k[0] += 1
                    ins.then_inc(tk, 1)
                    if wait:
                        dve.wait_ge(tk, i * N_TK + k[0])

                def hold():
                    dve.memset(gs[:, 0, :], 0.0)

                def top16(src, rest, vals, idx, count):
                    hold()
                    for x in range(count):
                        ins = dve.max(vals[:, x, 0:8], src[:, x, :])
                    step(ins)
                    hold()
                    for x in range(count):
                        dve.max_index(idx[:, x, 0:8], vals[:, x, 0:8], src[:, x, :])
                        ins = dve.match_replace(rest[:, x, :], vals[:, x, 0:8], src[:, x, :], -3e38)
                    step(ins)
                    hold()
                    for x in range(count):
                        ins = dve.max(vals[:, x, 8:16], rest[:, x, :])
                    step(ins)
                    hold()
                    for x in range(count):
                        ins = dve.max_index(idx[:, x, 8:16], vals[:, x, 8:16], rest[:, x, :])
                    step(ins)

                step(dve.tensor_copy(sA[:, :, :], S[:, bass.ds(i, 1), :, :].rearrange("p o a b -> p (o a) b")))
                top16(sA, sB, top, topi, NHC)
                step(dve.tensor_copy(topf[:, :, :], topi[:, :, :]))
                for h in range(NPH):
                    ins = dve.tensor_tensor(candA[:, h, :].rearrange("p (a b) -> p a b", a=TOPK),
                                            top[:, 2 * h, :].unsqueeze(2).broadcast_to((P, TOPK, TOPK)),
                                            top[:, 2 * h + 1, :].unsqueeze(1).broadcast_to((P, TOPK, TOPK)), ALU.add)
                step(ins)
                top16(candA, candB, best, bi, NPH)
                step(dve.tensor_scalar(ab[:, 0, :, :], bi[:, :, :], 4, None, ALU.logical_shift_right), False)
                step(dve.tensor_scalar(ab[:, 1, :, :], bi[:, :, :], 15, None, ALU.bitwise_and))
                step(dve.tensor_copy(abf[:, :, :, :], ab[:, :, :, :]))
                for half in range(2):
                    step(dve.tensor_tensor(eq, abf[:, half, :, :].rearrange("p h k -> p (h k)").unsqueeze(2)
                                           .broadcast_to((P, P, TOPK)),
                                           iota[:, 0:TOPK].unsqueeze(1).broadcast_to((P, P, TOPK)), ALU.is_equal))
                    eh = eq.rearrange("p (h k) c -> p h k c", h=NPH)
                    for h in range(NPH):
                        ins = dve.tensor_tensor(eh[:, h, :, :], eh[:, h, :, :],
                                                topf[:, 2 * h + half, :].unsqueeze(1).broadcast_to((P, TOPK, TOPK)),
                                                ALU.mult)
                    step(ins)
                    step(dve.tensor_reduce(trip[:, half, bass.ds(i, 1), :].rearrange("p o k -> p (o k)"), eq, AX.X, ALU.add))
                w3 = trip[:, 2, bass.ds(i, 1), :].rearrange("p o (h k) -> p (o h) k", h=NPH)
                step(dve.tensor_tensor(w3, best[:, :, :], best[:, :, 0:1].broadcast_to((P, NPH, TOPK)), ALU.subtract))
                assert k[0] == N_TK

            w3 = trip[:, 2, :, :].rearrange("p a (h k) -> p (a h) k", h=NPH)
            dve.wait_ge(tk_exp, 1)
            dve.tensor_reduce(gs[:, 0, :], w3, AX.X, ALU.add).then_inc(soft, 1)
            dve.wait_ge(soft, 1)
            dve.reciprocal(gs[:, 1, :], gs[:, 0, :]).then_inc(soft, 1)
            dve.wait_ge(soft, 2)
            dve.tensor_tensor(w3, w3, gs[:, 1, :].unsqueeze(2).broadcast_to((P, NTT * NPH, TOPK)), ALU.mult).then_inc(soft, 1)
            for c in range(2):
                dve.wait_ge(tk_turned, c + 1)
                dve.tensor_copy(pair[:, c, 0:TP], ps[:, 6 - 2 * c, :])
                dve.tensor_copy(pair[:, c, TP:T], ps[:, 7 - 2 * c, 0:TS]).then_inc(soft, 1)
            dve.wait_ge(tk_turned, 3)
            dve.tensor_copy(w16[:, 0:TP], ps[:, 6, :])
            dve.tensor_copy(w16[:, TP:T], ps[:, 7, 0:TS]).then_inc(soft, 1)
            dve.wait_ge(soft, 6)
            dve.tensor_tensor(pair[:, 3, 0:TP], ps[:, 6, :], w16[:, 0:TP], ALU.subtract)
            dve.tensor_tensor(pair[:, 3, TP:T], ps[:, 7, 0:TS], w16[:, TP:T], ALU.subtract)
            dve.tensor_copy(pair[:, 2, :], w16[:, :]).then_inc(paired, 1)
            dve.wait_ge(paired, 1)

            def one_hots(i, first=False):
                for c in range(2):
                    if not first:
                        dve.wait_ge(b_prod, i * 2 + c - 1)
                    dve.tensor_copy(tcol[:, c, :, :], pair[:, :, bass.ds(i * (2 * GT) + c * GT, GT)]).then_inc(b_col, 1)
                    dve.wait_ge(b_col, i * 2 + c + 1)
                    for u in range(GT):
                        dve.tensor_scalar(hot2[:, c, u, :], iota[:, :], tcol[:, c, 1, u:u + 1], None, ALU.is_equal)
                        for x, hot in ((2, hot_hi), (3, hot_lo)):
                            last = dve.tensor_scalar(hot[:, c, u, :], iota[:, :], tcol[:, c, 0, u:u + 1],
                                                     tcol[:, c, x, u:u + 1], ALU.is_equal, ALU.mult)
                    last.then_inc(b_hot, 1)

            one_hots(0, first=True)
            with dve.Fori(1, T // GT // 2) as i:
                one_hots(i)

            def w_low(c, pg, k):
                dve.wait_ge(w_hi_done, c + 1)
                dve.tensor_tensor(W_lo[:, pg, k, :], wb[:, k % 2, :], W_hi[:, pg, k, :], ALU.subtract).then_inc(w_lo_done, 1)

            def peer_w(g, pg, loads):
                dve.wait_ge(gh_in[pg], loads)
                for k in range(GRP):
                    c = g * GRP + k
                    if k >= 2:
                        dve.wait_ge(w_lo_done, c - 1)
                    dve.tensor_tensor(wb[:, k % 2, :].rearrange("p (b t) -> p b t", b=NBLK),
                                      Hb[:, pg, k, :].rearrange("p (b t) -> p b t", b=NBLK),
                                      Gb[:, pg, :, k, :], ALU.mult).then_inc(w_mul, 1)
                    if k:
                        w_low(c - 1, pg, k - 1)
                w_low(g * GRP + GRP - 1, pg, GRP - 1)

            def peer_acc(g):
                for d in range(KT):
                    if d < KT - 1:
                        dve.wait_ge(v_ready, g * (KT - 1) + d + 1)
                    else:
                        dve.wait_ge(unit_used, g * GRP + (U_V + GRP))
                    dve.tensor_tensor(two(xT[:, d, :]), ps[:, 2 * (d % 4):2 * (d % 4) + 2, 0:HALF], two(xT[:, d, :]),
                                      ALU.add).then_inc(acc_done, 1)

            peer_w(0, 0, 32)
            with dve.Fori(0, (NG - 2) // 2) as i:
                for b in range(2):
                    g = i * 2 + (1 + b)
                    dve.wait_ge(w_lo_done, g * GRP)
                    peer_w(g, (1 + b) % 2, i * 32 + (32 if b == 0 else 64))
                    peer_acc(g - 1)
            dve.wait_ge(w_lo_done, (NG - 1) * GRP)
            peer_w(NG - 1, (NG - 1) % 2, 16 * NG)
            peer_acc(NG - 2)
            peer_acc(NG - 1)
            norm(3, xT, C_FIN, wb[:, 0, :], fin_y, None, None)

        @block.tensor
        def _(pe):
            def sums(i, sq, out, n):
                for k in range(KT):
                    pe.wait_ge(n_sq, KT * i + k + 1)
                    for half in range(len(out)):
                        last = pe.matmul(out[half], ones[:, :], sq[:, k, half * n:(half + 1) * n],
                                         start=(k == 0), stop=(k == KT - 1))
                last.then_inc(n_ssq, 1)

            def tile(slot, rhs_hi, rhs_lo, bank, kts=KT, width=P, c0_=0, n=HALF, halves=2, ready=None):
                for k in range(kts):
                    if ready is not None:
                        pe.wait_ge(n_lo, ready + k + 1)
                    col = k * width + c0_
                    for w, x in ((w_hi, rhs_hi), (w_hi, rhs_lo), (w_lo, rhs_hi)):
                        for half in range(halves):
                            last = pe.matmul(ps[:, bank + half, 0:n], w[:, slot, col:col + P],
                                             x(k)[:, half * n:(half + 1) * n],
                                             start=(k == 0 and w is w_hi and x is rhs_hi),
                                             stop=(k == kts - 1 and w is w_lo))
                return last

            def natural(first, u, hi, lo, frames, banks):
                n = first + u
                pe.wait_ge(lo_ready, n + 1)
                for (f0, nf), bank in zip(frames, banks):
                    for k2 in range(2):
                        k = 2 * u + k2
                        for x, w in ((hi, w_hi), (lo, w_hi), (hi, w_lo)):
                            last = pe.matmul(ps[0:nf, bank, :], x[:, k, f0:f0 + nf],
                                             w[:, n % RING, k2 * 512:(k2 + 1) * 512],
                                             start=(k == 0 and x is hi and w is w_hi), stop=(k == KT - 1 and w is w_lo))
                last.then_inc(unit_used, 1)

            a_hi, a_lo = (lambda k: act_hi[:, k, :]), (lambda k: act_lo[:, k, :])

            pe.wait_ge(consts, 8)
            sums(0, mem_sq, [ps[:, 4, 0:NMEM]], NMEM)
            sums(1, mix_sq, [ps[:, 0, 0:HALF], ps[:, 1, 0:HALF]], HALF)

            pe.wait_ge(n_rms, 2)
            for q in range(N_MEMK):
                pe.wait_ge(lo_ready, q + 1)
                if q >= 2:
                    pe.wait_ge(t_evac, q - 1)
                tile(q % RING, lambda k: mem_hi[:, k, :], lambda k: mem_lo[:, k, :], 2 * (q % 2), n=NMEM,
                     halves=1, ready=None if q else 0).then_inc(unit_used, 1)
            for u in range(N_MEMV):
                natural(U_MEMV, u, mem_hi, mem_lo, [(0, P), (P, P)], [4, 5])

            pe.wait_ge(n_lo, 2 * KT)
            with pe.Fori(0, N_T // RING) as i:
                for k in range(RING):
                    pe.wait_ge(lo_ready, i * RING + U_T + k + 1)
                    pe.wait_ge(t_evac, i * RING + N_MEMK + k - 1)
                    tile((U_T + k) % RING, a_hi, a_lo, 2 * (k % 2)).then_inc(unit_used, 1)
            frames = [(t * P, P) for t in range(4)] + [(TP, TS)]
            pe.wait_ge(nat_evac, 1)
            pe.wait_ge(t_evac, N_MEMK + N_T)
            for u in range(N_MV):
                natural(U_MV, u, act_hi, act_lo, frames, [4, 5, 6, 7, 2])
            pe.wait_ge(nat_evac, 3)
            for u in range(N_FV):
                natural(U_FV, u, act_hi, act_lo, frames, [4, 5, 6, 7, 3])
            pe.wait_ge(lo_ready, U_SMALL + 1)
            tile(U_SMALL % RING, a_hi, a_lo, 0).then_inc(unit_used, 1)

            pe.wait_ge(row_dve, 8)
            pe.wait_ge(nat_evac, 5)
            for t in range(NTT):
                n = P if t < 4 else TS
                last = pe.transpose(ps[0:n, 2, 4 * t:4 * t + 4], c_row[:, t * P:t * P + n], ident[0:4, 0:4])
            last.then_inc(c_turned, 1)

            pe.wait_ge(row_dve, 16)
            pe.wait_ge(cS_ready, 2)
            pe.wait_ge(conv_done, KT)
            pe.wait_ge(small_in, 9 * 16)
            for h in range(HM):
                pick = ident[0:4, h:h + 1].broadcast_to((4, P))
                qT, kT = proj[:, MQ + h, :], proj[:, MK + h, :]
                if h:
                    pe.wait_ge(m_dve, N_MD * h)
                pe.matmul(ps[:, 2, :], pick, nM[:, 0:TP], start=True, stop=True)
                pe.matmul(ps[:, 3, 0:TS], pick, nM[:, TP:T], start=True, stop=True)
                pe.matmul(ps[:, 4, :], pick, m_row[:, 0:TP], start=True, stop=True)
                pe.matmul(ps[:, 3, TS:2 * TS], pick, m_row[:, TP:T], start=True, stop=True).then_inc(m_bc, 1)

                def scores(j):
                    q = 5 * h + j
                    if j >= 2:
                        pe.wait_ge(m_sw, q - 1)
                    if j < 4:
                        pe.matmul(ps[:, j % 2, 0:TP - P * j], kT[:, P * j:P * (j + 1)], qT[:, P * j:TP],
                                  start=True, stop=True).then_inc(m_s, 1)
                    else:
                        pe.matmul(ps[0:TS, 0, 0:TS], kT[:, TP:T], qT[:, TP:T], start=True, stop=True).then_inc(m_s, 1)

                scores(0)
                scores(1)
                for j in range(5):
                    pe.wait_ge(m_sw, 5 * h + j + 1)
                    if j < 4:
                        sw = wk[:, j % 2, 0:TP - P * j]
                        pe.matmul(ps[:, 5, P * j:TP], mv[:, j, P * h:P * (h + 1)], sw, start=(j == 0), stop=(j == 3))
                        pe.matmul(ps[:, 6, P * j:TP], ones[:, :], sw, start=(j == 0), stop=(j == 3)).then_inc(m_acc, 1)
                    else:
                        sw = wk[0:TS, 0, 0:TS]
                        pe.wait_ge(m_dve, N_MD * h + 2)
                        pe.matmul(ps[:, 7, 0:TS], mv[0:TS, 4, P * h:P * (h + 1)], sw, start=True, stop=False)
                        pe.matmul(ps[:, 7, 0:TS], c0[:, h, :], sm[:, 1, :], start=False, stop=True)
                        pe.matmul(ps[:, 7, TS:2 * TS], ones[0:TS, :], sw, start=True, stop=False)
                        pe.matmul(ps[:, 7, TS:2 * TS], n0[:, h:h + 1].broadcast_to((P, P)), sm[:, 1, :], start=False,
                                  stop=True).then_inc(m_acc, 1)
                    if j + 2 < 5:
                        scores(j + 2)
                pe.wait_ge(m_act, N_MA * h + 3)
                for j in range(4):
                    pe.transpose(ps[:, 4, P * j:P * (j + 1)], kT[:, P * j:P * (j + 1)], ident[:, :])
                pe.transpose(ps[0:TS, 3, 128:256], kT[:, TP:T], ident[:, :]).then_inc(m_kt, 1)
                pe.wait_ge(m_act, N_MA * h + 9)
                pe.matmul(ps[:, 0, :], ones[:, :], wk[:, 2, 0:TP], start=True, stop=True)
                pe.matmul(ps[:, 1, 0:TS], ones[:, :], wk[:, 2, TP:T], start=True, stop=True).then_inc(m_ssq, 1)
                pe.wait_ge(m_dve, N_MD * h + 10)
                for col, rhs in ((0, lambda j: mv[:, j, P * h:P * (h + 1)]), (P, lambda j: ones[:, 0:1])):
                    for j in range(4):
                        pe.matmul(ps[:, 2, col:col + (P if col == 0 else 1)], wk[:, 0, P * j:P * (j + 1)], rhs(j),
                                  start=(j == 0), stop=(j == 3))
                pe.matmul(ps[:, 2, 256:256 + P], wk[0:TS, 1, 0:P], mv[0:TS, 4, P * h:P * (h + 1)], start=True, stop=True)
                pe.matmul(ps[:, 2, 384:385], wk[0:TS, 1, 0:P], ones[0:TS, 0:1], start=True, stop=True).then_inc(m_st, 1)

            def att_scores(i):
                kind, h, qi = items[i]
                n, cols = P if qi < 4 else TS, columns(kind, qi)
                out = ps[0:n, i % 2, 0:cols]
                if i >= 2:
                    pe.wait_ge(a_exp, i - 1)
                if kind == "mem":
                    keys_ = mkT if qi < 4 else kc
                    pe.matmul(out, proj[:, CQ + h, qi * P:qi * P + n], keys_[:, h, :], start=True, stop=True).then_inc(a_sc, 1)
                    return
                hp = h // 2
                pe.wait_ge(q_apart, hp + 1)
                q = qz[:, hp % 2, h % 2, qi * P:qi * P + n]
                pick = ident[:, 32 + h:33 + h].broadcast_to((P, n))
                c_lo = 0 if qi < 4 else TP
                pe.matmul(out, pick, cum[:, c_lo:c_lo + cols], start=True, stop=False)
                if qi < 4:
                    pe.matmul(out, q, proj[:, FK + hp, 0:cols], start=False, stop=False)
                else:
                    pe.matmul(out[:, 0:PAST], q, kpast[:, hp, :], start=False, stop=False)
                    pe.matmul(out[:, PAST:cols], q, proj[:, FK + hp, TP:T], start=False, stop=False)
                pe.matmul(out[:, cols - n:cols], identb[0:n, 0:n], maskneg[0:n, 0:n], start=False,
                          stop=True).then_inc(a_sc, 1)

            def att_values(i):
                kind, h, qi = items[i]
                n, cols = P if qi < 4 else TS, columns(kind, qi)
                blocks = [(b * P, min(P, cols - b * P)) for b in range((cols + P - 1) // P)]
                pe.wait_ge(a_norm, i + 1)
                if i >= 2:
                    pe.wait_ge(a_pt, i - 1)
                for b, (s0, ns) in enumerate(blocks):
                    last = pe.transpose(ps[0:ns, 2 + i % 2, b * P:b * P + n], wk[0:n, i % 2, s0:s0 + ns], ident[0:n, 0:n])
                last.then_inc(a_tr, 1)

            def att_out(i):
                kind, h, qi = items[i]
                n, cols = P if qi < 4 else TS, columns(kind, qi)
                blocks = [(b * P, min(P, cols - b * P)) for b in range((cols + P - 1) // P)]
                x = out_index(i)
                pe.wait_ge(a_pt, i + 1)
                if x >= 2:
                    pe.wait_ge(a_ol, x - 1)
                r0 = FD * (h % 2) if kind == "fox" else 0
                rows = FD if kind == "fox" else P
                for b, (s0, ns) in enumerate(blocks):
                    if kind == "mem":
                        v = (mvN if qi < 4 else vc)[:, b, P * h:P * (h + 1)]
                    elif qi < 4:
                        v = fv[:, b, FD * h:FD * (h + 1)]
                    else:
                        v = vpast[:, FD * h:FD * (h + 1)] if b == 0 else fv[0:TS, 4, FD * h:FD * (h + 1)]
                    last = pe.matmul(ps[r0:r0 + rows, 4 + x % 2, 0:n], v, wk[0:ns, 2 + i % 2, b * P:b * P + n],
                                     start=(b == 0), stop=(b == len(blocks) - 1))
                last.then_inc(a_pv, 1)

            pe.wait_ge(m_dve, N_MD * HM)
            pe.wait_ge(m_act, N_MA * HM)
            att_scores(0)
            for i in range(len(items)):
                if i + 1 < len(items):
                    att_scores(i + 1)
                att_values(i)
                if i >= 1:
                    att_out(i - 1)
            att_out(len(items) - 1)

            branch_slot = [MO, 0, 4]
            pe.wait_ge(a_ol, HF * NTT // 2 + HC * NTT)
            for jp in range(N_JP):
                for u in range(N_PER_JP):
                    n = U_MERGE + jp * N_PER_JP + u
                    pe.wait_ge(lo_ready, n + 1)
                    if u < NB:
                        s0 = branch_slot[u]
                        for j2 in range(2):
                            r = jp * 12 + 2 * u + j2
                            if r >= 2:
                                pe.wait_ge(g_evac, r - 1)
                            last = tile(n % RING, lambda k: proj_b[:, s0 + k, 0, :], lambda k: proj_b[:, s0 + k, 1, :],
                                        2 * (r % 2), kts=4, width=2 * P, c0_=j2 * P)
                            last.then_inc(unit_used if j2 else g_ready, 1)
                    else:
                        r = jp * 12 + 6 + (u - NB)
                        pe.wait_ge(g_evac, r - 1)
                        tile(n % RING, a_hi, a_lo, 2 * (r % 2)).then_inc(unit_used, 1)

            pe.wait_ge(g_mlo, KT)
            pe.wait_ge(g_evac, 12 * N_JP)
            for j in range(KT):
                n = U_OUT + j
                pe.wait_ge(lo_ready, n + 1)
                if j >= 2:
                    pe.wait_ge(x2_ready, j - 1)
                tile(n % RING, lambda k: mg_hi[:, k, :], lambda k: mg_lo[:, k, :], 2 * (j % 2)).then_inc(unit_used, 1)

            sums(2, proj[:, 0:KT, :], [ps[:, 4, 0:HALF], ps[:, 5, 0:HALF]], HALF)

            def key_scores(q):
                pe.wait_ge(q_evac, q + 1)
                if q >= 2:
                    pe.wait_ge(s_evac, q - 1)
                for t in range(NTT):
                    n = P if t < 4 else TS
                    bank, col = (4 + 2 * (q % 2), t * P) if t < 4 else (5 + 2 * (q % 2), 0)
                    last = pe.matmul(ps[0:n, bank, col:col + NKEY], qr[:, q % 2, t * P:t * P + n], keys[:, q, :],
                                     start=True, stop=True)
                last.then_inc(s_ready, 1)

            pe.wait_ge(n_rms, 3)
            pe.wait_ge(keys_in, 16)
            for q in range(NHC):
                n = U_WQ + q
                pe.wait_ge(lo_ready, n + 1)
                if q >= 2:
                    pe.wait_ge(q_evac, q - 1)
                tile(n % RING, a_hi, a_lo, 2 * (q % 2), ready=None if q else 2 * KT).then_inc(unit_used, 1)
                if q:
                    key_scores(q - 1)
            key_scores(NHC - 1)

            pe.wait_ge(q_evac, NHC)

            def chunk(j, k, first=False):
                pe.wait_ge(lo_ready, j * BODY + (U_PEER + k + 1))
                if not (first and k < 2):
                    pe.wait_ge(gelu_done, j * BODY + (k - 1))
                tile((U_PEER + k) % RING, a_hi, a_lo, 2 * (k % 2)).then_inc(unit_used, 1)

            def g_step(j, k, e, first=False):
                s = j * G_BODY + (2 * k + e - J_G * G_BODY)
                pe.wait_ge(b_hot, s + 1)
                if not (first and k == 0):
                    pe.wait_ge(b_evac, s - 1)
                for u in range(GT):
                    pe.matmul(ps[:, 4 + e, u * P:(u + 1) * P], hot2[:, e, u, :], hot_hi[:, e, u, :], start=True, stop=False)
                    last = pe.matmul(ps[:, 4 + e, u * P:(u + 1) * P], hot2[:, e, u, :], hot_lo[:, e, u, :],
                                     start=False, stop=True)
                last.then_inc(b_prod, 1)

            for k in range(BODY):
                chunk(0, k, first=True)
            with pe.Fori(1, J_G) as j:
                for k in range(BODY):
                    chunk(j, k)
            pe.wait_ge(soft, 3)
            pe.wait_ge(s_evac, NHC)
            for c in range(3):
                if c == 2:
                    pe.wait_ge(soft, 4)
                bank = 4 if c == 1 else 6
                for t in range(NTT):
                    last = pe.transpose(ps[:, bank + t // 4, (t % 4) * P:(t % 4 + 1) * P], trip[:, c, t, :], ident[:, :])
                last.then_inc(tk_turned, 1)
            pe.wait_ge(paired, 1)
            for k in range(BODY):
                chunk(J_G, k)
                for e in range(2):
                    g_step(J_G, k, e, first=True)
            with pe.Fori(J_G + 1, J_END) as j:
                for k in range(BODY):
                    chunk(j, k)
                    for e in range(2):
                        g_step(j, k, e)
            with pe.Fori(J_END, NCH // BODY) as j:
                for k in range(BODY):
                    chunk(j, k)
            pe.wait_ge(b_evac, T // GT)
            pe.wait_ge(gelu_done, NCH)

            def peer_v(g, b, first=False):
                pe.wait_ge(lo_ready, g * GRP + (U_V + GRP))
                pe.wait_ge(w_lo_done, g * GRP + GRP)
                for d in range(KT):
                    if not (first and d < 4):
                        pe.wait_ge(acc_done, g * KT + d - 3)
                    bank = 2 * (d % 4)
                    for k in range(GRP):
                        slot = (U_V + b * GRP + k) % RING
                        for w, x in ((w_hi, W_hi), (w_hi, W_lo), (w_lo, W_hi)):
                            for half in range(2):
                                last = pe.matmul(ps[:, bank + half, 0:HALF], w[:, slot, d * P:(d + 1) * P],
                                                 x[:, b, k, half * HALF:(half + 1) * HALF],
                                                 start=(k == 0 and w is w_hi and x is W_hi),
                                                 stop=(k == GRP - 1 and w is w_lo))
                        if d == KT - 1:
                            last.then_inc(unit_used, 1)
                    if d < KT - 1:
                        last.then_inc(v_ready, 1)

            peer_v(0, 0, first=True)
            with pe.Fori(0, (NG - 2) // 2) as i:
                for b in range(2):
                    peer_v(i * 2 + (1 + b), (1 + b) % 2)
            peer_v(NG - 1, (NG - 1) % 2)

            pe.wait_ge(acc_done, NG * KT - 3)
            sums(3, fin_sq, [ps[:, 0, 0:HALF], ps[:, 1, 0:HALF]], HALF)


_OUTS = {
    "y": (P, KT, T), "fk": (P, 4, T), "fv_p": (P, 4, 512), "fv_s": (TS, 512), "lf_p": (8, TP), "lf_s": (8, TS),
    "cn_p": (P, HM, P + 1), "m_p": (HM, 1), "conv_p": (P, KT, 3), "memk": (P, HC, NMEM),
    "memv": (P, 2, 512), "cn_s": (P, HM, P + 1), "m_s": (HM, 1), "conv_s": (P, KT, 3),
}


def kernel(**x):
    import numpy as np
    import concourse.bacc as bacc
    from concourse.bass_utils import run_bass_kernel_spmd as run

    x = {k: np.asarray(v) for k, v in x.items()}
    f32 = np.float32
    assert x["x_prompt"].shape == (1, TP, D) and x["x_sample"].shape == (1, TS, D)

    def channels(v):
        return v.reshape((-1, P) + v.shape[1:]).swapaxes(0, 1)

    def tiles(w, width=P):
        k, c = w.shape
        return w.reshape(k // P, P, c // width, width).transpose(2, 1, 0, 3).reshape(c // width, P, -1)

    def pairs(w):
        return w.reshape(4, 2, P, 512).transpose(0, 2, 1, 3).reshape(4, P, 1024)

    w_in = x["w_in"][0]
    bounds = np.cumsum([0, 512, 512, 512, 512, HM, HM, 512, 512, 512, HF, 512, NB * D])
    mq, mk, mv, mo, mi, mf, fq, fk, fv, ff, cq, gates = [w_in[:, s:e] for s, e in zip(bounds[:-1], bounds[1:])]
    small = np.zeros((D, P), f32)
    small[:, 0:HM], small[:, 32:32 + HF], small[:, 64:64 + HM] = mf, ff, mi
    memkv = x["w_mem_kv"][0]
    gate_units = tiles(gates)
    up_units = [tiles(x[n][0], 2 * P) for n in ("w_up_m", "w_up_f", "w_up_c")]
    merge = []
    for jp in range(N_JP):
        merge += [up_units[b][jp] for b in range(NB)]
        merge += [gate_units[b * KT + 2 * jp + j2] for j2 in range(2) for b in range(NB)]
    units = np.concatenate([
        tiles(memkv[:, :512]), pairs(memkv[:, 512:]),
        tiles(np.concatenate([mq, mk, fq, fk, cq, mo], axis=1)), pairs(mv), pairs(fv), tiles(small),
        np.stack(merge), tiles(x["w_out"][0]), tiles(x["peer_wq"][0]),
    ])
    assert units.shape == (U_PEER, P, 1024)

    par = np.zeros((P, N_PAR), f32)
    for col, name in ((C_MIX, "norm_mix"), (C_FFN, "norm_ffn"), (C_FIN, "norm_final"), (C_MEM, "norm_mem")):
        par[:, col:col + KT] = channels(x[name].reshape(-1))
    par[:, C_HEAD:C_HEAD + HM] = channels(x["norm_m_head"][0])
    par[:, C_CW:C_CW + 32] = x["conv_w"][0].reshape(4, KT, P).transpose(2, 0, 1).reshape(P, 32)
    par[:, C_CB:C_CB + KT] = channels(x["conv_b"][0])
    par[0:HM, C_ZB], par[32:32 + HF, C_ZB], par[64:64 + HM, C_IB] = x["b_m_f"][0], x["b_fox_f"][0], x["b_m_i"][0]

    ins = {
        "units": units,
        "u_units": x["peer_u"][0].reshape(NCH, P, KT, P).transpose(0, 3, 2, 1).reshape(NCH, P, 1024),
        "v_units": x["peer_v"][0].reshape(NCH, P, D),
        "par": par,
        "xT": channels(np.concatenate([x["x_prompt"][0], x["x_sample"][0]]).T),
        "memT": channels(x["mem_prompt"][0].T),
        "conv_state": channels(x["state_conv"][0, 0].T),
        "lf_past": x["cache_fox_lf"][0, 0].T,
        "c0": x["state_mlstm_c"][0, 0].transpose(1, 0, 2),
        "n0": x["state_mlstm_n"][0, 0].T,
        "m0": x["state_mlstm_m"][0],
        "kc": x["cache_mem_k"][0, 0].transpose(2, 1, 0),
        "vc": x["cache_mem_v"][0, 0].reshape(2, P, 512).transpose(1, 0, 2),
        "kpast": channels(x["cache_fox_k"][0, 0].reshape(PAST, 512).T),
        "vpast": x["cache_fox_v"][0, 0].reshape(PAST, 512),
        "keysT": x["peer_keys"][0].reshape(NHC, NKEY, P).transpose(2, 0, 1),
    }
    ins = {k: np.ascontiguousarray(v) for k, v in ins.items()}

    nc = bacc.Bacc("TRN2", target_bir_lowering=False, num_devices=1)
    a = {k: nc.dram_tensor(f"in_{k}", v.shape, mybir.dt.from_np(v.dtype), kind="ExternalInput").ap()
         for k, v in ins.items()}
    o = {k: nc.dram_tensor(f"out_{k}", s, F32, kind="ExternalOutput").ap() for k, s in _OUTS.items()}
    program(nc, a, o)
    r = run(nc, [{f"in_{k}": v for k, v in ins.items()}], core_ids=[0]).results[0]
    r = {k: r[f"out_{k}"] for k in _OUTS}

    def rows(v):
        return v.transpose(2, 1, 0).reshape(v.shape[2], -1)

    y, fk = rows(r["y"]), rows(r["fk"])
    heads = (HF, FD)
    out = (
        y[:TP].reshape(1, TP, D), y[TP:].reshape(1, TS, D),
        fk[:TP].reshape(1, 1, TP, *heads), r["fv_p"].transpose(1, 0, 2).reshape(1, 1, TP, *heads),
        r["lf_p"].T.reshape(1, 1, TP, HF), r["cn_p"][:, :, :P].transpose(1, 0, 2).reshape(1, 1, HM, P, P),
        r["cn_p"][:, :, P].T.reshape(1, 1, HM, P), r["m_p"].reshape(1, 1, HM),
        rows(r["conv_p"]).reshape(1, 1, 3, D),
        r["memk"].transpose(2, 1, 0).reshape(1, 1, NMEM, HC, P),
        r["memv"].transpose(1, 0, 2).reshape(1, 1, NMEM, HC, P),
        fk[TP:].reshape(1, 1, TS, *heads), r["fv_s"].reshape(1, 1, TS, *heads),
        r["lf_s"].T.reshape(1, 1, TS, HF), r["cn_s"][:, :, :P].transpose(1, 0, 2).reshape(1, 1, HM, P, P),
        r["cn_s"][:, :, P].T.reshape(1, 1, HM, P), r["m_s"].reshape(1, 1, HM),
        rows(r["conv_s"]).reshape(1, 1, 3, D),
    )
    return tuple(np.ascontiguousarray(v) for v in out)
```

```python
from contextlib import ExitStack

import concourse.bass as bass
from concourse import mybir

F32 = mybir.dt.float32
BF16 = mybir.dt.bfloat16
U32 = mybir.dt.uint32
ALU = mybir.AluOpType
ACT = mybir.ActivationFunctionType
AX = mybir.AxisListType

P = 128
D = 1024
KT = D // P
TP, TS = 512, 64
T = TP + TS
HALF = T // 2
NTT = 5
NMEM = 256
PAST = 128
HM, HF, HC = 4, 8, 4
FD = 64
NB = 3
EPS = 1e-6
NPH = 8
NKEY = 128
TOPK = 16
NHC = NPH * 2
NCH = 128
GRP = 4
NG = NCH // GRP
SQRT_HM = 128 ** -0.5

N_T, N_SMALL, N_MEMK, N_MEMV, N_MV, N_FV = 8, 1, 4, 4, 4, 4
U_T = 0
U_SMALL = U_T + N_T
U_MEMK = U_SMALL + N_SMALL
U_MEMV = U_MEMK + N_MEMK
U_MV = U_MEMV + N_MEMV
U_FV = U_MV + N_MV
U_FILL = U_FV + N_FV
N_JP = 4
N_PROJ, N_GATE = 16, N_JP * 2 * NB
U_MERGE = U_FILL + N_PROJ + N_GATE
U_OUT = U_MERGE + N_JP * NB
U_WQ = U_OUT + KT
U_PEER = U_WQ + NHC
U_V = U_PEER + NCH
RAW, RING = 4, 8

MQ, MK, FQ, FK, CQ, MO = 0, 4, 8, 12, 16, 20
FILL_SLOTS = [MO + k for k in range(4)] + [FQ + k for k in range(12)]
PRE_TILES = 4
PIECE = 8
H_PIECES = (N_PROJ - PRE_TILES) * 6 // HM
LEAD = 6
GATE_SLOTS = 8
C_MIX, C_FFN, C_FIN, C_MEM, C_HEAD, C_CW, C_CB, C_ZB, C_IB = 0, 8, 16, 24, 32, 36, 68, 76, 77
N_PAR = 78

TBLK = 96
NBLK = T // TBLK
GT = 4
BODY = RING
J_G = 6
G_BODY = 2 * BODY
J_END = J_G + T // GT // G_BODY
PIECES = 8
N_TK = 21
N_SPLIT = 10
N_NB = 5
N_MD, N_MA = 9, 8


def attention_items():
    items = [("fox", 2 * hp + hh, qi) for hp in range(HF // 2) for qi in range(NTT) for hh in range(2)]
    return items + [("mem", h, qi) for h in range(HC) for qi in range(NTT)]


def out_slot(kind, h):
    return h // 2 if kind == "fox" else 4 + h


def columns(kind, qi):
    if kind == "mem":
        return NMEM
    return (qi + 1) * P if qi < 4 else PAST + TS


def scale_of(kind):
    return FD ** -0.5 if kind == "fox" else 128 ** -0.5


def out_index(i):
    nf = HF * NTT
    return i // 2 if i < nf else nf // 2 + i - nf


def norms_before(t):
    if t < PRE_TILES:
        return 0
    if t >= N_PROJ:
        return HM
    h, first = (t - PRE_TILES) // 3, (t - PRE_TILES) % 3 == 0
    return max(h - 1, 0) if first else h


def fill_index(x):
    return x + 2 * norms_before(x // 2)


def norm_index(h):
    return 2 * (PRE_TILES + 3 * (h + 1) + 1 + h) if h < HM - 1 else 2 * (N_PROJ + HM - 1)


def gate_pieces(i):
    n, first, total = (HF + HC) * NTT, 6 * N_PROJ + LEAD, 6 * N_GATE - LEAD
    return range(first + total * i // n, first + total * (i + 1) // n)


def gate_halves(i):
    return [p // 3 for p in gate_pieces(i) if p % 3 == 2]


def acc_slot(j):
    return CQ + j % 4


def merged_count(j):
    return 4 * (j // 2) + 3 + j % 2


def program(nc, a, o):
    ctx = ExitStack()
    with ctx:
        BASE = (nc.sbuf_base + 63) // 64 * 64
        used = [BASE]

        def place(name, offset, shape, dt):
            return nc.alloc_sbuf_tensor_at(name, shape, dt, offset=offset)

        def sb(name, shape, dt):
            size = 2 if dt == BF16 else 4
            n = size
            for x in shape[1:]:
                n *= x
            t = place(name, used[0], shape, dt)
            used[0] += (n + 31) // 32 * 32
            return t

        def sem(name):
            return ctx.enter_context(nc.semaphore(name))

        ps = ctx.enter_context(nc.psum_tensor("ps", [P, 8, 512], F32))

        xT = sb("xT", [P, KT, T], F32)
        act_hi = sb("act_hi", [P, KT, T], BF16)
        act_lo = sb("act_lo", [P, KT, T], BF16)
        raw = sb("raw", [P, RAW, 1024], F32)
        w_hi = sb("w_hi", [P, RING, 1024], BF16)
        w_lo = sb("w_lo", [P, RING, 1024], BF16)
        par = sb("par", [P, N_PAR], F32)
        ones = sb("ones", [P, P], F32)
        ident = sb("ident", [P, P], F32)
        causal = sb("causal", [P, P], F32)
        identb = sb("identb", [P, P], BF16)
        maskneg = sb("maskneg", [P, P], BF16)
        iota = sb("iota", [P, P], F32)
        epsb = sb("epsb", [P, 1], F32)
        oneb = sb("oneb", [P, 1], F32)
        warm = sb("warm", [P, 4], F32)
        ARENA = used[0]

        proj = place("proj", ARENA, [P, 24, T], F32)
        proj_b = place("proj_b", ARENA, [P, 24, 2, T], BF16)
        mix_sq = place("mix_sq", ARENA, [P, KT, T], F32)
        mem_x = place("mem_x", ARENA + 8 * T * 4, [P, KT, NMEM], F32)
        mem_sq = place("mem_sq", ARENA + 8 * T * 4 + 8192, [P, KT, NMEM], F32)
        mem_h = place("mem_h", ARENA + 8 * T * 4 + 8192, [P, KT, NMEM], F32)
        mix_h = place("mix_h", ARENA + 8 * T * 4 + 16384, [P, KT, T], F32)
        used[0] = ARENA + 24 * T * 4
        V0 = used[0]
        mv = sb("mv", [P, NTT, 512], F32)
        fv = sb("fv", [P, NTT, 512], F32)
        qz = place("qz", V0, [P, 2, 2, T], F32)
        mg_hi = place("mg_hi", V0, [P, KT, T], BF16)
        mg_lo = place("mg_lo", V0 + KT * T * 2, [P, KT, T], BF16)
        mem_hi = place("mem_hi", V0, [P, KT, NMEM], BF16)
        mem_lo = place("mem_lo", V0 + 4096, [P, KT, NMEM], BF16)
        mkT = sb("mkT", [P, HC, NMEM], F32)
        mvN = sb("mvN", [P, 2, 512], F32)
        kc = sb("kc", [P, HC, NMEM], F32)
        vc = sb("vc", [P, 2, 512], F32)
        kpast = sb("kpast", [P, HF // 2, PAST], F32)
        vpast = sb("vpast", [P, 512], F32)
        W0 = used[0]
        wk = sb("wk", [P, 5, T], F32)
        R0 = used[0]
        lsig = sb("lsig", [40, T], F32)
        m_row = sb("m_row", [4, T], F32)
        nM = sb("nM", [4, T], F32)
        cum = sb("cum", [P, 704], F32)
        c_row = sb("c_row", [4, T], F32)
        cum3 = place("cum3", used[0] - T * 4, [P, 704], BF16)
        pick3 = sb("pick3", [P, HF], BF16)
        cS = sb("cS", [P, NTT, HM], F32)
        stage = place("stage", R0, [P, 2, T], F32)
        zrow = place("zrow", W0, [40, T], F32)
        trow = place("trow", W0 + 2304, [40, T], F32)
        st = sb("st", [P, 2, 4], F32)
        sm = sb("sm", [P, 2, TS], F32)
        ws = sb("ws", [P, 8], F32)
        c0 = sb("c0", [P, HM, P], F32)
        n0 = sb("n0", [P, HM], F32)
        m0b = sb("m0b", [P, HM], F32)
        m0 = sb("m0", [4, 1], F32)
        xs = place("xs", W0 + 2 * T * 4, [P, KT, 3 + TS], F32)
        assert used[0] <= nc.sbuf_usable_end, used[0] - nc.sbuf_usable_end

        S = place("S", ARENA, [P, NTT, NHC, NKEY], F32)
        keys = place("keys", ARENA + 40960, [P, NHC, NKEY], F32)
        qr = place("qr", ARENA + 49152, [P, 2, T], F32)
        used[0] = ARENA + 40960
        sA = sb("sA", [P, NHC, NKEY], F32)
        sB = sb("sB", [P, NHC, NKEY], F32)
        candA = sb("candA", [P, NPH, TOPK * TOPK], F32)
        candB = sb("candB", [P, NPH, TOPK * TOPK], F32)
        top = sb("top", [P, NHC, TOPK], F32)
        topi = sb("topi", [P, NHC, TOPK], U32)
        topf = sb("topf", [P, NHC, TOPK], F32)
        best = sb("best", [P, NPH, TOPK], F32)
        bi = sb("bi", [P, NPH, TOPK], U32)
        ab = sb("ab", [P, 2, NPH, TOPK], U32)
        abf = sb("abf", [P, 2, NPH, TOPK], F32)
        trip = sb("trip", [P, 3, NTT, P], F32)
        gs = sb("gs", [P, 2, NTT * NPH], F32)
        w16 = sb("w16", [P, T], BF16)
        eq = sA[:, :, :].rearrange("p a (k c) -> p (a k) c", c=TOPK)
        gsb = place("gsb", ARENA, [P, 2, P, TBLK], F32)
        assert used[0] <= ARENA + 2 * P * TBLK * 4
        used[0] = ARENA + 2 * P * TBLK * 4
        pair = sb("pair", [P, 4, T], F32)
        hot_hi = sb("hot_hi", [P, 2, GT, P], BF16)
        hot_lo = sb("hot_lo", [P, 2, GT, P], BF16)
        hot2 = sb("hot2", [P, 2, GT, P], BF16)
        hb = sb("hb", [P, 2, T], F32)
        tcol = causal[:, 0:2 * 4 * GT].rearrange("p (a c u) -> p a c u", a=2, c=4)
        assert used[0] <= nc.sbuf_usable_end, used[0] - nc.sbuf_usable_end

        used[0] = ARENA
        W_hi = sb("W_hi", [P, 2, GRP, T], BF16)
        W_lo = sb("W_lo", [P, 2, GRP, T], BF16)
        Gb = sb("Gb", [P, 2, NBLK, GRP, TBLK], F32)
        Hb = sb("Hb", [P, 2, GRP, T], F32)
        assert used[0] - GRP * T * 4 <= ARENA + P * TBLK * 4
        wb = place("wb", ARENA + 2 * P * TBLK * 4, [P, 2, T], F32)
        fin_sq = sb("fin_sq", [P, KT, T], F32)
        fin_y = sb("fin_y", [P, KT, T], F32)

        gd = nc.dram_tensor("gd", (NBLK, P, NCH, TBLK), F32, kind="Internal").ap()
        hd = nc.dram_tensor("hd", (NCH, P, T), F32, kind="Internal").ap()

        gz = nc.dram_tensor("gz", (N_GATE, P, T), F32, kind="Internal").ap()

        raw_loaded = [sem(f"raw_loaded{i}") for i in range(RAW)]
        hi_ready, lo_ready, unit_used = sem("hi_ready"), sem("lo_ready"), sem("unit_used")
        mem_in, x_in, par_in, small_in, cw_in = sem("mem_in"), [sem("x_in0"), sem("x_in1")], sem("par_in"), sem("small_in"), sem("cw_in")
        keys_in = sem("keys_in")
        consts, filled = sem("consts"), sem("filled")
        n_sq, n_add, n_ssq, n_rms, n_inv = sem("n_sq"), sem("n_add"), sem("n_ssq"), sem("n_rms"), sem("n_inv")
        n_scaled, n_hi, n_lo = sem("n_scaled"), sem("n_hi"), sem("n_lo")
        t_evac, nat_evac, memk_evac = sem("t_evac"), sem("nat_evac"), sem("memk_evac")
        row_dve, row_act, c_turned, cS_ready = sem("row_dve"), sem("row_act"), sem("c_turned"), sem("cS_ready")
        xs_ready, conv_step, conv_y, conv_done = sem("xs_ready"), sem("conv_step"), sem("conv_y"), sem("conv_done")
        early_out, late_out, conv_out, state_out = sem("early_out"), sem("late_out"), sem("conv_out"), sem("state_out")
        m_bc, m_s, m_arg, m_exp, m_mask = sem("m_bc"), sem("m_s"), sem("m_arg"), sem("m_exp"), sem("m_mask")
        m_sw, m_acc, m_act, m_dve, m_ssq = sem("m_sw"), sem("m_acc"), sem("m_act"), sem("m_dve"), sem("m_ssq")
        m_kt, m_st = sem("m_kt"), sem("m_st")
        nb_sq, nb_hi, nb_dve, mo_sig = sem("nb_sq"), sem("nb_hi"), sem("nb_dve"), sem("mo_sig")
        q_apart, cum_zero, cum_split = sem("q_apart"), sem("cum_zero"), sem("cum_split")
        a_sc, a_max, a_neg, a_exp = sem("a_sc"), sem("a_max"), sem("a_neg"), sem("a_exp")
        a_rcp, a_norm, a_tr, a_pt = sem("a_rcp"), sem("a_norm"), sem("a_tr"), sem("a_pt")
        a_pv, a_oh, a_ol = sem("a_pv"), sem("a_oh"), sem("a_ol")
        g_ready, g_sig, g_prod, g_acc, g_mhi, g_mlo = (
            sem("g_ready"), sem("g_sig"), sem("g_prod"), sem("g_acc"), sem("g_mhi"), sem("g_mlo"))
        fill_half, fill_evac = sem("fill_half"), sem("fill_evac")
        gate_out = [sem("gate_out0"), sem("gate_out1")]
        gate_in = [sem(f"gate_in{i}") for i in range(GATE_SLOTS)]
        x2_ready = sem("x2_ready")
        q_evac, s_ready, s_evac = sem("q_evac"), sem("s_ready"), sem("s_evac")
        tk, tk_exp, tk_turned, soft, paired = sem("tk"), sem("tk_exp"), sem("tk_turned"), sem("soft"), sem("paired")
        b_col, b_hot, b_prod, b_evac, b_written = (
            sem("b_col"), sem("b_hot"), sem("b_prod"), sem("b_evac"), [sem("b_written0"), sem("b_written1")])
        first_piece = sem("first_piece")
        h_written = [sem("h_written0"), sem("h_written1")]
        gh_in = [sem("gh_in0"), sem("gh_in1")]
        gelu_done, w_mul, w_hi_done, w_lo_done = sem("gelu_done"), sem("w_mul"), sem("w_hi_done"), sem("w_lo_done")
        v_ready, acc_done = sem("v_ready"), sem("acc_done")
        y_out = sem("y_out")

        items = attention_items()
        block = ctx.enter_context(nc.Block())

        @block.sync
        def _(sp):
            def load(src, slot, first, need):
                if not first:
                    sp.wait_ge(lo_ready, need)
                sp.dma_start(raw[:, slot, :], src).then_inc(raw_loaded[slot], 16)

            sp.wait_ge(x_in[0], 16)
            for n in range(RAW):
                load(a["units"][n], n, True, 0)
            with sp.Fori(1, U_PEER // RAW) as i:
                for k in range(RAW):
                    load(a["units"][i * RAW + k], k, False, i * RAW + k - RAW + 1)
            for n in range(U_PEER // RAW * RAW, U_PEER):
                load(a["units"][n], n % RAW, False, n - RAW + 1)
            with sp.Fori(0, NCH // RAW) as i:
                for k in range(RAW):
                    load(a["u_units"][i * RAW + k], (U_PEER + k) % RAW, False, i * RAW + (U_PEER + k - RAW + 1))
            for k in range(GRP):
                load(a["v_units"][k], (U_V + k) % RAW, False, U_V + k - RAW + 1)

            def load_gh(g, pg, need):
                if need is not None:
                    sp.wait_ge(w_mul, need)
                sp.dma_start(Gb[:, pg, :, :, :].rearrange("e b c t -> e b (c t)"),
                             gd[:, :, bass.ds(g * GRP, GRP), :].rearrange("b e c t -> e b (c t)")).then_inc(gh_in[pg], 16)
                sp.dma_start(Hb[:, pg, :, :], hd[bass.ds(g * GRP, GRP)].rearrange("c e t -> e c t")).then_inc(gh_in[pg], 16)

            def load_group(g, pg):
                load_gh(g, pg, (g - 1) * GRP)
                for k in range(GRP):
                    load(a["v_units"][g * GRP + k], (U_V + k) % RAW, False, g * GRP + (U_V + k - RAW + 1))

            sp.wait_ge(b_written[0], NBLK // 2 * PIECES * 16)
            sp.wait_ge(b_written[1], (NBLK // 2 - 1) * PIECES * 16)
            sp.wait_ge(first_piece, 16)
            for b in range(2):
                sp.wait_ge(h_written[b], 8 * (NCH - 2 * GRP))
            load_gh(0, 0, None)
            for k in range(GRP, 2 * GRP):
                load(a["v_units"][k], (U_V + k) % RAW, False, U_V + k - RAW + 1)
            sp.wait_ge(b_written[1], (NBLK // 2 * PIECES - 1) * 16)
            load_gh(1, 1, None)
            with sp.Fori(0, (NG - 4) // 2) as i:
                for b in range(2):
                    load_group(i * 2 + 2 + b, b)
            for b in range(2):
                sp.wait_ge(h_written[b], 8 * NCH)
            for g in range(NG - 2, NG):
                load_group(g, g % 2)

            for k in range(0, KT, 2):
                sp.wait_ge(n_scaled, 3 * KT + k + 2)
                sp.dma_start(o["y"][:, k:k + 2, :], fin_y[:, k:k + 2, :]).then_inc(y_out, 16)
            sp.wait_ge(y_out, KT // 2 * 16)

        @block.gpsimd
        def _(pool):
            pool.memset(ones[:, :], 1.0).then_inc(consts, 1)
            pool.memset(ident[:, :], 0.0).then_inc(filled, 1)
            pool.memset(identb[:, :], 0.0).then_inc(filled, 1)
            pool.memset(causal[:, :], 1.0).then_inc(filled, 1)
            pool.memset(maskneg[:, :], 0.0).then_inc(filled, 1)
            pool.memset(epsb[:, :], EPS).then_inc(consts, 1)
            pool.memset(oneb[:, :], 1.0).then_inc(consts, 1)
            pool.memset(cum[:, :], 0.0).then_inc(cum_zero, 1)
            pool.iota(iota[:, :], [[1, P]], base=0, channel_multiplier=0,
                      allow_small_or_imprecise_dtypes=True).then_inc(consts, 1)
            pool.wait_ge(filled, 4)
            for m in (ident, identb):
                pool.affine_select(out=m[:, :], in_=m[:, :], compare_op=ALU.not_equal, fill=1.0, base=0,
                                   pattern=[[-1, P]], channel_multiplier=1).then_inc(consts, 1)
            pool.affine_select(out=causal[:, :], in_=causal[:, :], compare_op=ALU.is_ge, fill=0.0, base=0,
                               pattern=[[1, P]], channel_multiplier=-1).then_inc(consts, 1)
            pool.affine_select(out=maskneg[:, :], in_=maskneg[:, :], compare_op=ALU.is_ge, fill=-1e30, base=0,
                               pattern=[[-1, P]], channel_multiplier=1).then_inc(consts, 1)

            def low_half(n, k):
                pool.wait_ge(hi_ready, n + 1)
                pool.tensor_tensor(w_lo[:, k % RING, :], raw[:, k % RAW, :], w_hi[:, k % RING, :],
                                   ALU.subtract).then_inc(lo_ready, 1)

            with pool.Fori(0, U_PEER // RING) as i:
                for k in range(RING):
                    low_half(i * RING + k, k)
            for n in range(U_PEER // RING * RING, U_PEER):
                low_half(n, n)
            with pool.Fori(0, 2 * NCH // RING) as i:
                for k in range(RING):
                    low_half(i * RING + U_PEER + k, U_PEER + k)

        @block.scalar
        def _(act):
            for half in range(2):
                rows = slice(half * KT // 2, (half + 1) * KT // 2)
                act.dma_start(xT[:, rows, :], a["xT"][:, rows, :]).then_inc(x_in[half], 16)
            act.dma_start(par[:, :], a["par"]).then_inc(par_in, 16)

            def load_small():
                act.wait_ge(cum_zero, 1)
                act.dma_start(cum[32:40, TP:TP + PAST], a["lf_past"]).then_inc(small_in, 16)
                act.dma_start(c0[:, :, :], a["c0"]).then_inc(small_in, 16)
                act.dma_start(n0[:, :], a["n0"]).then_inc(small_in, 16)
                act.dma_start(m0[:, :], a["m0"].rearrange("a h -> h a")).then_inc(small_in, 16)
                act.dma_start(m0b[:, :], a["m0"].broadcast_to((P, HM))).then_inc(small_in, 16)
                act.dma_start(kc[:, :, :], a["kc"]).then_inc(small_in, 16)
                act.dma_start(vc[:, :, :], a["vc"]).then_inc(small_in, 16)
                act.dma_start(kpast[:, :, :], a["kpast"]).then_inc(small_in, 16)
                act.dma_start(vpast[:, :], a["vpast"]).then_inc(small_in, 16)

            def square(x, sq, ready=None, tiles=range(KT)):
                for k in tiles:
                    if ready:
                        act.wait_ge(*ready(k))
                    act.activation(sq[:, k, :], x[:, k, :], ACT.Square).then_inc(n_sq, 1)

            def root(i, out, sums):
                act.activation(warm[:, i:i + 1], epsb[:, 0:1], ACT.Sqrt)
                act.wait_ge(n_ssq, i + 1)
                act.activation(out, sums, ACT.Sqrt, bias=epsb[:, 0:1], scale=1.0 / D).then_inc(n_rms, 1)

            def high(i, h, hi):
                for k in range(KT):
                    act.wait_ge(n_scaled, KT * i + k + 1)
                    act.activation(hi[:, k, :], h[:, k, :], ACT.Copy).then_inc(n_hi, 1)

            def high_half(n, k, load_count=None):
                act.wait_ge(raw_loaded[k % RAW], load_count)
                act.activation(w_hi[:, k % RING, :], raw[:, k % RAW, :], ACT.Copy).then_inc(hi_ready, 1)

            def high_unit(n):
                if n >= RING:
                    act.wait_ge(unit_used, n - RING + 1)
                high_half(n, n, 16 * (n // RAW + 1))

            act.wait_ge(consts, 8)
            square(xT, mix_sq, lambda k: (x_in[k // (KT // 2)], 16))
            act.wait_ge(par_in, 16)
            for n in range(RAW):
                high_unit(n)
            act.dma_start(mem_x[:, :, :], a["memT"]).then_inc(mem_in, 16)
            act.dma_start(xs[:, :, 0:3], a["conv_state"]).then_inc(cw_in, 16)
            root(0, wk[:, 1, :].rearrange("p (a b) -> p a b", a=2), ps[:, 0:2, 0:HALF])
            high(0, mix_h, act_hi)
            act.wait_ge(mem_in, 16)
            square(mem_x, mem_sq)
            for n in range(RAW, RING + 4):
                high_unit(n)
            root(1, wk[:, 0, 0:NMEM], ps[:, 4, 0:NMEM])
            high(1, mem_h, mem_hi)
            load_small()
            for n in range(U_T + 4, U_T + N_T):
                high_unit(n + RING)

            act.wait_ge(t_evac, N_T)
            act.dma_start(o["conv_p"], proj[:, 0:KT, TP - 3:TP]).then_inc(conv_out, 16)
            act.dma_start(o["conv_s"], proj[:, 0:KT, T - 3:T]).then_inc(conv_out, 16)
            high_unit(U_SMALL + RING)

            def silu(c):
                act.wait_ge(conv_y, c + 1)
                act.activation(proj[:, c, :], wk[:, 3 + c % 2, :], ACT.Silu).then_inc(conv_done, 1)

            for q in range(N_MEMK):
                act.wait_ge(unit_used, U_MEMK + q + 1)
                act.activation(mkT[:, q, :], ps[:, 2 + q % 2, 0:NMEM], ACT.Copy).then_inc(memk_evac, 1)
                high_unit(U_MEMK + q + RING)
                if q == 1:
                    act.wait_ge(conv_out, 2 * 16)
                if q % 2:
                    silu(q // 2)
            act.wait_ge(memk_evac, N_MEMK)
            act.dma_start(o["memk"], mkT[:, :, :]).then_inc(early_out, 16)
            for n in range(U_MEMV, U_MEMV + N_MEMV):
                high_unit(n + RING)
            act.activation(mvN[:, :, :], ps[:, 4:6, :], ACT.Copy).then_inc(nat_evac, 1)
            silu(2)
            act.wait_ge(nat_evac, 1)
            act.dma_start(o["memv"], mvN[:, :, :]).then_inc(early_out, 16)
            for first, buf, convs in ((U_MV, mv, (3, 4)), (U_FV, fv, (5, 6, 7))):
                for k in range(4):
                    high_unit(first + k + RING)
                    if k < len(convs):
                        silu(convs[k])
                for t in (2, 3, 0, 1):
                    act.activation(buf[:, t, :], ps[:, 4 + t, :], ACT.Copy).then_inc(nat_evac, 1)
                act.activation(buf[0:TS, 4, :], ps[0:TS, 2 if buf is mv else 3, :], ACT.Copy).then_inc(nat_evac, 1)

            act.wait_ge(nat_evac, 11)
            act.dma_start(o["fv_p"], fv[:, 0:4, :]).then_inc(early_out, 16)
            act.dma_start(o["fv_s"], fv[0:TS, 4, :]).then_inc(early_out, 16)

            def fill_out(x):
                t, half = x // 2, x % 2
                if half:
                    act.wait_ge(unit_used, U_FILL + t + 1)
                else:
                    act.wait_ge(fill_half, t + 1)
                cols = slice(half * HALF, (half + 1) * HALF)
                g = t - N_PROJ
                if g < 0:
                    dst = proj[:, FILL_SLOTS[t], cols]
                else:
                    dst = stage[:, g % 2, cols]
                    if g == 0 and not half:
                        act.wait_ge(late_out, 4 * 16)
                    if g >= 2 and not half:
                        act.wait_ge(gate_out[g % 2], g // 2 * 16)
                act.activation(dst, ps[:, 6 + half, 0:HALF], ACT.Copy).then_inc(fill_evac, 1)
                if half:
                    if g >= 0:
                        act.wait_ge(fill_evac, fill_index(x) + 1)
                        act.dma_start(gz[g], stage[:, g % 2, :]).then_inc(gate_out[g % 2], 16)
                    high_unit(U_FILL + t + RING)

            act.wait_ge(row_dve, 2)
            act.activation(trow[:, :], zrow[:, :], ACT.Abs).then_inc(row_act, 1)
            act.wait_ge(row_act, 1)
            act.activation(trow[:, :], trow[:, :], ACT.Exp, scale=-1.0).then_inc(row_act, 1)
            act.wait_ge(row_act, 2)
            act.activation(trow[:, :], trow[:, :], ACT.Ln, bias=oneb[0:40, 0:1]).then_inc(row_act, 1)

            for x in range(2 * PRE_TILES):
                fill_out(x)
            act.wait_ge(fill_evac, 2 * PRE_TILES)
            act.activation(proj[:, MO:MO + HM, :], proj[:, MO:MO + HM, :], ACT.Sigmoid).then_inc(mo_sig, 1)
            act.wait_ge(row_dve, 16)
            act.dma_start(o["lf_p"], lsig[32:40, 0:TP]).then_inc(late_out, 16)
            act.dma_start(o["lf_s"], lsig[32:40, TP:T]).then_inc(late_out, 16)
            act.dma_start(o["m_p"], m_row[:, TP - 1:TP]).then_inc(late_out, 16)
            act.dma_start(o["m_s"], m_row[:, T - 1:T]).then_inc(late_out, 16)

            def head_square(h):
                act.wait_ge(m_dve, N_MD * h + 7)
                if h:
                    act.wait_ge(nb_dve, N_NB * (h - 1) + 3)
                act.activation(wk[:, 4, :], proj[:, MK + h, :], ACT.Square).then_inc(nb_sq, 1)

            def head_roots(h):
                for half in range(2):
                    act.wait_ge(m_ssq, 2 * h + half + 1)
                    act.activation(wk[:, 4, half * HALF:(half + 1) * HALF], ps[:, 6 + half, 0:HALF], ACT.Sqrt,
                                   bias=epsb[:, 0:1], scale=1.0 / P).then_inc(fill_evac, 1)

            def head_high(h):
                act.wait_ge(nb_dve, N_NB * h + 4)
                act.activation(proj_b[:, MO + h, 0, :], proj[:, MK + h, :], ACT.Copy).then_inc(nb_hi, 1)

            act.wait_ge(small_in, 9 * 16)
            for h in range(HM):
                x0 = 2 * PRE_TILES + h * (H_PIECES // 3)
                for j in range(5):
                    q = 5 * h + j
                    n = TP - P * j if j < 4 else TS
                    rows = P if j < 4 else TS
                    act.wait_ge(m_arg, q + 1)
                    buf = wk[0:rows, j % 2, 0:n]
                    act.activation(buf, buf, ACT.Exp).then_inc(m_exp, 1)
                    if j == 0:
                        act.wait_ge(m_bc, h + 1)
                        act.activation(sm[:, 0, :], ps[:, 3, 0:TS], ACT.Exp, bias=m0b[:, h:h + 1]).then_inc(m_act, 1)
                        act.activation(wk[:, 2, 0:TP], ps[:, 4, :], ACT.Exp, scale=-1.0).then_inc(m_act, 1)
                        act.activation(wk[:, 2, TP:T], ps[:, 3, TS:2 * TS], ACT.Exp, scale=-1.0).then_inc(m_act, 1)
                        act.wait_ge(m_dve, N_MD * h + 1)
                        act.activation(ws[:, 0:4], cS[:, 0:4, h], ACT.Exp, bias=ws[:, 6:7]).then_inc(m_act, 1)
                        act.activation(ws[0:TS, 4:5], cS[0:TS, 4, h:h + 1], ACT.Exp, bias=ws[0:TS, 7:8]).then_inc(m_act, 1)
                        act.activation(ws[:, 5:6], m0b[:, h:h + 1], ACT.Exp, bias=ws[:, 7:8]).then_inc(m_act, 1)
                        if h:
                            head_square(h - 1)
                        fill_out(x0)
                    if j == 1:
                        fill_out(x0 + 1)
                    if j == 2 and h:
                        head_roots(h - 1)
                    if j == 4:
                        fill_out(x0 + 2)
                act.wait_ge(m_acc, 5 * h + 5)
                act.activation(wk[:, 3, 0:TP], ps[:, 5, :], ACT.Abs).then_inc(m_act, 1)
                act.activation(wk[:, 3, TP:T], ps[:, 3, 320:320 + TS], ACT.Abs).then_inc(m_act, 1)
                fill_out(x0 + 3)
                if h:
                    head_high(h - 1)
                fill_out(x0 + 4)
                fill_out(x0 + 5)
            head_square(HM - 1)
            head_roots(HM - 1)
            act.wait_ge(m_dve, N_MD * HM)
            act.dma_start(o["cn_p"], proj[:, 0:HM, 0:P + 1]).then_inc(state_out, 16)
            act.dma_start(o["cn_s"], proj[:, 0:HM, 256:256 + P + 1]).then_inc(state_out, 16)
            act.wait_ge(fill_evac, fill_index(2 * N_PROJ - 1) + 1)
            act.dma_start(o["fk"], proj[:, FK:FK + 4, :]).then_inc(early_out, 16)

            def copy_turned(i):
                kind, h, qi = items[i]
                nb = (qi + 1 if qi < 4 else 2) if kind == "fox" else 2
                act.wait_ge(a_tr, i + 1)
                if i >= 2:
                    act.wait_ge(a_pv, i - 1)
                dst = wk[:, 2 + i % 2, 0:512]
                if qi < 4:
                    act.activation(dst[:, 0:nb * P], ps[:, 2 + i % 2, 0:nb * P], ACT.Copy).then_inc(a_pt, 1)
                elif kind == "mem":
                    act.activation(dst.rearrange("p (b t) -> p b t", b=4)[:, 0:2, 0:TS],
                                   ps[:, 2 + i % 2, :].rearrange("p (b t) -> p b t", b=4)[:, 0:2, 0:TS],
                                   ACT.Copy).then_inc(a_pt, 1)
                else:
                    act.activation(dst[:, 0:TS], ps[:, 2 + i % 2, 0:TS], ACT.Copy)
                    act.activation(dst[0:TS, P:P + TS], ps[0:TS, 2 + i % 2, P:P + TS], ACT.Copy).then_inc(a_pt, 1)

            def out_high(i):
                kind, h, qi = items[i]
                if kind == "fox" and h % 2 == 0:
                    return
                slot, n = out_slot(kind, h), P if qi < 4 else TS
                if i == 1:
                    act.wait_ge(state_out, 2 * 16)
                act.wait_ge(a_pv, i + 1)
                act.activation(proj_b[:, slot, 0, qi * P:qi * P + n], ps[:, 4 + out_index(i) % 2, 0:n],
                               ACT.Copy).then_inc(a_oh, 1)

            def load_gate(r):
                act.dma_start(proj[:, FQ + r % GATE_SLOTS, :], gz[r]).then_inc(gate_in[r % GATE_SLOTS], 16)

            for x in range(LEAD // 3):
                fill_out(2 * N_PROJ + x)
            for i in range(len(items)):
                kind, h, qi = items[i]
                n, cols = P if qi < 4 else TS, columns(kind, qi)
                act.wait_ge(a_neg, i + 1)
                if i >= 2:
                    act.wait_ge(a_tr, i - 1)
                act.activation(wk[0:n, i % 2, 0:cols], ps[0:n, i % 2, 0:cols], ACT.Exp,
                               bias=st[0:n, i % 2, 0:1], scale=scale_of(kind),
                               accum_out=st[0:n, i % 2, 1:2]).then_inc(a_exp, 1)
                if i == 4:
                    head_high(HM - 1)
                if i >= 1:
                    copy_turned(i - 1)
                    for x in gate_halves(i - 1):
                        fill_out(x)
                if i >= 2:
                    out_high(i - 2)
                if i == HF * NTT + 6:
                    act.wait_ge(early_out, 5 * 16)
                    act.wait_ge(a_pv, HF * NTT)
                    for b in range(2):
                        act.wait_ge(gate_out[b], GATE_SLOTS // 2 * 16)
                    for r in range(GATE_SLOTS):
                        load_gate(r)
            copy_turned(len(items) - 1)
            for x in gate_halves(len(items) - 1):
                fill_out(x)
            out_high(len(items) - 2)
            out_high(len(items) - 1)

            for b in range(2):
                act.wait_ge(gate_out[b], N_GATE // 2 * 16)

            def merged_high(j):
                act.wait_ge(g_acc, merged_count(j))
                act.activation(mg_hi[:, j, :], proj[:, acc_slot(j), :], ACT.Copy).then_inc(g_mhi, 1)

            for r in range(N_GATE):
                gate = proj[:, FQ + r % GATE_SLOTS, :]
                act.wait_ge(gate_in[r % GATE_SLOTS], 16 * (r // GATE_SLOTS + 1))
                act.activation(gate, gate, ACT.Sigmoid).then_inc(g_sig, 1)
                if r >= 2 and r + GATE_SLOTS - 2 < N_GATE:
                    if (r - 2) % 6 < 2:
                        act.wait_ge(g_prod, r - 1)
                    else:
                        act.wait_ge(g_acc, 4 * ((r - 2) // 6) + (r - 2) % 6 - 1)
                    load_gate(r + GATE_SLOTS - 2)
                if r % 2:
                    high_unit(U_MERGE + r // 2 + RING)
                if r % 6 == 1 and r > 6:
                    for j2 in range(2):
                        merged_high((r // 6 - 1) * 2 + j2)
            for j in range(KT - 2, KT):
                merged_high(j)
            for j in range(KT):
                high_unit(U_OUT + j + RING)
                if j:
                    square(xT, proj[:, 0:KT, :], lambda k: (x2_ready, k + 1), [j - 1])

            square(xT, proj[:, 0:KT, :], lambda k: (x2_ready, k + 1), [KT - 1])
            act.dma_start(keys[:, :, :], a["keysT"]).then_inc(keys_in, 16)
            root(2, wk[:, 1, :].rearrange("p (a b) -> p a b", a=2), ps[:, 4:6, 0:HALF])
            high(2, proj[:, 8:8 + KT, :], act_hi)

            for q in range(NHC):
                n = U_WQ + q
                act.wait_ge(unit_used, n + 1)
                if q >= 2:
                    act.wait_ge(s_ready, q - 1)
                act.activation(qr[:, q % 2, :].rearrange("p (a b) -> p a b", a=2),
                               ps[:, 2 * (q % 2):2 * (q % 2) + 2, 0:HALF], ACT.Copy).then_inc(q_evac, 1)
                high_unit(n + RING)

            def chunk(j, k, first=False):
                c = j * BODY + k
                act.wait_ge(unit_used, j * BODY + (U_PEER + k + 1))
                if not (first and k < 2):
                    act.wait_ge(h_written[k % 2], j * (16 * BODY // 2) + 16 * (k // 2))
                act.activation(hb[:, k % 2, :].rearrange("p (a b) -> p a b", a=2),
                               ps[:, 2 * (k % 2):2 * (k % 2) + 2, 0:HALF], ACT.Gelu_apprx_tanh).then_inc(gelu_done, 1)
                high_half(None, U_PEER + k, j * 32 + 16 * ((U_PEER + RING + k) // RAW + 1))
                act.wait_ge(gelu_done, j * BODY + (k + 1))
                act.dma_start(hd[bass.ds(c, 1)].rearrange("c e t -> e (c t)"), hb[:, k % 2, :]).then_inc(h_written[k % 2], 16)

            def write_piece(blk, b, piece, evacuated, done=None):
                rows = slice(piece * (NCH // PIECES), (piece + 1) * (NCH // PIECES))
                act.wait_ge(b_evac, evacuated)
                act.dma_start(gd[bass.ds(blk, 1), :, rows, :].rearrange("o e c t -> (o e) (c t)"),
                              gsb[:, b, rows, :].rearrange("e c t -> e (c t)"))\
                    .then_inc(b_written[b] if done is None else done, 16)

            steps = TBLK // GT

            def three_bodies(it, first=False):
                for jj in range(3):
                    for k in range(BODY):
                        chunk(it * 3 + (J_G + jj), k)
                        at_chunk = jj * BODY + k
                        if first and at_chunk == 0:
                            act.wait_ge(paired, 1)
                        for e in range(2):
                            s = 2 * at_chunk + e
                            b, at = s // steps, (s % steps) * GT
                            act.wait_ge(b_prod, it * (2 * steps) + s + 1)
                            if at == 0 and b == 0 and not first:
                                act.wait_ge(b_written[0], it * (PIECES * 16))
                            if at == 0 and b == 1 and not first:
                                act.wait_ge(b_written[1], it * (PIECES * 16))
                            act.activation(gsb[:, b, :, at:at + GT].rearrange("p k u -> p u k"),
                                           ps[:, 4 + e, :].rearrange("p (u k) -> p u k", u=GT), ACT.Copy).then_inc(b_evac, 1)
                        if at_chunk < PIECES and not first:
                            write_piece(it * 2 - 1, 1, at_chunk, it * (2 * steps))
                        if steps // 2 <= at_chunk < steps // 2 + PIECES:
                            write_piece(it * 2, 0, at_chunk - steps // 2, it * (2 * steps) + steps)

            for k in range(BODY):
                chunk(0, k, first=True)
            with act.Fori(1, J_G) as j:
                for k in range(BODY):
                    chunk(j, k)
            act.wait_ge(tk, NTT * N_TK)
            act.activation(trip[:, 2, :, :], trip[:, 2, :, :], ACT.Exp).then_inc(tk_exp, 1)
            three_bodies(0, first=True)
            with act.Fori(1, NBLK // 2) as it:
                three_bodies(it)
            def w_high(g, b, k):
                act.wait_ge(w_mul, (0 if g is None else g * GRP) + k + 1)
                act.activation(W_hi[:, b, k, :], wb[:, k % 2, :], ACT.Copy).then_inc(w_hi_done, 1)

            write_piece(NBLK - 1, 1, 0, T // GT, first_piece)
            for k in range(BODY):
                chunk(J_END, k)
                if k + 1 < PIECES:
                    write_piece(NBLK - 1, 1, k + 1, T // GT)
                if k >= BODY - 2:
                    for kk in range((k - BODY + 2) * GRP // 2, (k - BODY + 3) * GRP // 2):
                        w_high(None, 0, kk)

            def second(g, b, more):
                act.wait_ge(unit_used, g * GRP + (U_V - GRP))
                for k in range(GRP):
                    w_high(g, b, k)
                if more:
                    for k in range(GRP):
                        act.wait_ge(unit_used, g * GRP + (U_V - GRP + k + 1))
                        high_half(None, U_V + (0 if b else GRP) + k, loads(g, k))

            def loads(g, k):
                return g * 16 + 16 * ((U_V + GRP + k) // RAW + 1)

            with act.Fori(0, (NG - 2) // 2) as i:
                for b in range(2):
                    second(i * 2 + (1 + b), (1 + b) % 2, True)
            second(NG - 1, (NG - 1) % 2, False)

            square(xT, fin_sq, lambda k: (acc_done, (NG - 1) * KT + k + 1))
            root(3, wb[:, 0, :].rearrange("p (a b) -> p a b", a=2), ps[:, 0:2, 0:HALF])

        @block.vector
        def _(dve):
            def norm(i, x, col, rs, h, hi, lo):
                dve.wait_ge(n_rms, i + 1)
                dve.reciprocal(rs, rs).then_inc(n_inv, 1)
                dve.wait_ge(n_inv, i + 1)
                for k in range(KT + 1):
                    if k < KT:
                        dve.scalar_tensor_tensor(out=h[:, k, :], in0=x[:, k, :], scalar=par[:, col + k:col + k + 1],
                                                 in1=rs, op0=ALU.mult, op1=ALU.mult).then_inc(n_scaled, 1)
                    if k and hi is not None:
                        dve.wait_ge(n_hi, KT * i + k)
                        dve.tensor_tensor(lo[:, k - 1, :], h[:, k - 1, :], hi[:, k - 1, :], ALU.subtract).then_inc(n_lo, 1)

            def add_square(i, k, sq):
                dve.wait_ge(n_sq, KT * i + k + 1)
                if k > 1:
                    dve.wait_ge(n_add, (KT - 1) * i + k - 1)
                dve.tensor_tensor(sq[:, 0, :], sq[:, 0, :], sq[:, k, :], ALU.add).then_inc(n_add, 1)

            for k in range(1, KT):
                add_square(0, k, mix_sq)
            dve.wait_ge(par_in, 16)
            norm(0, xT, C_MIX, wk[:, 1, :], mix_h, act_hi, act_lo)

            def copy_tile(k):
                dve.wait_ge(unit_used, U_T + k + 1)
                dve.tensor_copy(proj[:, k, :].rearrange("p (a b) -> p a b", a=2),
                                ps[:, 2 * (k % 2):2 * (k % 2) + 2, 0:HALF]).then_inc(t_evac, 1)

            for k in range(3):
                copy_tile(k)
            for k in range(1, KT):
                add_square(1, k, mem_sq)
            copy_tile(3)
            norm(1, mem_x, C_MEM, wk[:, 0, 0:NMEM], mem_h, mem_hi, mem_lo)
            for k in range(4, N_T):
                copy_tile(k)

            dve.wait_ge(t_evac, N_T)
            dve.wait_ge(cw_in, 16)
            dve.tensor_copy(xs[:, :, 3:3 + TS], proj[:, 0:KT, TP:T]).then_inc(xs_ready, 1)
            dve.wait_ge(xs_ready, 1)
            rd = [0]

            def row(ins, wait=True):
                rd[0] += 1
                ins.then_inc(row_dve, 1)
                if wait:
                    dve.wait_ge(row_dve, rd[0])

            two = lambda x: x.rearrange("p (a b) -> p a b", a=2)
            step = 0
            for c in range(KT):
                y = wk[:, 3 + c % 2, :]
                w = [par[:, C_CW + 8 * j + c:C_CW + 8 * j + c + 1] for j in range(4)]
                if c >= 2:
                    dve.wait_ge(conv_done, c - 1)
                dve.tensor_scalar(y, proj[:, c, :], w[3], par[:, C_CB + c:C_CB + c + 1], ALU.mult,
                                  ALU.add).then_inc(conv_step, 1)
                step += 1
                for j in range(1, 4):
                    dve.wait_ge(conv_step, step)
                    dve.scalar_tensor_tensor(out=y[:, j:TP], in0=proj[:, c, 0:TP - j], scalar=w[3 - j],
                                             in1=y[:, j:TP], op0=ALU.mult, op1=ALU.add)
                    last = dve.scalar_tensor_tensor(out=y[:, TP:T], in0=xs[:, c, 3 - j:3 - j + TS], scalar=w[3 - j],
                                                    in1=y[:, TP:T], op0=ALU.mult, op1=ALU.add)
                    last.then_inc(conv_step if j < 3 else conv_y, 1)
                    step += j < 3
                if c == 0:
                    dve.wait_ge(unit_used, U_SMALL + 1)
                    row(dve.tensor_scalar(two(zrow[:, :]), ps[0:40, 0:2, 0:HALF], par[0:40, C_ZB:C_ZB + 1], None,
                                          ALU.add), False)
                    row(dve.tensor_scalar(two(c_row[:, :]), ps[64:68, 0:2, 0:HALF], par[64:68, C_IB:C_IB + 1], None,
                                          ALU.add), False)

            dve.wait_ge(row_act, 3)
            row(dve.scalar_tensor_tensor(out=lsig[:, :], in0=zrow[:, :], scalar=0.0, in1=trow[:, :],
                                         op0=ALU.min, op1=ALU.subtract))
            for lo_, hi_ in ((0, TP), (TP, T)):
                row(dve.tensor_tensor_scan(m_row[:, lo_:hi_], ones[0:4, 0:1].broadcast_to((4, hi_ - lo_)),
                                           lsig[0:4, lo_:hi_], 0.0, ALU.mult, ALU.add), hi_ == T)
            row(dve.tensor_tensor(c_row[:, :], c_row[:, :], m_row[:, :], ALU.subtract))
            dve.wait_ge(small_in, 9 * 16)
            row(dve.tensor_tensor_scan(nM[:, 0:TP], c_row[:, 0:TP], c_row[:, 0:TP], 0.0, ALU.max, ALU.max), False)
            row(dve.tensor_tensor_scan(nM[:, TP:T], c_row[:, TP:T], c_row[:, TP:T], m0[:, 0:1], ALU.max, ALU.max))
            row(dve.tensor_tensor(m_row[:, :], m_row[:, :], nM[:, :], ALU.add))
            row(dve.tensor_scalar(nM[:, :], nM[:, :], -1.0, None, ALU.mult))
            row(dve.tensor_copy(cum[32:40, TP + PAST:704], lsig[32:40, TP:T]), True)
            row(dve.tensor_tensor_scan(cum[32:40, 0:TP], ones[32:40, 0:1].broadcast_to((8, TP)), lsig[32:40, 0:TP],
                                       0.0, ALU.mult, ALU.add), False)
            row(dve.tensor_tensor_scan(wk[32:40, 2, 0:192], ones[32:40, 0:1].broadcast_to((8, 192)),
                                       cum[32:40, TP:704], 0.0, ALU.mult, ALU.add))
            row(dve.tensor_scalar(cum[32:40, 0:TP], cum[32:40, 0:TP], -(FD ** 0.5), None, ALU.mult), False)
            row(dve.tensor_scalar(cum[32:40, TP:704], wk[32:40, 2, 0:192], -(FD ** 0.5), None, ALU.mult))
            dve.wait_ge(c_turned, 1)
            dve.tensor_copy(cS[:, 0:4, :], ps[:, 2, 0:16].rearrange("p (a b) -> p a b", a=4)).then_inc(cS_ready, 1)
            dve.tensor_copy(cS[0:TS, 4, :], ps[0:TS, 2, 16:20]).then_inc(cS_ready, 1)
            row(dve.memset(st[:, :, :], 0.0))
            dve.wait_ge(cS_ready, 2)

            def head_root(h, half):
                root_ = wk[:, 4, half * HALF:(half + 1) * HALF]
                dve.wait_ge(fill_evac, norm_index(h) + half + 1)
                dve.reciprocal(root_, root_).then_inc(nb_dve, 1)

            def head_scale(h):
                out = proj[:, MK + h, :]
                dve.wait_ge(nb_dve, N_NB * h + 2)
                dve.scalar_tensor_tensor(out=out, in0=out, scalar=par[:, C_HEAD + h:C_HEAD + h + 1],
                                         in1=wk[:, 4, :], op0=ALU.mult, op1=ALU.mult).then_inc(nb_dve, 1)
                dve.wait_ge(nb_dve, N_NB * h + 3)
                dve.wait_ge(mo_sig, 1)
                dve.tensor_tensor(out, out, proj[:, MO + h, :], ALU.mult).then_inc(nb_dve, 1)

            def head_low(h):
                dve.wait_ge(nb_hi, h + 1)
                dve.tensor_tensor(proj_b[:, MO + h, 1, :], proj[:, MK + h, :], proj_b[:, MO + h, 0, :],
                                  ALU.subtract).then_inc(nb_dve, 1)

            n_split = [0]

            def split_cum(part):
                def step(ins):
                    n_split[0] += 1
                    ins.then_inc(cum_split, 1)
                    dve.wait_ge(cum_split, n_split[0])

                work, rest = cum3[32:40, :], cum[32:40, :]
                if part == 0:
                    step(dve.memset(cum3[:, :], 0.0))
                    step(dve.tensor_tensor(pick3[:, :], identb[:, 32:40], identb[:, 64:72], ALU.add))
                    step(dve.tensor_tensor(pick3[:, :], pick3[:, :], identb[:, 96:104], ALU.add))
                step(dve.tensor_copy(work, rest))
                if part < 2:
                    step(dve.tensor_tensor(rest, rest, work, ALU.subtract))
                    row_ = (96, 64)[part]
                    step(dve.tensor_copy(cum3[row_:row_ + 8, :], work))
                else:
                    assert n_split[0] == N_SPLIT

            for h in range(HM):
                md = N_MD * h
                dve.wait_ge(m_bc, h + 1)
                dve.tensor_copy(ws[:, 6:7], ps[:, 2, TP - 1:TP])
                dve.tensor_copy(ws[:, 7:8], ps[:, 3, TS - 1:TS]).then_inc(m_dve, 1)

                def argument(j):
                    q = 5 * h + j
                    n = TP - P * j if j < 4 else TS
                    rows = P if j < 4 else TS
                    src = ps[0:rows, 2, P * j:TP] if j < 4 else ps[0:rows, 3, 0:TS]
                    if q >= 2:
                        dve.wait_ge(m_acc, q - 1)
                    dve.tensor_scalar(wk[0:rows, j % 2, 0:n], src, cS[0:rows, j, h:h + 1], 0.0, ALU.add,
                                      ALU.min).then_inc(m_arg, 1)

                def weigh(j):
                    q = 5 * h + j
                    n = TP - P * j if j < 4 else TS
                    rows = P if j < 4 else TS
                    buf = wk[0:rows, j % 2, :]
                    dve.wait_ge(m_exp, q + 1)
                    dve.tensor_tensor(buf[:, 0:rows], buf[:, 0:rows], causal[0:rows, 0:rows], ALU.mult).then_inc(m_mask, 1)
                    dve.wait_ge(m_mask, q + 1)
                    dve.wait_ge(m_s, q + 1)
                    dve.scalar_tensor_tensor(out=buf[:, 0:n], in0=ps[0:rows, j % 2, 0:n], scalar=SQRT_HM,
                                             in1=buf[:, 0:n], op0=ALU.mult, op1=ALU.mult).then_inc(m_sw, 1)

                argument(0)
                argument(1)
                dve.wait_ge(m_act, N_MA * h + 1)
                dve.tensor_tensor(sm[:, 1, :], sm[:, 0, :], proj[:, MQ + h, TP:T], ALU.mult).then_inc(m_dve, 1)
                for j in range(5):
                    weigh(j)
                    if j + 2 < 5:
                        argument(j + 2)
                    if j in (2, 3) and h:
                        head_root(h - 1, j - 2)
                    if h == 0 and j >= 2:
                        split_cum(j - 2)
                if h:
                    head_scale(h - 1)
                dve.wait_ge(m_kt, h + 1)
                dve.wait_ge(m_act, N_MA * h + 6)
                for j in range(4):
                    dve.tensor_scalar(wk[:, 0, j * P:(j + 1) * P], ps[:, 1, j * P:(j + 1) * P], ws[:, j:j + 1], SQRT_HM,
                                      ALU.mult, ALU.mult)
                dve.tensor_scalar(wk[0:TS, 1, 0:P], ps[0:TS, 2, 0:P], ws[0:TS, 4:5], SQRT_HM, ALU.mult,
                                  ALU.mult).then_inc(m_dve, 1)
                dve.wait_ge(m_act, N_MA * h + 8)
                dve.tensor_tensor(wk[:, 3, :], wk[:, 3, :], wk[:, 2, :], ALU.max).then_inc(m_dve, 1)
                dve.wait_ge(m_dve, md + 4)
                dve.reciprocal(wk[:, 3, :], wk[:, 3, :]).then_inc(m_dve, 1)
                dve.wait_ge(m_dve, md + 5)
                dve.tensor_tensor(proj[:, MK + h, 0:TP], ps[:, 4, :], wk[:, 3, 0:TP], ALU.mult).then_inc(m_dve, 1)
                dve.tensor_tensor(proj[:, MK + h, TP:T], ps[:, 3, 256:256 + TS], wk[:, 3, TP:T], ALU.mult).then_inc(m_dve, 1)
                if h:
                    head_low(h - 1)
                dve.wait_ge(m_st, h + 1)
                dve.tensor_copy(proj[:, MQ + h, 0:P + 1], ps[:, 2, 0:P + 1]).then_inc(m_dve, 1)
                dve.scalar_tensor_tensor(out=proj[:, MQ + h, 256:256 + P], in0=c0[:, h, :], scalar=ws[:, 5:6],
                                         in1=ps[:, 2, 256:256 + P], op0=ALU.mult, op1=ALU.add)
                dve.scalar_tensor_tensor(out=proj[:, MQ + h, 384:385], in0=n0[:, h:h + 1], scalar=ws[:, 5:6],
                                         in1=ps[:, 2, 384:385], op0=ALU.mult, op1=ALU.add).then_inc(m_dve, 1)

            def maxima(i):
                kind, h, qi = items[i]
                n, cols = P if qi < 4 else TS, columns(kind, qi)
                dve.wait_ge(a_sc, i + 1)
                if i >= 2:
                    dve.wait_ge(a_norm, i - 1)
                dve.reduce_max(st[0:n, i % 2, 3:4], ps[0:n, i % 2, 0:cols], AX.X).then_inc(a_max, 1)
                dve.wait_ge(a_max, i + 1)
                dve.tensor_scalar(st[0:n, i % 2, 0:1], st[0:n, i % 2, 3:4], -scale_of(kind), None,
                                  ALU.mult).then_inc(a_neg, 1)

            def out_low(i):
                kind, h, qi = items[i]
                if kind == "fox" and h % 2 == 0:
                    return
                slot, n, x = out_slot(kind, h), P if qi < 4 else TS, out_index(i)
                if i == 1:
                    dve.wait_ge(state_out, 2 * 16)
                dve.wait_ge(a_oh, x + 1)
                dve.tensor_tensor(proj_b[:, slot, 1, qi * P:qi * P + n], ps[:, 4 + x % 2, 0:n],
                                  proj_b[:, slot, 0, qi * P:qi * P + n], ALU.subtract).then_inc(a_ol, 1)

            dve.wait_ge(fill_evac, fill_index(2 * N_PROJ - 1) + 1)
            def queries_apart(hp):
                for hh in range(2):
                    rows = slice(FD * hh, FD * hh + FD)
                    last = dve.tensor_copy(qz[rows, hp % 2, hh, :], proj[rows, FQ + hp, :])
                last.then_inc(q_apart, 1)

            dve.memset(qz[FD:P, :, 0, :], 0.0)
            dve.memset(qz[0:FD, :, 1, :], 0.0)
            queries_apart(0)
            queries_apart(1)
            maxima(0)
            for i in range(len(items)):
                kind, h, qi = items[i]
                n, cols = P if qi < 4 else TS, columns(kind, qi)
                if i + 1 < len(items):
                    maxima(i + 1)
                if kind == "fox" and i % (2 * NTT) == 0 and 1 <= i // (2 * NTT) < HF // 2 - 1:
                    queries_apart(i // (2 * NTT) + 1)
                if i in (1, 2):
                    head_root(HM - 1, i - 1)
                if i == 3:
                    head_scale(HM - 1)
                if i == 5:
                    head_low(HM - 1)
                dve.wait_ge(a_exp, i + 1)
                dve.reciprocal(st[0:n, i % 2, 2:3], st[0:n, i % 2, 1:2]).then_inc(a_rcp, 1)
                dve.wait_ge(a_rcp, i + 1)
                dve.tensor_scalar(wk[0:n, i % 2, 0:cols], wk[0:n, i % 2, 0:cols], st[0:n, i % 2, 2:3], None,
                                  ALU.mult).then_inc(a_norm, 1)
                if i >= 2:
                    out_low(i - 2)
            out_low(len(items) - 2)
            out_low(len(items) - 1)

            def merged_low(j):
                dve.wait_ge(g_mhi, j + 1)
                dve.tensor_tensor(mg_lo[:, j, :], proj[:, acc_slot(j), :], mg_hi[:, j, :], ALU.subtract).then_inc(g_mlo, 1)

            for r in range(N_GATE):
                jp, b, j2 = r // 6, r % 6 // 2, r % 2
                gate = proj[:, FQ + r % GATE_SLOTS, :]
                acc = proj[:, acc_slot(2 * jp + j2), :]
                if b == 0 and jp >= 2:
                    dve.wait_ge(g_mlo, 2 * (jp - 2) + j2 + 1)
                dve.wait_ge(g_sig, r + 1)
                if j2:
                    dve.wait_ge(unit_used, U_MERGE + r // 2 + 1)
                else:
                    dve.wait_ge(g_ready, r // 2 + 1)
                dve.tensor_tensor(two((gate if b else acc)), ps[:, 2 * (r % 4):2 * (r % 4) + 2, 0:HALF], two(gate),
                                  ALU.mult).then_inc(g_prod, 1)
                if b:
                    dve.wait_ge(g_prod, r + 1)
                    if b == 2:
                        dve.wait_ge(g_acc, 4 * jp + j2 + 1)
                    dve.tensor_tensor(acc, acc, gate, ALU.add).then_inc(g_acc, 1)
                if b == 1 and jp:
                    merged_low(2 * (jp - 1) + j2)
            for j in range(KT - 2, KT):
                merged_low(j)

            for j in range(KT):
                dve.wait_ge(unit_used, U_OUT + j + 1)
                dve.tensor_tensor(two(xT[:, j, :]), ps[:, 2 * (j % 2):2 * (j % 2) + 2, 0:HALF], two(xT[:, j, :]),
                                  ALU.add).then_inc(x2_ready, 1)
                if j >= 2:
                    add_square(2, j - 1, proj)
            add_square(2, KT - 1, proj)
            dve.wait_ge(x2_ready, KT)
            norm(2, xT, C_FFN, wk[:, 1, :], proj[:, 8:8 + KT, :], act_hi, act_lo)

            dve.wait_ge(n_lo, 3 * KT)
            dve.memset(S[64:128, 4, :, :], 0.0)
            for q in range(NHC):
                dve.wait_ge(s_ready, q + 1)
                dve.tensor_copy(S[:, 0:4, q, :], ps[:, 4 + 2 * (q % 2), :].rearrange("p (a b) -> p a b", a=4))
                dve.tensor_copy(S[0:TS, 4, q, :], ps[0:TS, 5 + 2 * (q % 2), 0:NKEY]).then_inc(s_evac, 1)
            dve.wait_ge(s_evac, NHC)

            with dve.Fori(0, NTT) as i:
                k = [0]

                def step(ins, wait=True):
                    k[0] += 1
                    ins.then_inc(tk, 1)
                    if wait:
                        dve.wait_ge(tk, i * N_TK + k[0])

                def hold():
                    dve.memset(gs[:, 0, :], 0.0)

                def top16(src, rest, vals, idx, count):
                    hold()
                    for x in range(count):
                        ins = dve.max(vals[:, x, 0:8], src[:, x, :])
                    step(ins)
                    hold()
                    for x in range(count):
                        dve.max_index(idx[:, x, 0:8], vals[:, x, 0:8], src[:, x, :])
                        ins = dve.match_replace(rest[:, x, :], vals[:, x, 0:8], src[:, x, :], -3e38)
                    step(ins)
                    hold()
                    for x in range(count):
                        ins = dve.max(vals[:, x, 8:16], rest[:, x, :])
                    step(ins)
                    hold()
                    for x in range(count):
                        ins = dve.max_index(idx[:, x, 8:16], vals[:, x, 8:16], rest[:, x, :])
                    step(ins)

                step(dve.tensor_copy(sA[:, :, :], S[:, bass.ds(i, 1), :, :].rearrange("p o a b -> p (o a) b")))
                top16(sA, sB, top, topi, NHC)
                step(dve.tensor_copy(topf[:, :, :], topi[:, :, :]))
                for h in range(NPH):
                    ins = dve.tensor_tensor(candA[:, h, :].rearrange("p (a b) -> p a b", a=TOPK),
                                            top[:, 2 * h, :].unsqueeze(2).broadcast_to((P, TOPK, TOPK)),
                                            top[:, 2 * h + 1, :].unsqueeze(1).broadcast_to((P, TOPK, TOPK)), ALU.add)
                step(ins)
                top16(candA, candB, best, bi, NPH)
                step(dve.tensor_scalar(ab[:, 0, :, :], bi[:, :, :], 4, None, ALU.logical_shift_right), False)
                step(dve.tensor_scalar(ab[:, 1, :, :], bi[:, :, :], 15, None, ALU.bitwise_and))
                step(dve.tensor_copy(abf[:, :, :, :], ab[:, :, :, :]))
                for half in range(2):
                    step(dve.tensor_tensor(eq, abf[:, half, :, :].rearrange("p h k -> p (h k)").unsqueeze(2)
                                           .broadcast_to((P, P, TOPK)),
                                           iota[:, 0:TOPK].unsqueeze(1).broadcast_to((P, P, TOPK)), ALU.is_equal))
                    eh = eq.rearrange("p (h k) c -> p h k c", h=NPH)
                    for h in range(NPH):
                        ins = dve.tensor_tensor(eh[:, h, :, :], eh[:, h, :, :],
                                                topf[:, 2 * h + half, :].unsqueeze(1).broadcast_to((P, TOPK, TOPK)),
                                                ALU.mult)
                    step(ins)
                    step(dve.tensor_reduce(trip[:, half, bass.ds(i, 1), :].rearrange("p o k -> p (o k)"), eq, AX.X, ALU.add))
                w3 = trip[:, 2, bass.ds(i, 1), :].rearrange("p o (h k) -> p (o h) k", h=NPH)
                step(dve.tensor_tensor(w3, best[:, :, :], best[:, :, 0:1].broadcast_to((P, NPH, TOPK)), ALU.subtract))
                assert k[0] == N_TK

            w3 = trip[:, 2, :, :].rearrange("p a (h k) -> p (a h) k", h=NPH)
            dve.wait_ge(tk_exp, 1)
            dve.tensor_reduce(gs[:, 0, :], w3, AX.X, ALU.add).then_inc(soft, 1)
            dve.wait_ge(soft, 1)
            dve.reciprocal(gs[:, 1, :], gs[:, 0, :]).then_inc(soft, 1)
            dve.wait_ge(soft, 2)
            dve.tensor_tensor(w3, w3, gs[:, 1, :].unsqueeze(2).broadcast_to((P, NTT * NPH, TOPK)), ALU.mult).then_inc(soft, 1)
            for c in range(2):
                dve.wait_ge(tk_turned, c + 1)
                dve.tensor_copy(pair[:, c, 0:TP], ps[:, 6 - 2 * c, :])
                dve.tensor_copy(pair[:, c, TP:T], ps[:, 7 - 2 * c, 0:TS]).then_inc(soft, 1)
            dve.wait_ge(tk_turned, 3)
            dve.tensor_copy(w16[:, 0:TP], ps[:, 6, :])
            dve.tensor_copy(w16[:, TP:T], ps[:, 7, 0:TS]).then_inc(soft, 1)
            dve.wait_ge(soft, 6)
            dve.tensor_tensor(pair[:, 3, 0:TP], ps[:, 6, :], w16[:, 0:TP], ALU.subtract)
            dve.tensor_tensor(pair[:, 3, TP:T], ps[:, 7, 0:TS], w16[:, TP:T], ALU.subtract)
            dve.tensor_copy(pair[:, 2, :], w16[:, :]).then_inc(paired, 1)
            dve.wait_ge(paired, 1)

            def one_hots(i, first=False):
                for c in range(2):
                    if not first:
                        dve.wait_ge(b_prod, i * 2 + c - 1)
                    dve.tensor_copy(tcol[:, c, :, :], pair[:, :, bass.ds(i * (2 * GT) + c * GT, GT)]).then_inc(b_col, 1)
                    dve.wait_ge(b_col, i * 2 + c + 1)
                    for u in range(GT):
                        dve.tensor_scalar(hot2[:, c, u, :], iota[:, :], tcol[:, c, 1, u:u + 1], None, ALU.is_equal)
                        for x, hot in ((2, hot_hi), (3, hot_lo)):
                            last = dve.tensor_scalar(hot[:, c, u, :], iota[:, :], tcol[:, c, 0, u:u + 1],
                                                     tcol[:, c, x, u:u + 1], ALU.is_equal, ALU.mult)
                    last.then_inc(b_hot, 1)

            one_hots(0, first=True)
            with dve.Fori(1, T // GT // 2) as i:
                one_hots(i)

            def w_low(c, pg, k):
                dve.wait_ge(w_hi_done, c + 1)
                dve.tensor_tensor(W_lo[:, pg, k, :], wb[:, k % 2, :], W_hi[:, pg, k, :], ALU.subtract).then_inc(w_lo_done, 1)

            def peer_w(g, pg, loads):
                dve.wait_ge(gh_in[pg], loads)
                for k in range(GRP):
                    c = g * GRP + k
                    if k >= 2:
                        dve.wait_ge(w_lo_done, c - 1)
                    dve.tensor_tensor(wb[:, k % 2, :].rearrange("p (b t) -> p b t", b=NBLK),
                                      Hb[:, pg, k, :].rearrange("p (b t) -> p b t", b=NBLK),
                                      Gb[:, pg, :, k, :], ALU.mult).then_inc(w_mul, 1)
                    if k:
                        w_low(c - 1, pg, k - 1)
                w_low(g * GRP + GRP - 1, pg, GRP - 1)

            def peer_acc(g, last=False):
                for d in range(KT):
                    if d < KT - 1:
                        dve.wait_ge(v_ready, g * (KT - 1) + d + 1)
                    else:
                        dve.wait_ge(unit_used, g * GRP + (U_V + GRP))
                    dve.tensor_tensor(two(xT[:, d, :]), ps[:, 2 * (d % 4):2 * (d % 4) + 2, 0:HALF], two(xT[:, d, :]),
                                      ALU.add).then_inc(acc_done, 1)
                    if last and d >= 2:
                        add_square(3, d - 1, fin_sq)

            peer_w(0, 0, 32)
            with dve.Fori(0, (NG - 2) // 2) as i:
                for b in range(2):
                    g = i * 2 + (1 + b)
                    dve.wait_ge(w_lo_done, g * GRP)
                    peer_w(g, (1 + b) % 2, i * 32 + (32 if b == 0 else 64))
                    peer_acc(g - 1)
            dve.wait_ge(w_lo_done, (NG - 1) * GRP)
            peer_w(NG - 1, (NG - 1) % 2, 16 * NG)
            peer_acc(NG - 2)
            peer_acc(NG - 1, last=True)
            add_square(3, KT - 1, fin_sq)
            norm(3, xT, C_FIN, wb[:, 0, :], fin_y, None, None)

        @block.tensor
        def _(pe):
            def sums(i, sq, out, n):
                pe.wait_ge(n_add, (KT - 1) * (i + 1))
                for half in range(len(out)):
                    last = pe.matmul(out[half], ones[:, :], sq[:, 0, half * n:(half + 1) * n], start=True, stop=True)
                last.then_inc(n_ssq, 1)

            def tile(slot, rhs_hi, rhs_lo, bank, kts=KT, width=P, c0_=0, n=HALF, halves=2, ready=None, split=n_lo):
                for k in range(kts):
                    if ready is not None:
                        pe.wait_ge(split, ready + k + 1)
                    col = k * width + c0_
                    for w, x in ((w_hi, rhs_hi), (w_hi, rhs_lo), (w_lo, rhs_hi)):
                        for half in range(halves):
                            last = pe.matmul(ps[:, bank + half, 0:n], w[:, slot, col:col + P],
                                             x(k)[:, half * n:(half + 1) * n],
                                             start=(k == 0 and w is w_hi and x is rhs_hi),
                                             stop=(k == kts - 1 and w is w_lo))
                return last

            def natural(first, u, hi, lo, frames, banks, freed=None):
                n = first + u
                pe.wait_ge(lo_ready, n + 1)
                for i, ((f0, nf), bank) in enumerate(zip(frames, banks)):
                    if freed and u == 0 and freed[i]:
                        pe.wait_ge(nat_evac, freed[i])
                    for k2 in range(2):
                        k = 2 * u + k2
                        for x, w in ((hi, w_hi), (lo, w_hi), (hi, w_lo)):
                            last = pe.matmul(ps[0:nf, bank, :], x[:, k, f0:f0 + nf],
                                             w[:, n % RING, k2 * 512:(k2 + 1) * 512],
                                             start=(k == 0 and x is hi and w is w_hi), stop=(k == KT - 1 and w is w_lo))
                last.then_inc(unit_used, 1)

            a_hi, a_lo = (lambda k: act_hi[:, k, :]), (lambda k: act_lo[:, k, :])

            pe.wait_ge(consts, 8)
            sums(0, mix_sq, [ps[:, 0, 0:HALF], ps[:, 1, 0:HALF]], HALF)

            pe.wait_ge(n_rms, 1)
            for k in range(N_T):
                if k == 4:
                    sums(1, mem_sq, [ps[:, 4, 0:NMEM]], NMEM)
                pe.wait_ge(lo_ready, U_T + k + 1)
                if k >= 2:
                    pe.wait_ge(t_evac, k - 1)
                tile((U_T + k) % RING, a_hi, a_lo, 2 * (k % 2), ready=None if k else 0).then_inc(unit_used, 1)
            pe.wait_ge(lo_ready, U_SMALL + 1)
            pe.wait_ge(t_evac, N_T)
            tile(U_SMALL % RING, a_hi, a_lo, 0).then_inc(unit_used, 1)
            pe.wait_ge(n_rms, 2)
            for q in range(N_MEMK):
                pe.wait_ge(lo_ready, U_MEMK + q + 1)
                if q >= 2:
                    pe.wait_ge(memk_evac, q - 1)
                tile((U_MEMK + q) % RING, lambda k: mem_hi[:, k, :], lambda k: mem_lo[:, k, :], 2 + q % 2, n=NMEM,
                     halves=1, ready=None if q else KT).then_inc(unit_used, 1)
            for u in range(N_MEMV):
                natural(U_MEMV, u, mem_hi, mem_lo, [(0, P), (P, P)], [4, 5])
            frames = [(t * P, P) for t in (2, 3, 0, 1)] + [(TP, TS)]
            pe.wait_ge(memk_evac, N_MEMK)
            for u in range(N_MV):
                natural(U_MV, u, act_hi, act_lo, frames, [6, 7, 4, 5, 2], [0, 0, 1, 1, 0])
            for u in range(N_FV):
                natural(U_FV, u, act_hi, act_lo, frames, [6, 7, 4, 5, 3], [2, 3, 4, 5, 6])

            def fill(p):
                f, part = p // 3, p % 3
                n, half = U_FILL + f // 2, f % 2
                if part == 0:
                    pe.wait_ge(lo_ready, n + 1)
                    if f >= 2:
                        pe.wait_ge(fill_evac, fill_index(f) - 1)
                    else:
                        pe.wait_ge(nat_evac, 7 + f)
                for m in range(part * PIECE, (part + 1) * PIECE):
                    k = m // 3
                    w, x = ((w_hi, act_hi), (w_hi, act_lo), (w_lo, act_hi))[m % 3]
                    last = pe.matmul(ps[:, 6 + half, 0:HALF], w[:, n % RING, k * P:(k + 1) * P],
                                     x[:, k, half * HALF:(half + 1) * HALF], start=(m == 0), stop=(m == 3 * KT - 1))
                if part == 2:
                    last.then_inc(unit_used if half else fill_half, 1)

            for p in range(6 * PRE_TILES):
                fill(p)

            def head_sums(h):
                pe.wait_ge(nb_sq, h + 1)
                for half in range(2):
                    pe.wait_ge(fill_evac, norm_index(h) + half - 1)
                    pe.matmul(ps[:, 6 + half, 0:HALF], ones[:, :], wk[:, 4, half * HALF:(half + 1) * HALF],
                              start=True, stop=True).then_inc(m_ssq, 1)

            pe.wait_ge(row_dve, 8)
            pe.wait_ge(nat_evac, 11)
            for t in range(NTT):
                n = P if t < 4 else TS
                last = pe.transpose(ps[0:n, 2, 4 * t:4 * t + 4], c_row[:, t * P:t * P + n], ident[0:4, 0:4])
            last.then_inc(c_turned, 1)

            pe.wait_ge(row_dve, 16)
            pe.wait_ge(cS_ready, 2)
            pe.wait_ge(conv_done, KT)
            pe.wait_ge(small_in, 9 * 16)
            for h in range(HM):
                pick = ident[0:4, h:h + 1].broadcast_to((4, P))
                qT, kT = proj[:, MQ + h, :], proj[:, MK + h, :]
                if h:
                    pe.wait_ge(m_dve, N_MD * h)
                pe.matmul(ps[:, 2, :], pick, nM[:, 0:TP], start=True, stop=True)
                pe.matmul(ps[:, 3, 0:TS], pick, nM[:, TP:T], start=True, stop=True)
                pe.matmul(ps[:, 4, :], pick, m_row[:, 0:TP], start=True, stop=True)
                pe.matmul(ps[:, 3, TS:2 * TS], pick, m_row[:, TP:T], start=True, stop=True).then_inc(m_bc, 1)

                def scores(j):
                    q = 5 * h + j
                    if j >= 2:
                        pe.wait_ge(m_sw, q - 1)
                    if j < 4:
                        pe.matmul(ps[:, j % 2, 0:TP - P * j], kT[:, P * j:P * (j + 1)], qT[:, P * j:TP],
                                  start=True, stop=True).then_inc(m_s, 1)
                    else:
                        pe.matmul(ps[0:TS, 0, 0:TS], kT[:, TP:T], qT[:, TP:T], start=True, stop=True).then_inc(m_s, 1)

                p0 = 6 * PRE_TILES + h * H_PIECES
                scores(0)
                scores(1)
                for p in range(3):
                    fill(p0 + p)
                pe.wait_ge(m_act, N_MA * h + 3)
                for j in range(5):
                    pe.wait_ge(m_sw, 5 * h + j + 1)
                    if j < 4:
                        sw = wk[:, j % 2, 0:TP - P * j]
                        pe.matmul(ps[:, 4, P * j:TP], mv[:, j, P * h:P * (h + 1)], sw, start=(j == 0), stop=(j == 3))
                        pe.matmul(ps[:, 5, P * j:TP], ones[:, :], sw, start=(j == 0), stop=(j == 3)).then_inc(m_acc, 1)
                    else:
                        sw = wk[0:TS, 0, 0:TS]
                        pe.wait_ge(m_dve, N_MD * h + 2)
                        pe.matmul(ps[:, 3, 256:256 + TS], mv[0:TS, 4, P * h:P * (h + 1)], sw, start=True, stop=False)
                        pe.matmul(ps[:, 3, 256:256 + TS], c0[:, h, :], sm[:, 1, :], start=False, stop=True)
                        pe.matmul(ps[:, 3, 320:320 + TS], ones[0:TS, :], sw, start=True, stop=False)
                        pe.matmul(ps[:, 3, 320:320 + TS], n0[:, h:h + 1].broadcast_to((P, P)), sm[:, 1, :], start=False,
                                  stop=True).then_inc(m_acc, 1)
                    if j + 2 < 5:
                        scores(j + 2)
                    for p in ((3, 4, 5), (), (6, 7, 8, 9), (10,), (11, 12))[j]:
                        fill(p0 + p)
                    if j == 1 and h:
                        head_sums(h - 1)
                for j in range(4):
                    pe.transpose(ps[:, 1, P * j:P * (j + 1)], kT[:, P * j:P * (j + 1)], ident[:, :])
                pe.transpose(ps[0:TS, 2, 0:P], kT[:, TP:T], ident[:, :]).then_inc(m_kt, 1)
                for p in range(13, 16):
                    fill(p0 + p)
                for p in range(16, H_PIECES):
                    fill(p0 + p)
                pe.wait_ge(m_dve, N_MD * h + 3)
                for col, rhs in ((0, lambda j: mv[:, j, P * h:P * (h + 1)]), (P, lambda j: ones[:, 0:1])):
                    for j in range(4):
                        pe.matmul(ps[:, 2, col:col + (P if col == 0 else 1)], wk[:, 0, P * j:P * (j + 1)], rhs(j),
                                  start=(j == 0), stop=(j == 3))
                pe.matmul(ps[:, 2, 256:256 + P], wk[0:TS, 1, 0:P], mv[0:TS, 4, P * h:P * (h + 1)], start=True, stop=True)
                pe.matmul(ps[:, 2, 384:385], wk[0:TS, 1, 0:P], ones[0:TS, 0:1], start=True, stop=True).then_inc(m_st, 1)

            def att_scores(i):
                kind, h, qi = items[i]
                n, cols = P if qi < 4 else TS, columns(kind, qi)
                out = ps[0:n, i % 2, 0:cols]
                if i >= 2:
                    pe.wait_ge(a_exp, i - 1)
                if kind == "mem":
                    keys_ = mkT if qi < 4 else kc
                    pe.matmul(out, proj[:, CQ + h, qi * P:qi * P + n], keys_[:, h, :], start=True, stop=True).then_inc(a_sc, 1)
                    return
                hp = h // 2
                pe.wait_ge(q_apart, hp + 1)
                q = qz[:, hp % 2, h % 2, qi * P:qi * P + n]
                pick = pick3[:, h:h + 1].broadcast_to((P, n))
                c_lo = 0 if qi < 4 else TP
                pe.matmul(out, pick, cum3[:, c_lo:c_lo + cols], start=True, stop=False)
                if qi < 4:
                    pe.matmul(out, q, proj[:, FK + hp, 0:cols], start=False, stop=False)
                else:
                    pe.matmul(out[:, 0:PAST], q, kpast[:, hp, :], start=False, stop=False)
                    pe.matmul(out[:, PAST:cols], q, proj[:, FK + hp, TP:T], start=False, stop=False)
                pe.matmul(out[:, cols - n:cols], identb[0:n, 0:n], maskneg[0:n, 0:n], start=False,
                          stop=True).then_inc(a_sc, 1)

            def att_values(i):
                kind, h, qi = items[i]
                n, cols = P if qi < 4 else TS, columns(kind, qi)
                blocks = [(b * P, min(P, cols - b * P)) for b in range((cols + P - 1) // P)]
                pe.wait_ge(a_norm, i + 1)
                if i >= 2:
                    pe.wait_ge(a_pt, i - 1)
                for b, (s0, ns) in enumerate(blocks):
                    last = pe.transpose(ps[0:ns, 2 + i % 2, b * P:b * P + n], wk[0:n, i % 2, s0:s0 + ns], ident[0:n, 0:n])
                last.then_inc(a_tr, 1)

            def att_out(i):
                kind, h, qi = items[i]
                n, cols = P if qi < 4 else TS, columns(kind, qi)
                blocks = [(b * P, min(P, cols - b * P)) for b in range((cols + P - 1) // P)]
                x = out_index(i)
                pe.wait_ge(a_pt, i + 1)
                if x >= 2:
                    pe.wait_ge(a_ol, x - 1)
                r0 = FD * (h % 2) if kind == "fox" else 0
                rows = FD if kind == "fox" else P
                for b, (s0, ns) in enumerate(blocks):
                    if kind == "mem":
                        v = (mvN if qi < 4 else vc)[:, b, P * h:P * (h + 1)]
                    elif qi < 4:
                        v = fv[:, b, FD * h:FD * (h + 1)]
                    else:
                        v = vpast[:, FD * h:FD * (h + 1)] if b == 0 else fv[0:TS, 4, FD * h:FD * (h + 1)]
                    last = pe.matmul(ps[r0:r0 + rows, 4 + x % 2, 0:n], v, wk[0:ns, 2 + i % 2, b * P:b * P + n],
                                     start=(b == 0), stop=(b == len(blocks) - 1))
                last.then_inc(a_pv, 1)

            pe.wait_ge(cum_split, N_SPLIT)
            head_sums(HM - 1)
            for p in range(LEAD):
                fill(6 * N_PROJ + p)
            pe.wait_ge(m_dve, N_MD * HM)
            pe.wait_ge(m_act, N_MA * HM)
            pe.wait_ge(fill_evac, fill_index(2 * N_PROJ - 1) + 1)
            att_scores(0)
            for i in range(len(items)):
                if i + 1 < len(items):
                    att_scores(i + 1)
                pieces = list(gate_pieces(i))
                for p in pieces:
                    fill(p)
                att_values(i)
                if i >= 1:
                    att_out(i - 1)
            att_out(len(items) - 1)

            branch_slot = [MO, 0, 4]
            pe.wait_ge(a_ol, HF * NTT // 2 + HC * NTT)
            pe.wait_ge(fill_evac, 2 * (N_PROJ + N_GATE + HM))
            pe.wait_ge(nb_dve, N_NB * HM)
            for u in range(N_JP * NB):
                n, s0 = U_MERGE + u, branch_slot[u % NB]
                pe.wait_ge(lo_ready, n + 1)
                for j2 in range(2):
                    r = 2 * u + j2
                    if r >= 4:
                        pe.wait_ge(g_prod, r - 3)
                    last = tile(n % RING, lambda k: proj_b[:, s0 + k, 0, :], lambda k: proj_b[:, s0 + k, 1, :],
                                2 * (r % 4), kts=4, width=2 * P, c0_=j2 * P)
                    last.then_inc(unit_used if j2 else g_ready, 1)

            pe.wait_ge(g_prod, N_GATE)
            for j in range(KT):
                n = U_OUT + j
                pe.wait_ge(lo_ready, n + 1)
                if j >= 2:
                    pe.wait_ge(x2_ready, j - 1)
                tile(n % RING, lambda k: mg_hi[:, k, :], lambda k: mg_lo[:, k, :], 2 * (j % 2),
                     ready=None if j else 0, split=g_mlo).then_inc(unit_used, 1)

            sums(2, proj[:, 0:KT, :], [ps[:, 4, 0:HALF], ps[:, 5, 0:HALF]], HALF)

            def key_scores(q):
                pe.wait_ge(q_evac, q + 1)
                if q >= 2:
                    pe.wait_ge(s_evac, q - 1)
                for t in range(NTT):
                    n = P if t < 4 else TS
                    bank, col = (4 + 2 * (q % 2), t * P) if t < 4 else (5 + 2 * (q % 2), 0)
                    last = pe.matmul(ps[0:n, bank, col:col + NKEY], qr[:, q % 2, t * P:t * P + n], keys[:, q, :],
                                     start=True, stop=True)
                last.then_inc(s_ready, 1)

            pe.wait_ge(n_rms, 3)
            pe.wait_ge(keys_in, 16)
            for q in range(NHC):
                n = U_WQ + q
                pe.wait_ge(lo_ready, n + 1)
                if q >= 2:
                    pe.wait_ge(q_evac, q - 1)
                tile(n % RING, a_hi, a_lo, 2 * (q % 2), ready=None if q else 2 * KT).then_inc(unit_used, 1)
                if q:
                    key_scores(q - 1)
            key_scores(NHC - 1)

            pe.wait_ge(q_evac, NHC)

            def chunk(j, k, first=False):
                pe.wait_ge(lo_ready, j * BODY + (U_PEER + k + 1))
                if not (first and k < 2):
                    pe.wait_ge(gelu_done, j * BODY + (k - 1))
                tile((U_PEER + k) % RING, a_hi, a_lo, 2 * (k % 2)).then_inc(unit_used, 1)

            def g_step(j, k, e, first=False):
                s = j * G_BODY + (2 * k + e - 2 - J_G * G_BODY)
                pe.wait_ge(b_hot, s + 1)
                if not (first and k == 1):
                    pe.wait_ge(b_evac, s - 1)
                for u in range(GT):
                    pe.matmul(ps[:, 4 + e, u * P:(u + 1) * P], hot2[:, e, u, :], hot_hi[:, e, u, :], start=True, stop=False)
                    last = pe.matmul(ps[:, 4 + e, u * P:(u + 1) * P], hot2[:, e, u, :], hot_lo[:, e, u, :],
                                     start=False, stop=True)
                last.then_inc(b_prod, 1)

            for k in range(BODY):
                chunk(0, k, first=True)
            with pe.Fori(1, J_G) as j:
                for k in range(BODY):
                    chunk(j, k)
            for k in range(2):
                chunk(J_G, k)
            pe.wait_ge(soft, 3)
            pe.wait_ge(s_evac, NHC)
            for c in range(3):
                if c == 2:
                    pe.wait_ge(soft, 4)
                bank = 4 if c == 1 else 6
                for t in range(NTT):
                    last = pe.transpose(ps[:, bank + t // 4, (t % 4) * P:(t % 4 + 1) * P], trip[:, c, t, :], ident[:, :])
                last.then_inc(tk_turned, 1)
            for k in range(1, BODY):
                if k >= 2:
                    chunk(J_G, k)
                for e in range(2):
                    g_step(J_G, k, e, first=True)
            with pe.Fori(J_G + 1, J_END) as j:
                for k in range(BODY):
                    chunk(j, k)
                    for e in range(2):
                        g_step(j, k, e)
            for k in range(BODY):
                chunk(J_END, k)
                if k == 0:
                    for e in range(2):
                        g_step(J_END, k, e)
            pe.wait_ge(b_evac, T // GT)
            pe.wait_ge(gelu_done, NCH)

            def peer_v(g, b, first=False):
                pe.wait_ge(lo_ready, g * GRP + (U_V + GRP))
                pe.wait_ge(w_lo_done, g * GRP + GRP)
                for d in range(KT):
                    if not (first and d < 4):
                        pe.wait_ge(acc_done, g * KT + d - 3)
                    bank = 2 * (d % 4)
                    for k in range(GRP):
                        slot = (U_V + b * GRP + k) % RING
                        for w, x in ((w_hi, W_hi), (w_hi, W_lo), (w_lo, W_hi)):
                            for half in range(2):
                                last = pe.matmul(ps[:, bank + half, 0:HALF], w[:, slot, d * P:(d + 1) * P],
                                                 x[:, b, k, half * HALF:(half + 1) * HALF],
                                                 start=(k == 0 and w is w_hi and x is W_hi),
                                                 stop=(k == GRP - 1 and w is w_lo))
                        if d == KT - 1:
                            last.then_inc(unit_used, 1)
                    if d < KT - 1:
                        last.then_inc(v_ready, 1)

            peer_v(0, 0, first=True)
            with pe.Fori(0, (NG - 2) // 2) as i:
                for b in range(2):
                    peer_v(i * 2 + (1 + b), (1 + b) % 2)
            peer_v(NG - 1, (NG - 1) % 2)

            pe.wait_ge(acc_done, NG * KT - 3)
            sums(3, fin_sq, [ps[:, 0, 0:HALF], ps[:, 1, 0:HALF]], HALF)


_OUTS = {
    "y": (P, KT, T), "fk": (P, 4, T), "fv_p": (P, 4, 512), "fv_s": (TS, 512), "lf_p": (8, TP), "lf_s": (8, TS),
    "cn_p": (P, HM, P + 1), "m_p": (HM, 1), "conv_p": (P, KT, 3), "memk": (P, HC, NMEM),
    "memv": (P, 2, 512), "cn_s": (P, HM, P + 1), "m_s": (HM, 1), "conv_s": (P, KT, 3),
}


def kernel(**x):
    import numpy as np
    import concourse.bacc as bacc
    from concourse.bass_utils import run_bass_kernel_spmd as run

    x = {k: np.asarray(v) for k, v in x.items()}
    f32 = np.float32
    assert x["x_prompt"].shape == (1, TP, D) and x["x_sample"].shape == (1, TS, D)

    def channels(v):
        return v.reshape((-1, P) + v.shape[1:]).swapaxes(0, 1)

    def tiles(w, width=P):
        k, c = w.shape
        return w.reshape(k // P, P, c // width, width).transpose(2, 1, 0, 3).reshape(c // width, P, -1)

    def pairs(w):
        return w.reshape(4, 2, P, 512).transpose(0, 2, 1, 3).reshape(4, P, 1024)

    w_in = x["w_in"][0]
    bounds = np.cumsum([0, 512, 512, 512, 512, HM, HM, 512, 512, 512, HF, 512, NB * D])
    mq, mk, mv, mo, mi, mf, fq, fk, fv, ff, cq, gates = [w_in[:, s:e] for s, e in zip(bounds[:-1], bounds[1:])]
    small = np.zeros((D, P), f32)
    small[:, 0:HM], small[:, 32:32 + HF], small[:, 64:64 + HM] = mf, ff, mi
    memkv = x["w_mem_kv"][0]
    gate_units = tiles(gates)
    up_units = [tiles(x[n][0], 2 * P) for n in ("w_up_m", "w_up_f", "w_up_c")]
    merge, gate_order = [], []
    for jp in range(N_JP):
        merge += [up_units[b][jp] for b in range(NB)]
        gate_order += [gate_units[b * KT + 2 * jp + j2] for b in range(NB) for j2 in range(2)]
    units = np.concatenate([
        tiles(np.concatenate([mq, mk], axis=1)), tiles(small), tiles(memkv[:, :512]), pairs(memkv[:, 512:]),
        pairs(mv), pairs(fv),
        tiles(np.concatenate([mo, fq, fk, cq], axis=1)), np.stack(gate_order), np.stack(merge), tiles(x["w_out"][0]), tiles(x["peer_wq"][0]),
    ])
    assert units.shape == (U_PEER, P, 1024)

    par = np.zeros((P, N_PAR), f32)
    for col, name in ((C_MIX, "norm_mix"), (C_FFN, "norm_ffn"), (C_FIN, "norm_final"), (C_MEM, "norm_mem")):
        par[:, col:col + KT] = channels(x[name].reshape(-1))
    par[:, C_HEAD:C_HEAD + HM] = channels(x["norm_m_head"][0])
    par[:, C_CW:C_CW + 32] = x["conv_w"][0].reshape(4, KT, P).transpose(2, 0, 1).reshape(P, 32)
    par[:, C_CB:C_CB + KT] = channels(x["conv_b"][0])
    par[0:HM, C_ZB], par[32:32 + HF, C_ZB], par[64:64 + HM, C_IB] = x["b_m_f"][0], x["b_fox_f"][0], x["b_m_i"][0]

    ins = {
        "units": units,
        "u_units": x["peer_u"][0].reshape(NCH, P, KT, P).transpose(0, 3, 2, 1).reshape(NCH, P, 1024),
        "v_units": x["peer_v"][0].reshape(NCH, P, D),
        "par": par,
        "xT": channels(np.concatenate([x["x_prompt"][0], x["x_sample"][0]]).T),
        "memT": channels(x["mem_prompt"][0].T),
        "conv_state": channels(x["state_conv"][0, 0].T),
        "lf_past": x["cache_fox_lf"][0, 0].T,
        "c0": x["state_mlstm_c"][0, 0].transpose(1, 0, 2),
        "n0": x["state_mlstm_n"][0, 0].T,
        "m0": x["state_mlstm_m"][0],
        "kc": x["cache_mem_k"][0, 0].transpose(2, 1, 0),
        "vc": x["cache_mem_v"][0, 0].reshape(2, P, 512).transpose(1, 0, 2),
        "kpast": channels(x["cache_fox_k"][0, 0].reshape(PAST, 512).T),
        "vpast": x["cache_fox_v"][0, 0].reshape(PAST, 512),
        "keysT": x["peer_keys"][0].reshape(NHC, NKEY, P).transpose(2, 0, 1),
    }
    ins = {k: np.ascontiguousarray(v) for k, v in ins.items()}

    nc = bacc.Bacc("TRN2", target_bir_lowering=False, num_devices=1)
    a = {k: nc.dram_tensor(f"in_{k}", v.shape, mybir.dt.from_np(v.dtype), kind="ExternalInput").ap()
         for k, v in ins.items()}
    o = {k: nc.dram_tensor(f"out_{k}", s, F32, kind="ExternalOutput").ap() for k, s in _OUTS.items()}
    program(nc, a, o)
    r = run(nc, [{f"in_{k}": v for k, v in ins.items()}], core_ids=[0]).results[0]
    r = {k: r[f"out_{k}"] for k in _OUTS}

    def rows(v):
        return v.transpose(2, 1, 0).reshape(v.shape[2], -1)

    y, fk = rows(r["y"]), rows(r["fk"])
    heads = (HF, FD)
    out = (
        y[:TP].reshape(1, TP, D), y[TP:].reshape(1, TS, D),
        fk[:TP].reshape(1, 1, TP, *heads), r["fv_p"].transpose(1, 0, 2).reshape(1, 1, TP, *heads),
        r["lf_p"].T.reshape(1, 1, TP, HF), r["cn_p"][:, :, :P].transpose(1, 0, 2).reshape(1, 1, HM, P, P),
        r["cn_p"][:, :, P].T.reshape(1, 1, HM, P), r["m_p"].reshape(1, 1, HM),
        rows(r["conv_p"]).reshape(1, 1, 3, D),
        r["memk"].transpose(2, 1, 0).reshape(1, 1, NMEM, HC, P),
        r["memv"].transpose(1, 0, 2).reshape(1, 1, NMEM, HC, P),
        fk[TP:].reshape(1, 1, TS, *heads), r["fv_s"].reshape(1, 1, TS, *heads),
        r["lf_s"].T.reshape(1, 1, TS, HF), r["cn_s"][:, :, :P].transpose(1, 0, 2).reshape(1, 1, HM, P, P),
        r["cn_s"][:, :, P].T.reshape(1, 1, HM, P), r["m_s"].reshape(1, 1, HM),
        rows(r["conv_s"]).reshape(1, 1, 3, D),
    )
    return tuple(np.ascontiguousarray(v) for v in out)
```
